# Optimizing a Trainium2 kernel written in Bass

```python
import math
import jax
import jax.numpy as jnp
from jax import lax
import numpy as np

D_MODEL = 1024
BATCH = 1
SEQ = 1024
DEPTH = 1

GRID_W = 64
CTX_LEN = 256
NORM_EPS = 1e-6
MASK_VALUE = -1e30
Q_BLOCK = 128
N_BRANCH = 4
BRANCH_WIDTH = D_MODEL // 4

MLA_HEADS = 4
MLA_Q_RANK = D_MODEL // 4
MLA_KV_RANK = D_MODEL // 8
MLA_NOPE = 64
MLA_ROPE = 32
MLA_V = BRANCH_WIDTH // MLA_HEADS
MLA_SCALE = 1.0 / math.sqrt(MLA_NOPE + MLA_ROPE)
ROPE_BASE = 10000.0

HY_WIDTH = BRANCH_WIDTH
HY_ORDER = 2
HY_BANDS = 16
HY_EMB = 1 + 2 * HY_BANDS
HY_HIDDEN = 64
HY_DECAY_TARGET = 1e-2
HY_DECAY_SHORT_PCT = 0.3
HY_DECAY_LONG_PCT = 1.5

FN_GROUPS = 4
FN_GROUP_DIM = BRANCH_WIDTH // FN_GROUPS

NA_HEADS = 4
NA_HEAD_DIM = BRANCH_WIDTH // NA_HEADS
NA_KH = 8
NA_KW = 16
NA_SCALE = 1.0 / math.sqrt(NA_HEAD_DIM)

MOE_GROUPS = 4
MOE_PER_GROUP = 4
MOE_EXPERTS = MOE_GROUPS * MOE_PER_GROUP
MOE_TOPK = 2
MOE_HIDDEN = 256

MLA_IN = MLA_Q_RANK + MLA_KV_RANK + MLA_ROPE
HY_IN = (HY_ORDER + 1) * HY_WIDTH
FN_IN = BRANCH_WIDTH
NA_IN = 3 * BRANCH_WIDTH
GATE_IN = N_BRANCH * D_MODEL
IN_WIDTH = MLA_IN + HY_IN + FN_IN + NA_IN + GATE_IN

kernel_name = 'hybrid_flow_backbone'

def rmsnorm(x, g):
    xf = x.astype(jnp.float32)
    y = xf * lax.rsqrt(jnp.mean(xf * xf, axis=-1, keepdims=True) + NORM_EPS)
    return (y * g.astype(jnp.float32)).astype(x.dtype)

def modulate(h, shift, scale):
    return h * (1.0 + scale) + shift

def split_columns(p):
    bounds = (MLA_Q_RANK, MLA_Q_RANK + MLA_KV_RANK, MLA_IN, MLA_IN + HY_IN,
              MLA_IN + HY_IN + FN_IN, MLA_IN + HY_IN + FN_IN + NA_IN)
    return jnp.split(p, bounds, axis=-1)

def axial_rope(n_tokens):
    t = jnp.arange(n_tokens, dtype=jnp.int32)
    row = (t // GRID_W).astype(jnp.float32)
    col = (t % GRID_W).astype(jnp.float32)
    n_freq = MLA_ROPE // 4
    inv = ROPE_BASE ** (-jnp.arange(n_freq, dtype=jnp.float32) / n_freq)
    ang = jnp.concatenate([row[:, None] * inv, col[:, None] * inv], axis=-1)
    return jnp.cos(ang), jnp.sin(ang)

def apply_rope(x, cos, sin):
    xf = x.astype(jnp.float32)
    xe, xo = xf[..., 0::2], xf[..., 1::2]
    c = cos[None, :, None, :]
    s = sin[None, :, None, :]
    out = jnp.stack([xe * c - xo * s, xe * s + xo * c], axis=-1).reshape(x.shape)
    return out.astype(x.dtype)

def blocked_attention(q, k, v, scale):
    b, n_q, h, dk = q.shape
    n_blocks = n_q // Q_BLOCK
    q_blocks = jnp.moveaxis(q.reshape(b, n_blocks, Q_BLOCK, h, dk), 1, 0)

    def one_block(qb):
        s = jnp.einsum('bqhd,bkhd->bhqk', qb, k).astype(jnp.float32) * scale
        p = jax.nn.softmax(s, axis=-1).astype(v.dtype)
        return jnp.einsum('bhqk,bkhd->bqhd', p, v)

    o = lax.map(one_block, q_blocks)
    return jnp.moveaxis(o, 0, 1).reshape(b, n_q, h * v.shape[-1])

def mla_qkv(cq, ckv, kr, q_norm, w_uq, kv_norm, w_ukv, rope):
    b, n, _ = cq.shape
    q = (rmsnorm(cq, q_norm) @ w_uq).reshape(b, n, MLA_HEADS, MLA_NOPE + MLA_ROPE)
    kv = (rmsnorm(ckv, kv_norm) @ w_ukv).reshape(b, n, MLA_HEADS, MLA_NOPE + MLA_V)
    q_nope, q_rot = q[..., :MLA_NOPE], q[..., MLA_NOPE:]
    k_nope, v = kv[..., :MLA_NOPE], kv[..., MLA_NOPE:]
    k_rot = kr[:, :, None, :]
    if rope is not None:
        cos, sin = rope
        q_rot = apply_rope(q_rot, cos, sin)
        k_rot = apply_rope(k_rot, cos, sin)
    k_rot = jnp.broadcast_to(k_rot, (b, n, MLA_HEADS, MLA_ROPE))
    return (jnp.concatenate([q_nope, q_rot], axis=-1),
            jnp.concatenate([k_nope, k_rot], axis=-1), v)

def split_heads_qkv(p):
    b, n, _ = p.shape
    q, k, v = jnp.split(p, 3, axis=-1)
    shape = (b, n, NA_HEADS, NA_HEAD_DIM)
    return q.reshape(shape), k.reshape(shape), v.reshape(shape)

def neighbourhood_attention(q, k, v, k_ctx, v_ctx, rpb):
    b, n, h, dh = q.shape
    rows = n // GRID_W
    kh = min(NA_KH, rows)
    r = jnp.arange(rows)
    row_idx = jnp.clip(r - kh // 2, 0, rows - kh)[:, None] + jnp.arange(kh)[None, :]
    col = jnp.arange(GRID_W)
    col_start = jnp.clip(col - NA_KW // 2, 0, GRID_W - NA_KW)
    col_ok = (col[None, :] >= col_start[:, None]) & (col[None, :] < col_start[:, None] + NA_KW)
    dr = row_idx - r[:, None]
    dc = jnp.clip(col[None, :] - col[:, None], -(NA_KW - 1), NA_KW - 1)
    bias = rpb[:, :, dc + NA_KW - 1][:, dr + NA_KH - 1]
    bias = jnp.transpose(bias, (0, 1, 3, 2, 4)).astype(jnp.float32)
    qg = q.reshape(b, rows, GRID_W, h, dh)
    kg = k.reshape(b, rows, GRID_W, h, dh)[:, row_idx]
    vg = v.reshape(b, rows, GRID_W, h, dh)[:, row_idx]
    s_loc = jnp.einsum('brqhd,brjkhd->bhrqjk', qg, kg).astype(jnp.float32) * NA_SCALE + bias[None]
    s_loc = jnp.where(col_ok[:, None, :], s_loc, MASK_VALUE)
    s_ctx = jnp.einsum('brqhd,bchd->bhrqc', qg, k_ctx).astype(jnp.float32) * NA_SCALE
    n_loc = kh * GRID_W
    s = jnp.concatenate([s_loc.reshape(b, h, rows, GRID_W, n_loc), s_ctx], axis=-1)
    p = jax.nn.softmax(s, axis=-1).astype(v.dtype)
    p_loc = p[..., :n_loc].reshape(b, h, rows, GRID_W, kh, GRID_W)
    p_ctx = p[..., n_loc:]
    o = (jnp.einsum('bhrqjk,brjkhd->brqhd', p_loc, vg)
         + jnp.einsum('bhrqc,bchd->brqhd', p_ctx, v_ctx))
    return o.reshape(b, n, h * dh)

def short_conv(u, w):
    up = jnp.pad(u, ((0, 0), (1, 1), (0, 0)))
    return up[:, :-2] * w[0] + up[:, 1:-1] * w[1] + up[:, 2:] * w[2]

def hyena_filters(n_tokens, w1, b1, freq1, w2, b2, freq2, w3):
    f32 = jnp.float32
    t = jnp.linspace(0.0, 1.0, n_tokens, dtype=f32)[:, None]
    bands = jnp.linspace(1e-4, HY_BANDS - 1, HY_BANDS, dtype=f32)
    ang = (2.0 * math.pi / n_tokens) * jnp.arange(n_tokens, dtype=f32)[:, None] * bands
    z = jnp.concatenate([t, jnp.cos(ang), -jnp.sin(ang)], axis=-1)
    h = jnp.sin(freq1.astype(f32) * (z @ w1.astype(f32) + b1.astype(f32)))
    h = jnp.sin(freq2.astype(f32) * (h @ w2.astype(f32) + b2.astype(f32)))
    h = h @ w3.astype(f32)
    deltas = jnp.linspace(math.log(HY_DECAY_TARGET) / HY_DECAY_LONG_PCT,
                          math.log(HY_DECAY_TARGET) / HY_DECAY_SHORT_PCT, HY_WIDTH, dtype=f32)
    window = jnp.exp(-t * jnp.abs(deltas))
    return h.reshape(n_tokens, 2, HY_ORDER, HY_WIDTH) * window[:, None, None, :]

def bidir_fftconv(u, h_fwd, h_bwd):
    n = u.shape[1]
    g = jnp.concatenate([h_fwd, jnp.zeros_like(h_fwd[:1]), h_bwd[:0:-1]], axis=0)
    g = g * lax.rsqrt(jnp.sum(g * g, axis=0, keepdims=True) + NORM_EPS)
    u_f = jnp.fft.rfft(u.astype(jnp.float32), n=2 * n, axis=1)
    g_f = jnp.fft.rfft(g, n=2 * n, axis=0)
    return jnp.fft.irfft(u_f * g_f[None], n=2 * n, axis=1)[:, :n]

def hyena(u, short_w, filt, bias):
    u = short_conv(u, short_w)
    v, x1, x2 = jnp.split(u, 3, axis=-1)
    z = v
    for n, gate in enumerate((x1, x2)):
        y = bidir_fftconv(z, filt[:, 0, n], filt[:, 1, n]).astype(z.dtype) + z * bias[n]
        z = gate * y
    return z

def fnet_mix(u):
    b, n, _ = u.shape
    ug = u.astype(jnp.float32).reshape(b, n, FN_GROUPS, FN_GROUP_DIM)
    y = jnp.fft.fftn(ug, axes=(1, 3), norm='ortho').real
    return y.reshape(b, n, FN_GROUPS * FN_GROUP_DIM).astype(u.dtype)

def merge_branches(outs, gate_logits, w_branch, w_out):
    o = jnp.stack(outs, axis=2)
    proj = jnp.einsum('blnc,ncd->blnd', o, w_branch)
    g = jax.nn.sigmoid(gate_logits.reshape(proj.shape))
    return jnp.sum(g * proj, axis=2) @ w_out

def token_mixers(h_lat, h_ctx, w_in, mla_q_norm, mla_w_uq, mla_kv_norm, mla_w_ukv,
                 hy_short_w, hy_w1, hy_b1, hy_freq1, hy_w2, hy_b2, hy_freq2, hy_w3, hy_bias,
                 na_rpb, w_branch, w_out, update_ctx):
    n_lat = h_lat.shape[1]
    n_ctx = h_ctx.shape[1]
    cq_l, ckv_l, kr_l, hy_l, fn_l, na_l, gate_l = split_columns(h_lat @ w_in)
    cq_c, ckv_c, kr_c, hy_c, fn_c, na_c, gate_c = split_columns(h_ctx @ w_in)

    qa_l, ka_l, va_l = mla_qkv(cq_l, ckv_l, kr_l, mla_q_norm, mla_w_uq, mla_kv_norm, mla_w_ukv,
                               axial_rope(n_lat))
    qa_c, ka_c, va_c = mla_qkv(cq_c, ckv_c, kr_c, mla_q_norm, mla_w_uq, mla_kv_norm, mla_w_ukv, None)
    oa_l = blocked_attention(qa_l, jnp.concatenate([ka_l, ka_c], axis=1),
                             jnp.concatenate([va_l, va_c], axis=1), MLA_SCALE)
    qd_l, kd_l, vd_l = split_heads_qkv(na_l)
    qd_c, kd_c, vd_c = split_heads_qkv(na_c)
    od_l = neighbourhood_attention(qd_l, kd_l, vd_l, kd_c, vd_c, na_rpb)
    filt_l = hyena_filters(n_lat, hy_w1, hy_b1, hy_freq1, hy_w2, hy_b2, hy_freq2, hy_w3)
    ob_l = hyena(hy_l, hy_short_w, filt_l, hy_bias)
    oc_l = fnet_mix(fn_l)
    m_lat = merge_branches((oa_l, ob_l, oc_l, od_l), gate_l, w_branch, w_out)

    m_ctx = None
    if update_ctx:
        oa_c = blocked_attention(qa_c, ka_c, va_c, MLA_SCALE)
        filt_c = hyena_filters(n_ctx, hy_w1, hy_b1, hy_freq1, hy_w2, hy_b2, hy_freq2, hy_w3)
        ob_c = hyena(hy_c, hy_short_w, filt_c, hy_bias)
        oc_c = fnet_mix(fn_c)
        od_c = blocked_attention(qd_c, kd_c, vd_c, NA_SCALE)
        m_ctx = merge_branches((oa_c, ob_c, oc_c, od_c), gate_c, w_branch, w_out)
    return m_lat, m_ctx

def hier_moe(h, w_group, b_group, w_expert, b_expert, w_gate, w_up, w_down):
    t_count = h.shape[0]
    f32 = jnp.float32
    g_prob = jax.nn.softmax((h @ w_group).astype(f32) + b_group.astype(f32), axis=-1)
    g_p, g_idx = lax.top_k(g_prob, 1)
    g_onehot = jax.nn.one_hot(g_idx[:, 0], MOE_GROUPS, dtype=f32)
    e_logits = ((h @ w_expert).astype(f32) + b_expert.astype(f32)).reshape(
        t_count, MOE_GROUPS, MOE_PER_GROUP)
    e_sel = jnp.sum(e_logits * g_onehot[:, :, None], axis=1)
    e_p, e_idx = lax.top_k(jax.nn.softmax(e_sel, axis=-1), MOE_TOPK)
    e_p = e_p / jnp.sum(e_p, axis=-1, keepdims=True)
    w_local = jnp.sum(jax.nn.one_hot(e_idx, MOE_PER_GROUP, dtype=f32) * e_p[..., None], axis=1)
    weights = (g_onehot[:, :, None] * (g_p * w_local)[:, None, :]).astype(h.dtype)
    out = jnp.zeros_like(h)
    for gi in range(MOE_GROUPS):
        sl = slice(gi * MOE_PER_GROUP, (gi + 1) * MOE_PER_GROUP)
        a = jnp.einsum('td,edf->tef', h, w_gate[sl])
        u = jnp.einsum('td,edf->tef', h, w_up[sl])
        act = jax.nn.silu(a) * u * weights[:, gi, :, None]
        out = out + jnp.einsum('tef,efd->td', act, w_down[sl])
    return out

def setup_inputs(seed: int = 0) -> dict:
    key = jax.random.key(seed)
    ks = jax.random.split(key, 33)

    def nrm(k, shape, scale):
        return scale * jax.random.normal(k, shape, jnp.float32)

    D, L = D_MODEL, DEPTH
    E, F = MOE_EXPERTS, MOE_HIDDEN
    return {
        'x': nrm(ks[0], (BATCH, SEQ, D), 1.0),
        'c': nrm(ks[1], (BATCH, D), 1.0),
        'ctx': nrm(ks[2], (BATCH, CTX_LEN, D), 1.0),
        'c_ctx': nrm(ks[3], (D,), 1.0),
        'ada_w': nrm(ks[4], (L, D, 6 * D), 0.5 * D ** -0.5),
        'ada_b': nrm(ks[5], (L, 6 * D), 0.02),
        'norm1_g': 1.0 + nrm(ks[6], (L, D), 0.1),
        'norm2_g': 1.0 + nrm(ks[7], (L, D), 0.1),
        'w_in': nrm(ks[8], (L, D, IN_WIDTH), D ** -0.5),
        'mla_q_norm': 1.0 + nrm(ks[9], (L, MLA_Q_RANK), 0.1),
        'mla_w_uq': nrm(ks[10], (L, MLA_Q_RANK, MLA_HEADS * (MLA_NOPE + MLA_ROPE)), MLA_Q_RANK ** -0.5),
        'mla_kv_norm': 1.0 + nrm(ks[11], (L, MLA_KV_RANK), 0.1),
        'mla_w_ukv': nrm(ks[12], (L, MLA_KV_RANK, MLA_HEADS * (MLA_NOPE + MLA_V)), MLA_KV_RANK ** -0.5),
        'hy_short_w': nrm(ks[13], (L, 3, HY_IN), 3 ** -0.5),
        'hy_w1': nrm(ks[14], (L, HY_EMB, HY_HIDDEN), HY_EMB ** -0.5),
        'hy_b1': nrm(ks[15], (L, HY_HIDDEN), 0.1),
        'hy_freq1': 1.0 + nrm(ks[16], (L, HY_HIDDEN), 0.1),
        'hy_w2': nrm(ks[17], (L, HY_HIDDEN, HY_HIDDEN), HY_HIDDEN ** -0.5),
        'hy_b2': nrm(ks[18], (L, HY_HIDDEN), 0.1),
        'hy_freq2': 1.0 + nrm(ks[19], (L, HY_HIDDEN), 0.1),
        'hy_w3': nrm(ks[20], (L, HY_HIDDEN, 2 * HY_ORDER * HY_WIDTH), HY_HIDDEN ** -0.5),
        'hy_bias': nrm(ks[21], (L, HY_ORDER, HY_WIDTH), 0.5),
        'na_rpb': nrm(ks[22], (L, NA_HEADS, 2 * NA_KH - 1, 2 * NA_KW - 1), 0.1),
        'w_branch': nrm(ks[23], (L, N_BRANCH, BRANCH_WIDTH, D), BRANCH_WIDTH ** -0.5),
        'w_out': nrm(ks[24], (L, D, D), D ** -0.5),
        'moe_w_group': nrm(ks[25], (L, D, MOE_GROUPS), D ** -0.5),
        'moe_b_group': nrm(ks[26], (L, MOE_GROUPS), 0.01),
        'moe_w_expert': nrm(ks[27], (L, D, E), D ** -0.5),
        'moe_b_expert': nrm(ks[28], (L, E), 0.01),
        'moe_w_gate': nrm(ks[29], (L, E, D, F), D ** -0.5),
        'moe_w_up': nrm(ks[30], (L, E, D, F), D ** -0.5),
        'moe_w_down': nrm(ks[31], (L, E, F, D), F ** -0.5),
        'final_norm_g': 1.0 + nrm(ks[32], (D,), 0.1),
    }

def reference(x, c, ctx, c_ctx, ada_w, ada_b, norm1_g, norm2_g, w_in,
              mla_q_norm, mla_w_uq, mla_kv_norm, mla_w_ukv,
              hy_short_w, hy_w1, hy_b1, hy_freq1, hy_w2, hy_b2, hy_freq2, hy_w3, hy_bias,
              na_rpb, w_branch, w_out,
              moe_w_group, moe_b_group, moe_w_expert, moe_b_expert, moe_w_gate, moe_w_up, moe_w_down,
              final_norm_g):
    n_lat_tokens = x.shape[0] * x.shape[1]
    for l in range(DEPTH):
        last = l == DEPTH - 1
        mod_lat = jax.nn.silu(c) @ ada_w[l] + ada_b[l]
        mod_ctx = jax.nn.silu(c_ctx) @ ada_w[l] + ada_b[l]
        sh1, sc1, gt1, sh2, sc2, gt2 = jnp.split(mod_lat[:, None, :], 6, axis=-1)
        sh1c, sc1c, gt1c, sh2c, sc2c, gt2c = jnp.split(mod_ctx, 6, axis=-1)

        h_lat = modulate(rmsnorm(x, norm1_g[l]), sh1, sc1)
        h_ctx = modulate(rmsnorm(ctx, norm1_g[l]), sh1c, sc1c)
        m_lat, m_ctx = token_mixers(h_lat, h_ctx, w_in[l], mla_q_norm[l], mla_w_uq[l], mla_kv_norm[l],
                                    mla_w_ukv[l], hy_short_w[l], hy_w1[l], hy_b1[l], hy_freq1[l],
                                    hy_w2[l], hy_b2[l], hy_freq2[l], hy_w3[l], hy_bias[l],
                                    na_rpb[l], w_branch[l], w_out[l], not last)
        x = x + gt1 * m_lat

        h_lat = modulate(rmsnorm(x, norm2_g[l]), sh2, sc2).reshape(-1, D_MODEL)
        if last:
            f = hier_moe(h_lat, moe_w_group[l], moe_b_group[l], moe_w_expert[l], moe_b_expert[l],
                         moe_w_gate[l], moe_w_up[l], moe_w_down[l])
            x = x + gt2 * f.reshape(x.shape)
        else:
            ctx = ctx + gt1c * m_ctx
            h_ctx = modulate(rmsnorm(ctx, norm2_g[l]), sh2c, sc2c).reshape(-1, D_MODEL)
            f = hier_moe(jnp.concatenate([h_lat, h_ctx], axis=0), moe_w_group[l], moe_b_group[l],
                         moe_w_expert[l], moe_b_expert[l], moe_w_gate[l], moe_w_up[l], moe_w_down[l])
            x = x + gt2 * f[:n_lat_tokens].reshape(x.shape)
            ctx = ctx + gt2c * f[n_lat_tokens:].reshape(ctx.shape)
    return rmsnorm(x, final_norm_g)


_drawn_inputs = setup_inputs


def setup_inputs(seed=0):
    import zlib

    import numpy as np

    out = dict(_drawn_inputs(seed))
    spreads = {}
    factors = {'ctx': 4.299,
     'mla_q_norm': 8.0,
     'mla_w_uq': 4.003,
     'mla_kv_norm': 8.0,
     'na_rpb': 64.0,
     'moe_b_group': 61.725,
     'moe_b_expert': 61.901,
     'norm2_g': 3.633}
    for name, (base, spread) in spreads.items():
        noise = np.random.default_rng([zlib.crc32(name.encode()), seed]).standard_normal(out[name].shape)
        drawn = base * np.exp(spread * noise) if base else spread * noise
        out[name] = jnp.asarray(drawn.astype(out[name].dtype))
    for name, factor in factors.items():
        out[name] = (out[name] * factor).astype(out[name].dtype)
    return out
```

```python
import concourse.bass as bass
from concourse import mybir
from contextlib import ExitStack

F32 = mybir.dt.float32
I32 = mybir.dt.int32
ALU = mybir.AluOpType
ACT = mybir.ActivationFunctionType
AX = mybir.AxisListType

P = 128
D = 1024
KT = D // P
T = 1024
TT = T // P
C = 256
CT = C // P
AT = TT + CT
BW = 256
HEADS = 4
NOPE, ROPE, VD = 64, 32, 64
QK = NOPE + ROPE
KEYS = T + C
MLA_SCALE = float(QK) ** -0.5
NA_SCALE = 64.0 ** -0.5
EPS = 1e-6
MASK = -1e30
PI = 3.14159265
TURN = 6.283185307179586
ROUND = 1.5 * 2.0 ** 23
EXPERTS, HID = 16, 256
CQ, KR, HY, FN, NQ, NV, GATE, IN_END = 0, 384, 416, 1184, 1440, 1952, 2208, 6304
SLOT = 4096
V_ADAB, V_N1, V_N2, V_QN, V_KVN, V_TAP, V_HB, V_B1, V_F1, V_B2, V_F2, V_END = 0, 48, 56, 64, 66, 67, 85, 89, 90, 91, 92, 93


class Steps:

    def __init__(self, eng, sem):
        self.eng, self.sem, self.base, self.n = eng, sem, 0, 0

    def __call__(self, ins):
        self.mark(ins)
        self.eng.wait_ge(self.sem, self.base + self.n)

    def mark(self, ins):
        ins.then_inc(self.sem, 1)
        self.n += 1

    def sync(self):
        self.eng.wait_ge(self.sem, self.base + self.n)

    def enter(self, i, per):
        self.before = self.base + self.n
        self.base, self.n = self.before + i * per, 0

    def leave(self, rounds, per):
        assert self.n == per, (self.n, per)
        self.base, self.n = self.before + rounds * per, 0


def hybrid_flow_backbone(nc, out, x, c, ctx, c_ctx, ada_w, ada_b, norm1_g, norm2_g, w_in, mla_q_norm, mla_w_uq,
                         mla_kv_norm, mla_w_ukv, hy_short_w, hy_w1, hy_b1, hy_freq1, hy_w2, hy_b2, hy_freq2,
                         hy_w3, hy_bias, na_rpb, w_branch, w_out, moe_w_group, moe_b_group, moe_w_expert,
                         moe_b_expert, moe_w_gate, moe_w_up, moe_w_down, final_norm_g,
                         features, window, filter_basis, forward_basis, inverse_basis, token_basis,
                         relative_columns, pack):
    stack = ExitStack()
    with stack:
        def sb(name, shape, dt=F32):
            return stack.enter_context(nc.sbuf_tensor(name, shape, dt))

        def sem(name):
            return stack.enter_context(nc.semaphore(name))

        def cut(t, at, *shape, rows=P):
            size = 1
            for s in shape:
                size *= s
            v = t[0:rows, at:at + size]
            if len(shape) == 1:
                return v
            names = "abcde"[:len(shape)]
            return v.rearrange(f"p ({' '.join(names)}) -> p {' '.join(names)}", **dict(zip(names, shape)))

        normed = sb("normed", [P, 10240])
        branches = sb("branches", [P, 8192])
        ring = sb("ring", [P, 3 * SLOT])
        arena = sb("arena", [P, 20700])
        pk = sb("pk", [P, 1153])
        ident = sb("ident", [P, P])
        ones = sb("ones", [P, 2])
        vec = sb("vec", [P, V_END])
        small = sb("small", [P, 256])
        psum = stack.enter_context(nc.psum_tensor("psum", [P, 4096], F32))

        def bank(b, lo=0, hi=512):
            return psum[:, b * 512 + lo:b * 512 + hi]

        def slot(n, *shape, rows=P):
            return cut(ring, (n % 3) * SLOT, *shape, rows=rows)

        rope_t = cut(pk, 0, 2, TT, 16)
        row_mask = cut(pk, 256, 10, 64)
        chan_basis = cut(pk, 896, 2 * P)
        alternate = pk[:, 1152:1153]

        scale1 = cut(small, 0, 2, KT)
        shift1 = cut(small, 16, 2, KT)
        scale2 = cut(small, 32, KT)
        shift2 = cut(small, 40, KT)
        cond = cut(small, 48, KT, 2)
        cond_raw = cut(small, 64, 2, KT)
        ssq = cut(small, 80, 32)
        rstd = cut(small, 112, 32)
        filter_norm = cut(small, 144, 4)
        neg_max = cut(small, 148, 8)
        row_sum = cut(small, 156, 8)
        row_inv = cut(small, 164, 8)

        window_sb = cut(normed, 0, TT, 2, BW)
        feat = cut(normed, 4096, T, rows=33)
        arg = cut(normed, 5120, T, rows=64)
        turn = cut(normed, 6144, T, rows=64)
        hid = cut(normed, 7168, T, rows=64)
        w3_sb = cut(normed, 8192, T, rows=64)
        w1_sb = cut(normed, 9216, 64, rows=33)
        w2_sb = cut(normed, 9280, 64, rows=64)
        staged = cut(normed, 9344, P)
        spec = cut(arena, 0, 2, KT, 512)
        fsum = cut(arena, 8192, TT, 512)
        fdif = cut(arena, 12288, TT, 512)
        x_ctx = cut(arena, 16400, CT, D)
        fir_f = cut(arena, 18448, 512)
        fir_b = cut(arena, 18960, 512)
        sq_acc = cut(arena, 19472, 512)
        sq_tmp = cut(arena, 19984, 512)
        x_sb = cut(branches, 0, TT, D)
        hT = cut(normed, 0, KT, KEYS)
        conv = cut(arena, 8192, 6, T)
        raw = cut(arena, 14336, 2, T + 2)
        folded_t = cut(arena, 14336, 4, 2, BW)
        prod_r = cut(arena, 16400, 2, BW)
        prod_i = cut(arena, 16912, 2, BW)
        mix = cut(arena, 17424, T)
        conv_spec = cut(branches, 4096, KT, 2, BW)
        folded = cut(branches, 0, 2, 2, 512)
        halves = cut(branches, 0, 2, 2, 512)
        oT = [cut(branches, n * 2048, 2, T) for n in range(4)]
        fnT = cut(arena, 0, 2, T)
        chan_mixed = cut(arena, 2048, TT, 2, 2, P)
        sine_part = cut(arena, 6144, 2, 512)

        mla_tok = cut(arena, 0, AT, 416)
        cqT = cut(arena, 4160, 2, T)
        ckvT = cut(arena, 6208, KEYS)
        q_tok = cut(arena, 7488, TT, HEADS, QK)
        k_tok = cut(arena, 10560, AT, HEADS, QK)
        v_tok = cut(arena, 14400, AT, HEADS * VD)
        qT = cut(arena, 0, HEADS, T, rows=QK)
        kT = cut(arena, 4160, HEADS, KEYS, rows=QK)
        prob = cut(arena, 10560, 2, KEYS)
        probT = cut(arena, 13120, AT, P)
        w_uq = cut(arena, 16960, 2, HEADS * QK)
        w_ukv = cut(arena, 17728, HEADS * (NOPE + VD))
        q_now = cut(arena, 18240, 2, P, rows=QK)
        rot = [cut(arena, 18496 + 512 * n, TT, HEADS, 16) for n in range(4)]
        oa_tok = cut(branches, 0, TT, BW)
        nqT = cut(arena, 0, HEADS, T, rows=64)
        nkT = cut(arena, 4096, HEADS, KEYS)
        nv_tok = cut(arena, 9216, AT, BW)
        rel_bias = cut(arena, 11776, HEADS, 14 * 64)
        inner_bias = cut(arena, 15360, 640)
        nprob = cut(arena, 16000, 2, 896)
        nprobT = cut(arena, 17792, 7, P)
        nq_now = cut(arena, 18688, 2, P)
        rpb_t = cut(small, 176, HEADS, 14, rows=64)
        od_tok = cut(branches, 6144, TT, BW)
        NA_TILES = [(0, 512, 384), (0, 512, 256)] + [(q - 2, 640, None) for q in range(2, 6)] + \
                   [(4, 512, 128), (4, 512, 0)]
        merged = cut(arena, 0, KT, T)
        cond_rows = cut(arena, 0, KT, P)
        wb = cut(arena, 8192, 2, 8, P)
        gate_sb = cut(arena, 15360, 2, 512)
        gated = cut(arena, 12288, 512)
        final_gain = cut(arena, 16384, D)
        res_gate1 = cut(arena, 17408, D)
        res_gate2 = cut(arena, 18432, D)
        x1 = cut(normed, 0, TT, D)
        x1n = cut(branches, 0, TT, D)
        h2T = cut(arena, 0, KT, T)
        square2 = cut(normed, 8192, D)
        wr = cut(arena, 19456, KT, 20)
        wr_bias = cut(arena, 19616, 20)
        logits = cut(arena, 19640, TT, 20)
        route = cut(arena, 19800, TT, EXPERTS)
        pick = cut(arena, 19928, TT, 16)
        group_hot, expert_hot, second_hot, expert_logit = (cut(arena, 20056 + 32 * n, TT, 4) for n in range(4))
        rc = [cut(arena, 20184 + 8 * n, TT) for n in range(8)]
        group_exp = cut(arena, 20248, TT, 4)
        w_down = cut(arena, 8192, 2, 2, D)
        actT = cut(arena, 12288, 2, T)
        silu = cut(arena, 14336, 2, 512)
        moe = cut(branches, 0, TT, D)
        s = {n: sem(n) for n in (
            "in_small", "in_x", "in_rope", "pool_const", "pool_pad", "dve_chain", "act_chain", "dve_zero",
            "pe_vec", "dve_vec", "act_cond", "pe_sin", "dve_arg", "act_sin", "pe_filt", "dve_filt", "pool_sq",
            "pe_spec", "act_spec", "pe_fnorm", "pe_ada", "act_ssq", "dve_xn", "pe_xT", "act_hT",
            "pe_hy", "act_hy", "dve_conv", "dve_fold", "pe_fold", "act_fold", "pe_fwd", "dve_spec",
            "pe_inv", "act_inv", "dve_z", "pe_fn", "act_fn", "pe_chan", "act_chan", "pe_tok", "act_tok", "dve_oc",
            "in_uq", "pe_mla", "dve_mla", "act_msq", "act_mrt", "dve_mn", "pe_mT", "act_mT", "pe_uq", "dve_uq", "pe_ukv",
            "act_ukv", "dve_rope", "pe_qT", "dve_qT", "pe_kT", "act_kT", "pool_q", "pe_qk", "dve_mx", "act_p", "pe_t", "dve_pt",
            "act_pt", "pe_pv", "dve_o", "pe_oaT", "act_oaT", "pe_nqk", "act_nqk", "dve_nqk", "pe_nv", "act_nv", "in_rpb", "pool_rpb",
            "pe_bb", "dve_bb", "pool_nq", "pe_nqk2", "dve_nmx", "act_np", "pe_nt", "act_npt", "pe_npv", "dve_no", "pe_odT", "act_odT",
            "pool_npad",
            "pe_ada2", "dve_ada2", "pe_res", "dve_res", "in_res", "dve_cond", "pe_gg", "pe_gate", "act_gate", "dve_gate",
            "in_w_out", "in_x1", "pe_out", "dve_x1", "act_ssq2", "act_rt2", "dve_ms2", "dve_x1n", "pe_hT2", "act_hT2",
            "in_router", "pe_route", "act_route", "dve_route", "pe_au", "act_silu", "dve_act", "pe_down", "dve_moe", "act_fin",
            "in_final", "dve_fin", "dve_fms", "act_frt",
            "stored", "in_w3", "in_pack", "in_vec", "in_ctx", "in_win", "in_feat", "dve_mod")}
        in_gate = [sem(f"in_gate{n}") for n in range(2)]
        in_expert = [sem(f"in_expert{n}") for n in range(2)]
        in_ring = [sem(f"in_ring{n}") for n in range(3)]
        block = stack.enter_context(nc.Block())

        w_in_k = w_in[0].rearrange("(t p) n -> p t n", p=P)
        ada_k = ada_w[0].rearrange("(p t) n -> p t n", t=KT)

        chunks = []

        def chunk(src, shape, done, value):
            n = len(chunks)
            chunks.append((src, slot(n, *shape), done, value))
            return n

        K_SPEC = [chunk(filter_basis[:, 2 * n:2 * n + 2], (2, TT, 2, P), "pe_spec", 4 * n + 4) for n in range(4)]
        K_ADA1 = [chunk(ada_k[:, :, n * 512:n * 512 + 512], (KT, 512), "pe_ada", n + 1) for n in range(4)]
        K_HY = [chunk(w_in_k[:, :, HY:HY + 512], (KT, 512), "pe_hy", 8),
                chunk(w_in_k[:, :, HY + 512:FN], (KT, 256), "pe_hy", 12)]
        K_CONV = []
        K_ADA2 = []

        def ada_columns(n):
            K_ADA2.append(chunk(ada_k[:, :, (6 + n) * 512:(7 + n) * 512], (KT, 512), "pe_ada2", n + 1))

        for n in range(2):
            K_CONV.append((
                [chunk(forward_basis[:, 4 * m:4 * m + 4], (4, 4, 2, P), "pe_fwd", 8 * n + 4 * m + 4) for m in range(2)],
                [chunk(inverse_basis[:, 4 * m:4 * m + 4], (4, 2, 512), "pe_inv", 2 * n + m + 1) for m in range(2)]))
            ada_columns(n)
        K_FN = chunk(w_in_k[:, :, FN:NQ], (KT, BW), "pe_fn", 4)
        K_TOK = [chunk(token_basis[:, m], (TT, 512), "pe_tok", m + 1) for m in range(2)]

        ada_columns(2)
        K_MLA = chunk(w_in_k[:, :, CQ:HY], (KT, 416), "pe_mla", AT)
        ada_columns(3)
        K_NQK = chunk(w_in_k[:, :, NQ:NV], (KT, 512), "pe_nqk", 10)
        K_NV = chunk(w_in_k[:, :, NV:GATE], (KT, BW), "pe_nv", AT)
        K_REL = []
        for n in range(2):
            K_REL.append(len(chunks))
            chunks.append((relative_columns[:, n * SLOT:n * SLOT + SLOT], slot(len(chunks), 32, P, rows=64).rearrange(
                "p a b -> p (a b)"), "pe_bb", 4 * n + 4))
        K_RES = [chunk(ada_k[:, :, n * 512:n * 512 + 512], (KT, 512), "pe_res", m + 1)
                 for m, n in enumerate((4, 5, 10, 11))]
        G0 = len(chunks)
        gate_slots = [slot(G0 + n, KT, 4, P) for n in range(2)]
        w_out_slots = [slot(G0 + 2, KT, 512), slot(G0, KT, 512)]
        expert_slots = [slot(G0 + 1 + n, 2, KT, HID) for n in range(2)]
        def arrived(eng, n):
            eng.wait_ge(in_ring[n % 3], 16 * (n // 3 + 1))

        def na_group(g):
            block_of = g // 2
            if block_of < 2:
                return nqT, block_of * 512, 512
            return nkT, (block_of - 2) * 512, 512 if block_of < 4 else C
        @block.sync
        def _(sp):
            def load(dst, src, signal):
                sp.dma_start(dst, src).then_inc(s[signal], 16)

            sp.wait_ge(s["dve_zero"], 1)
            row = 0
            for src, n in ((ada_b, 48), (norm1_g, 8), (norm2_g, 8), (mla_q_norm, 2), (mla_kv_norm, 1),
                           (hy_short_w, 18), (hy_bias, 4)):
                flat = src[0] if len(src.shape) == 2 else src[0].rearrange("a n -> (a n)")
                load(staged[row:row + n, :], flat.rearrange("(r q) -> r q", q=P), "in_vec")
                row += n
            for src in (hy_b1, hy_freq1, hy_b2, hy_freq2):
                load(staged[row:row + 1, 0:64], src, "in_vec")
                row += 1
            load(w1_sb, hy_w1[0], "in_feat")
            load(w2_sb, hy_w2[0], "in_feat")
            load(feat, features, "in_feat")
            load(w3_sb, hy_w3[0], "in_w3")
            load(window_sb, window, "in_win")
            load(cond_raw[:, 0, :], c[0].rearrange("(p t) -> p t", t=KT), "in_small")
            load(cond_raw[:, 1, :], c_ctx.rearrange("(p t) -> p t", t=KT), "in_small")
            sp.wait_ge(s["pool_rpb"], 1)
            with nc.allow_non_contiguous_dma(reason="a small table, transposed"):
                for r in range(2):
                    for h in range(HEADS):
                        load(rpb_t[32 * r:32 * r + 31, h, :], na_rpb[0, h, 1 - r:15 - r, :].rearrange("d c -> c d"), "in_rpb")
            for n, (src, dst, _, _) in enumerate(chunks):
                if n == 1:
                    load(x_sb, x[0].rearrange("(t p) d -> p t d", p=P), "in_x")
                    load(x_ctx, ctx[0].rearrange("(t p) d -> p t d", p=P), "in_ctx")
                    load(pk[:, :], pack, "in_pack")
                if n >= 3:
                    sp.wait_ge(s[chunks[n - 3][2]], chunks[n - 3][3])
                sp.dma_start(dst, src).then_inc(in_ring[n % 3], 16)
                if n == K_MLA:
                    sp.wait_ge(s["pe_tok"], 2)
                    sp.wait_ge(s["dve_oc"], 2)
                    load(w_uq, mla_w_uq[0].rearrange("(t p) n -> p t n", p=P), "in_uq")
                    load(w_ukv, mla_w_ukv[0], "in_uq")

            sp.wait_ge(s["pe_odT"], 4)
            for dst, lo in ((res_gate1, 2048), (res_gate2, 5120)):
                load(dst, ada_b[0:1, lo:lo + D].to_broadcast([P, D]), "in_res")
            load(final_gain, final_norm_g.rearrange("(a d) -> a d", a=1).to_broadcast([P, D]), "in_final")
            load(wr[:, :, 0:4], moe_w_group[0].rearrange("(t p) n -> p t n", p=P), "in_router")
            load(wr[:, :, 4:20], moe_w_expert[0].rearrange("(t p) n -> p t n", p=P), "in_router")
            load(wr_bias[:, 0:4], moe_b_group[0:1, :].to_broadcast([P, 4]), "in_router")
            load(wr_bias[:, 4:20], moe_b_expert[0:1, :].to_broadcast([P, 16]), "in_router")

            def load_gate(d, m):
                for n in range(4):
                    sp.dma_start(gate_slots[m][:, :, n, :], w_in_k[:, :, bass.ds(d * P + GATE + n * D, P)])\
                      .then_inc(in_gate[m], 16)
                sp.dma_start(wb[:, m, :, :], w_branch[0].rearrange("n (t p) d -> p (n t) d", p=P)[:, :, bass.ds(d * P, P)])\
                  .then_inc(in_gate[m], 16)

            for m in range(2):
                sp.wait_ge(s[chunks[G0 + m - 3][2]], chunks[G0 + m - 3][3])
                load_gate(m, m)
            sp.wait_ge(s[chunks[G0 - 1][2]], chunks[G0 - 1][3])
            w_out_k = w_out[0].rearrange("(t p) n -> p t n", p=P)
            load(w_out_slots[0], w_out_k[:, :, 0:512], "in_w_out")
            with sp.Fori(0, 3) as i:
                for m in range(2):
                    sp.wait_ge(s["pe_gate"], i * 16 + 8 * (m + 1))
                    load_gate(i * 2 + m + 2, m)
            sp.wait_ge(s["pe_gate"], 56)
            sp.wait_ge(s["in_w_out"], 16)
            load(w_out_slots[1], w_out_k[:, :, 512:1024], "in_w_out")
            sp.wait_ge(s["pe_gate"], 64)
            load(x1, x[0].rearrange("(t p) d -> p t d", p=P), "in_x1")

            def load_expert(e, m):
                for n, w in enumerate((moe_w_gate, moe_w_up)):
                    sp.dma_start(expert_slots[m][:, n, :, :], w[0, bass.ds(e, 1)].rearrange("e (t p) f -> p (e t) f", p=P))\
                      .then_inc(in_expert[m], 16)
                sp.dma_start(w_down[:, m, :, :], moe_w_down[0, bass.ds(e, 1)].rearrange("e (t p) d -> p (e t) d", p=P))\
                  .then_inc(in_expert[m], 16)

            sp.wait_ge(s["dve_gate"], 64)
            load_expert(0, 0)
            sp.wait_ge(s["pe_out"], 8)
            load_expert(1, 1)
            with sp.Fori(0, EXPERTS // 2 - 1) as i:
                for m in range(2):
                    sp.wait_ge(s["pe_down"], i * 32 + 16 * (m + 1))
                    load_expert(i * 2 + m + 2, m)
            for i in range(TT):
                sp.wait_ge(s["dve_fin"], i + 1)
                sp.dma_start(out[0, i * P:i * P + P, :], x1[:, i, :]).then_inc(s["stored"], 16)
            sp.wait_ge(s["stored"], 16 * TT)

        @block.gpsimd
        def _(pool):
            pool.memset(ident[:, :], 0.0).then_inc(s["pool_const"], 1)
            pool.memset(rpb_t, MASK).then_inc(s["pool_rpb"], 1)
            pool.memset(ones[:, :], 1.0).then_inc(s["pool_const"], 1)
            pool.wait_ge(s["pool_const"], 2)
            pool.affine_select(out=ident[:, :], in_=ident[:, :], compare_op=ALU.not_equal, fill=1.0, base=0,
                               pattern=[[-1, P]], channel_multiplier=1).then_inc(s["pool_const"], 1)
            step = Steps(pool, s["pool_sq"])
            for i in range(TT):
                pool.wait_ge(s["dve_filt"], i + 1)
                for f in (fsum, fdif):
                    if i == 0 and f is fsum:
                        step(pool.tensor_tensor(sq_acc, f[:, i, :], f[:, i, :], ALU.mult))
                        continue
                    step(pool.tensor_tensor(sq_tmp, f[:, i, :], f[:, i, :], ALU.mult))
                    step(pool.tensor_tensor(sq_acc, sq_acc, sq_tmp, ALU.add))
            pool.wait_ge(s["pe_spec"], 16)
            pool.memset(raw[:, :, 0:1], 0.0).then_inc(s["pool_pad"], 1)
            pool.memset(raw[:, :, T + 1:T + 2], 0.0).then_inc(s["pool_pad"], 1)
            pool.wait_ge(s["dve_qT"], 8)
            with pool.Fori(0, HEADS) as h:
                for q in range(TT):
                    pool.wait_ge(s["pe_qk"], h * TT + max(q - 1, 0))
                    pool.tensor_copy(q_now[:, q % 2, :].rearrange("p (a w) -> p a w", a=1),
                                     qT[:, bass.ds(h, 1), q * P:q * P + P]).then_inc(s["pool_q"], 1)
            pool.wait_ge(s["pe_oaT"], 4)
            pool.memset(nkT[64:128, :, :], 0.0).then_inc(s["pool_npad"], 1)
            pool.memset(nq_now[64:128, :, :], 0.0).then_inc(s["pool_npad"], 1)
            pool.wait_ge(s["act_nqk"], 10)
            pool.wait_ge(s["dve_nqk"], 10)
            with pool.Fori(0, HEADS) as h:
                for q in range(TT):
                    pool.wait_ge(s["pe_nqk2"], h * TT + max(q - 1, 0))
                    pool.tensor_copy(nq_now[0:64, q % 2, :].rearrange("p (a w) -> p a w", a=1),
                                     nqT[:, bass.ds(h, 1), q * P:q * P + P]).then_inc(s["pool_nq"], 1)

        @block.scalar
        def _(act):
            step = Steps(act, s["act_chain"])
            for layer in range(2):
                act.wait_ge(s["dve_arg"], layer + 1)
                if layer == 1:
                    act.wait_ge(s["pe_sin"], 4)
                act.activation(hid, arg, ACT.Sin).then_inc(s["act_sin"], 1)
            act.wait_ge(s["in_small"], 32)
            act.activation(cond.rearrange("p t v -> p v t"), cond_raw, ACT.Silu).then_inc(s["act_cond"], 1)
            act.wait_ge(s["in_x"], 16)
            act.wait_ge(s["in_ctx"], 16)
            scratch = cut(normed, 4096, D)
            for i in range(AT):
                src = x_sb[:, i, :] if i < TT else x_ctx[:, i - TT, :]
                step.mark(act.activation(scratch, src, ACT.Square, accum_out=ssq[:, i:i + 1]))
                step.sync()
            act.wait_ge(s["dve_vec"], 2)
            act.activation(rstd[:, 0:AT], ssq[:, 0:AT], ACT.Sqrt).then_inc(s["act_ssq"], 1)
            for g in range(16):
                act.wait_ge(s["pe_spec"], g + 1)
                act.activation(spec[:, g % 2, g // 2, :], bank(g % 4), ACT.Copy).then_inc(s["act_spec"], 1)
            act.wait_ge(s["dve_vec"], 3)
            act.activation(filter_norm, filter_norm, ACT.Sqrt).then_inc(s["act_ssq"], 1)
            act.wait_ge(s["dve_mod"], 1)
            act.wait_ge(s["dve_xn"], AT)
            for n in range(3 * KT):
                kt, g = n // 3, n % 3
                w = 512 if g < 2 else C
                act.wait_ge(s["pe_xT"], n + 1)
                act.activation(hT[:, kt, g * 512:g * 512 + w], bank(n % 4, 0, w), ACT.Identity,
                               bias=shift1[:, g // 2, kt:kt + 1], scale=scale1[:, g // 2, kt:kt + 1])\
                   .then_inc(s["act_hT"], 1)
            act.wait_ge(s["pool_pad"], 2)
            for g in range(12):
                ct, half = g // 2, g % 2
                if half == 0 and ct >= 2:
                    act.wait_ge(s["dve_conv"], ct - 1)
                act.wait_ge(s["pe_hy"], g + 1)
                act.activation(raw[:, ct % 2, 1 + half * 512:513 + half * 512], bank(4 + g % 4), ACT.Copy)\
                   .then_inc(s["act_hy"], 1)
            for order in range(2):
                for tt in range(4):
                    if order == 0 and tt == 0:
                        act.wait_ge(s["dve_conv"], 6)
                    act.wait_ge(s["pe_fold"], 4 * order + tt + 1)
                    act.activation(folded_t[:, tt, :, :], bank(tt), ACT.Copy).then_inc(s["act_fold"], 1)
                act.wait_ge(s["pe_inv"], 2 * order + 2)
                for ct in range(2):
                    for ab in range(2):
                        act.activation(halves[:, ct, ab, :], bank(2 * ct + ab), ACT.Copy,
                                       scale=filter_norm[:, 2 * order + ct:2 * order + ct + 1])\
                           .then_inc(s["act_inv"], 1)
            act.wait_ge(s["dve_z"], 4)
            for g in range(4):
                act.wait_ge(s["pe_fn"], g + 1)
                act.activation(fnT[:, g // 2, (g % 2) * 512:(g % 2) * 512 + 512], bank(g), ACT.Copy)\
                   .then_inc(s["act_fn"], 1)
            for i in range(TT):
                act.wait_ge(s["pe_chan"], i + 1)
                act.activation(chan_mixed[:, i, :, :, :], bank(4 + i % 4), ACT.Copy).then_inc(s["act_chan"], 1)
            act.wait_ge(s["pe_tok"], 2)
            for ct in range(2):
                act.activation(sine_part[:, ct, :], bank(4 + ct), ACT.Copy).then_inc(s["act_tok"], 1)
            square = q_tok[:, 0, :, :].rearrange("p h f -> p (h f)")
            sums = Steps(act, s["act_msq"])
            for i in range(AT):
                act.wait_ge(s["dve_mla"], i + 1)
                if i < TT:
                    sums(act.activation(square[:, 0:256], mla_tok[:, i, 0:256], ACT.Square, accum_out=ssq[:, i:i + 1]))
                sums(act.activation(square[:, 0:128], mla_tok[:, i, 256:384], ACT.Square,
                                    accum_out=ssq[:, 8 + i:9 + i]))
            act.wait_ge(s["dve_mn"], 2)
            act.activation(rstd[:, 0:18], ssq[:, 0:18], ACT.Sqrt).then_inc(s["act_mrt"], 1)
            for g in range(7):
                act.wait_ge(s["pe_mT"], g + 1)
                if g < 4:
                    act.activation(cqT[:, g // 2, (g % 2) * 512:(g % 2) * 512 + 512], bank(g), ACT.Copy,
                                   scale=vec[:, V_QN + g // 2:V_QN + g // 2 + 1]).then_inc(s["act_mT"], 1)
                else:
                    w = 512 if g < 6 else C
                    act.activation(ckvT[:, (g - 4) * 512:(g - 4) * 512 + w], bank(g, 0, w), ACT.Copy,
                                   scale=vec[:, V_KVN:V_KVN + 1]).then_inc(s["act_mT"], 1)
            for i in range(AT):
                act.wait_ge(s["pe_ukv"], i + 1)
                kv = bank(4 + i % 4).rearrange("p (h f) -> p h f", h=HEADS)
                act.activation(k_tok[:, i, :, 0:NOPE], kv[:, :, 0:NOPE], ACT.Copy).then_inc(s["act_ukv"], 1)
                act.activation(v_tok[:, i, :].rearrange("p (h f) -> p h f", h=HEADS), kv[:, :, NOPE:], ACT.Copy)\
                   .then_inc(s["act_ukv"], 1)
            for g in range(12):
                w = 512 if g % 3 < 2 else C
                act.wait_ge(s["pe_kT"], g + 1)
                if g == 0:
                    act.wait_ge(s["pe_qT"], 8)
                act.activation(kT[:, g // 3, (g % 3) * 512:(g % 3) * 512 + w], psum[0:QK, (4 + g % 4) * 512:(4 + g % 4) * 512 + w],
                               ACT.Copy).then_inc(s["act_kT"], 1)
            act.wait_ge(s["pe_kT"], 12)
            with act.Fori(0, HEADS) as h:
                def exponentials(q):
                    act.wait_ge(s["dve_mx"], h * TT + q + 1)
                    act.wait_ge(s["pe_t"], h * 3 * TT + 3 * max(q - 1, 0))
                    act.activation(prob[:, q % 2, :], psum[:, (q % 2) * 1536:(q % 2) * 1536 + KEYS], ACT.Exp,
                                   bias=neg_max[:, q:q + 1], scale=MLA_SCALE, accum_out=row_sum[:, q:q + 1])\
                       .then_inc(s["act_p"], 1)

                exponentials(0)
                for q in range(TT):
                    act.wait_ge(s["pe_pv"], h * TT + q)
                    act.wait_ge(s["pe_t"], h * 3 * TT + 3 * q + 2)
                    act.activation(probT[:, 4:8, :], bank(7), ACT.Copy).then_inc(s["act_pt"], 1)
                    if q + 1 < TT:
                        exponentials(q + 1)
            for g in range(4):
                act.wait_ge(s["pe_oaT"], 4)
                act.activation(oT[0][:, g // 2, (g % 2) * 512:(g % 2) * 512 + 512], bank(g), ACT.Copy)\
                   .then_inc(s["act_oaT"], 1)
            for g in range(10):
                act.wait_ge(s["pe_nqk"], g + 1)
                dst, lo, w = na_group(g)
                act.activation(dst[0:64, (g % 2) * 2, lo:lo + w], psum[0:64, (g % 4) * 512:(g % 4) * 512 + w], ACT.Copy)\
                   .then_inc(s["act_nqk"], 1)
            for i in range(AT):
                act.wait_ge(s["pe_nv"], i + 1)
                act.activation(nv_tok[:, i, :], bank(4 + i % 4, 0, BW), ACT.Copy).then_inc(s["act_nv"], 1)
            with act.Fori(0, HEADS) as h:
                def exponentials(q):
                    n = NA_TILES[q][1] + C
                    act.wait_ge(s["dve_nmx"], h * TT + q + 1)
                    act.activation(nprob[:, q % 2, 0:n], nprob[:, q % 2, 0:n], ACT.Exp, bias=neg_max[:, q:q + 1],
                                   accum_out=row_sum[:, q:q + 1]).then_inc(s["act_np"], 1)

                exponentials(0)
                for q in range(TT):
                    n = (NA_TILES[q][1] + C) // P
                    act.wait_ge(s["pe_npv"], h * TT + q)
                    for r in range(2):
                        act.wait_ge(s["pe_nt"], h * 2 * TT + 2 * q + r + 1)
                        w = min(4, n - 4 * r)
                        act.activation(nprobT[:, 4 * r:4 * r + w, :], bank(4 + r, 0, w * P), ACT.Copy)\
                           .then_inc(s["act_npt"], 1)
                    if q + 1 < TT:
                        exponentials(q + 1)
            for g in range(4):
                act.wait_ge(s["pe_odT"], 4)
                act.activation(oT[3][:, g // 2, (g % 2) * 512:(g % 2) * 512 + 512], bank(g), ACT.Copy)\
                   .then_inc(s["act_odT"], 1)
            with act.Fori(0, KT // 2) as i:
                for m in range(16):
                    if m < 2:
                        act.wait_ge(s["dve_gate"], i * 16)
                    else:
                        act.wait_ge(s["dve_gate"], i * 16 + m - 1)
                    act.wait_ge(s["pe_gg"], i * 16 + m + 1)
                    act.activation(gate_sb[:, m % 2, :], bank(m % 4), ACT.Sigmoid).then_inc(s["act_gate"], 1)
            sums = Steps(act, s["act_ssq2"])
            for g in range(2):
                for i in range(4 * g, 4 * g + 4):
                    act.wait_ge(s["dve_x1"], TT + i + 1)
                    sums(act.activation(square2, x1[:, i, :], ACT.Square, accum_out=ssq[:, i:i + 1]))
                act.wait_ge(s["dve_ms2"], g + 1)
                act.activation(rstd[:, 4 * g:4 * g + 4], ssq[:, 4 * g:4 * g + 4], ACT.Sqrt).then_inc(s["act_rt2"], 1)
            act.wait_ge(s["dve_ada2"], 6)
            for n in range(2 * KT):
                g, kt = n // KT, n % KT
                act.wait_ge(s["pe_hT2"], n + 1)
                act.activation(h2T[:, kt, g * 512:g * 512 + 512], bank(n % 4), ACT.Identity,
                               bias=shift2[:, kt:kt + 1], scale=scale2[:, kt:kt + 1]).then_inc(s["act_hT2"], 1)
            act.wait_ge(s["dve_route"], 1)
            act.activation(group_exp, group_exp, ACT.Exp).then_inc(s["act_route"], 1)
            act.wait_ge(s["dve_route"], 2)
            act.activation(rc[3], rc[3], ACT.Exp).then_inc(s["act_route"], 1)
            with act.Fori(0, EXPERTS // 2) as i:
                for m in range(8):
                    act.wait_ge(s["dve_act"], i * 8 + max(m - 1, 0))
                    act.wait_ge(s["pe_au"], i * 8 + m + 1)
                    act.activation(silu[:, m % 2, :], bank(2 * (m % 2)), ACT.Silu).then_inc(s["act_silu"], 1)
            sums = Steps(act, s["act_fin"])
            for i in range(TT):
                act.wait_ge(s["dve_moe"], 16 * EXPERTS + i + 1)
                sums(act.activation(square2, x1[:, i, :], ACT.Square, accum_out=ssq[:, i:i + 1]))
                act.wait_ge(s["dve_fms"], i + 1)
                act.activation(rstd[:, i:i + 1], ssq[:, i:i + 1], ACT.Sqrt).then_inc(s["act_frt"], 1)

        @block.vector
        def _(dve):
            step = Steps(dve, s["dve_chain"])
            dve.memset(staged, 0.0).then_inc(s["dve_zero"], 1)
            dve.wait_ge(s["pe_vec"], 1)
            dve.tensor_copy(vec[:, :], bank(7, 0, V_END)).then_inc(s["dve_vec"], 1)
            dve.wait_ge(s["dve_vec"], 1)
            for layer, (b, f) in enumerate(((V_B1, V_F1), (V_B2, V_F2))):
                dve.wait_ge(s["pe_sin"], 2 * layer + 2)
                if layer == 1:
                    dve.wait_ge(s["act_sin"], 1)
                step(dve.tensor_scalar(arg, psum[0:64, layer * 1024:layer * 1024 + 1024], vec[0:64, b:b + 1],
                                       vec[0:64, f:f + 1], ALU.add, ALU.mult))
                step(dve.tensor_scalar(turn, arg, 1.0 / TURN, ROUND, ALU.mult, ALU.add))
                step(dve.tensor_scalar(turn, turn, -ROUND, -TURN, ALU.add, ALU.mult))
                step(dve.tensor_tensor(arg, arg, turn, ALU.add))
                dve.tensor_scalar(arg, arg, PI, -PI, ALU.min, ALU.max).then_inc(s["dve_arg"], 1)
            dve.wait_ge(s["in_win"], 16)
            for i in range(TT):
                dve.wait_ge(s["pe_filt"], i + 1)
                b = 4 + 2 * (i % 2)
                for dst, n in ((fir_f, 0), (fir_b, 1)):
                    step.mark(dve.tensor_tensor(
                        dst.rearrange("p (o w) -> p o w", o=2), bank(b + n).rearrange("p (o w) -> p o w", o=2),
                        window_sb[:, i, n:n + 1, :].to_broadcast([P, 2, BW]), ALU.mult))
                step.sync()
                step.mark(dve.tensor_tensor(fsum[:, i, :], fir_f, fir_b, ALU.add))
                dve.tensor_tensor(fdif[:, i, :], fir_f, fir_b, ALU.subtract).then_inc(s["dve_filt"], 1)
                dve.wait_ge(s["dve_filt"], i + 1)
                step.sync()
            dve.wait_ge(s["act_chain"], AT)
            dve.tensor_scalar(ssq[:, 0:AT], ssq[:, 0:AT], 1.0 / D, EPS, ALU.mult, ALU.add).then_inc(s["dve_vec"], 1)
            dve.wait_ge(s["act_ssq"], 1)
            step(dve.reciprocal(rstd[:, 0:AT], rstd[:, 0:AT]))
            for i in range(AT):
                row = x_sb[:, i, :] if i < TT else x_ctx[:, i - TT, :]
                dve.tensor_scalar(row, row, rstd[:, i:i + 1], None, ALU.mult).then_inc(s["dve_xn"], 1)
            dve.wait_ge(s["pe_fnorm"], 1)
            dve.tensor_scalar(filter_norm, bank(4, 0, 4), 0.5, EPS, ALU.mult, ALU.add).then_inc(s["dve_vec"], 1)
            dve.wait_ge(s["act_ssq"], 2)
            step(dve.reciprocal(filter_norm, filter_norm))
            dve.wait_ge(s["pe_ada"], 4)
            for v in range(2):
                m = bank(5, 0, 32).rearrange("p (b v) -> p b v", v=2)
                step(dve.tensor_tensor(shift1[:, v, :], m[:, 0:8, v], vec[:, 0:8], ALU.add))
                step(dve.tensor_tensor(scale1[:, v, :], m[:, 8:16, v], vec[:, 8:16], ALU.add))
                ins = dve.scalar_tensor_tensor(out=scale1[:, v, :], in0=scale1[:, v, :], scalar=1.0,
                                               in1=vec[:, V_N1:V_N1 + 8], op0=ALU.add, op1=ALU.mult)
                if v == 0:
                    step(ins)
                else:
                    ins.then_inc(s["dve_mod"], 1)
            for ct in range(6):
                dve.wait_ge(s["act_hy"], 2 * ct + 2)
                tap = [vec[:, V_TAP + 6 * j + ct:V_TAP + 6 * j + ct + 1] for j in range(3)]
                u = raw[:, ct % 2, :]
                step(dve.tensor_scalar(conv[:, ct, :], u[:, 1:T + 1], tap[1], None, ALU.mult))
                step(dve.scalar_tensor_tensor(out=conv[:, ct, :], in0=u[:, 0:T], scalar=tap[0],
                                              in1=conv[:, ct, :], op0=ALU.mult, op1=ALU.add))
                dve.scalar_tensor_tensor(out=conv[:, ct, :], in0=u[:, 2:T + 2], scalar=tap[2],
                                         in1=conv[:, ct, :], op0=ALU.mult, op1=ALU.add)\
                   .then_inc(s["dve_conv"], 1)
            dve.wait_ge(s["dve_conv"], 6)
            def ada_column(n):
                dst = (shift2, scale2)[n // 2][:, 4 * (n % 2):4 * (n % 2) + 4]
                b = V_ADAB + 24 + 4 * n
                dve.wait_ge(s["pe_ada2"], n + 1)
                dve.tensor_tensor(dst, bank((4, 4, 7, 7)[n], 0, 8).rearrange("p (m v) -> p m v", v=2)[:, :, 0],
                                  vec[:, b:b + 4], ALU.add).then_inc(s["dve_ada2"], 1)

            for order in range(2):
                if order == 1:
                    dve.wait_ge(s["dve_z"], 2)
                for ct in range(2):
                    z = conv[:, ct, :]
                    for n, op in enumerate((ALU.add, ALU.subtract)):
                        dve.tensor_tensor(folded[:, n, ct, :], z[:, 0:512], z[:, T - 1:511:-1], op)\
                           .then_inc(s["dve_fold"], 1)
                for j in range(KT):
                    re, im = (spec[:, n, j:j + 1, order * BW:order * BW + BW].to_broadcast([P, 2, BW]) for n in range(2))
                    u = bank(4 + j % 4).rearrange("p (n w) -> p n w", n=2)
                    if j == 0 and order == 0:
                        dve.wait_ge(s["act_spec"], 16)
                    dve.wait_ge(s["pe_fwd"], 8 * order + j + 1)
                    step.mark(dve.tensor_tensor(prod_r, u, re, ALU.mult))
                    step(dve.tensor_tensor(prod_i, u, im, ALU.mult))
                    step.mark(dve.tensor_tensor(conv_spec[:, j, 0, :], prod_r[:, 0, :], prod_i[:, 1, :], ALU.subtract))
                    dve.tensor_tensor(conv_spec[:, j, 1, :], prod_r[:, 1, :], prod_i[:, 0, :], ALU.add)\
                       .then_inc(s["dve_spec"], 1)
                    dve.wait_ge(s["dve_spec"], 8 * order + j + 1)
                    step.sync()
                ada_column(order)
                dve.wait_ge(s["act_inv"], 4 * order + 4)
                for ct in range(2):
                    a, b = halves[:, ct, 0, :], halves[:, ct, 1, :]
                    step.mark(dve.tensor_tensor(mix[:, 0:512], a, b, ALU.add))
                    step(dve.tensor_tensor(mix[:, T - 1:511:-1], a, b, ALU.subtract))
                    h = V_HB + 2 * order + ct
                    step(dve.scalar_tensor_tensor(out=mix, in0=conv[:, ct, :], scalar=vec[:, h:h + 1], in1=mix,
                                                  op0=ALU.mult, op1=ALU.add))
                    dst = conv[:, ct, :] if order == 0 else oT[1][:, ct, :]
                    dve.tensor_tensor(dst, mix, conv[:, 2 + 2 * order + ct, :], ALU.mult).then_inc(s["dve_z"], 1)
                    dve.wait_ge(s["dve_z"], 2 * order + ct + 1)
            dve.wait_ge(s["act_tok"], 2)
            for ct in range(2):
                o = oT[2][:, ct, :]
                sn = sine_part[:, ct, :]
                step.mark(dve.tensor_tensor(o[:, 0:512], bank(ct), sn, ALU.add))
                step.mark(dve.tensor_tensor(o[:, T - 1:512:-1], bank(ct, 1, 512), sn[:, 1:512], ALU.subtract))
                dve.tensor_copy(o[:, 512:513], bank(2, ct, ct + 1)).then_inc(s["dve_oc"], 1)
            step.sync()
            ada_column(2)
            for i in range(AT):
                lo = 0 if i < TT else 256
                dve.wait_ge(s["pe_mla"], i + 1)
                dve.tensor_copy(mla_tok[:, i, lo:416], bank(i % 4, lo, 416)).then_inc(s["dve_mla"], 1)
            dve.wait_ge(s["act_msq"], 2 * TT + CT)
            norms = Steps(dve, s["dve_mn"])
            norms.mark(dve.tensor_scalar(ssq[:, 0:8], ssq[:, 0:8], 1.0 / 256, EPS, ALU.mult, ALU.add))
            norms.mark(dve.tensor_scalar(ssq[:, 8:18], ssq[:, 8:18], 1.0 / 128, EPS, ALU.mult, ALU.add))
            dve.wait_ge(s["act_mrt"], 1)
            dve.wait_ge(s["dve_mla"], AT)
            step(dve.reciprocal(rstd[:, 0:18], rstd[:, 0:18]))
            for i in range(TT):
                norms.mark(dve.tensor_scalar(mla_tok[:, i, 0:256], mla_tok[:, i, 0:256], rstd[:, i:i + 1], None, ALU.mult))
            for i in range(AT):
                norms.mark(dve.tensor_scalar(mla_tok[:, i, 256:384], mla_tok[:, i, 256:384], rstd[:, 8 + i:9 + i], None,
                                             ALU.mult))
            for i in range(TT):
                dve.wait_ge(s["pe_uq"], i + 1)
                dve.tensor_copy(q_tok[:, i, :, :], bank(i % 4, 0, 384)).then_inc(s["dve_uq"], 1)
            dve.wait_ge(s["dve_uq"], TT)
            kr = mla_tok[:, 0:TT, KR:416].rearrange("p t (h f) -> p t h f", h=1)
            for x4, heads in ((q_tok[:, :, :, NOPE:QK], HEADS), (kr, 1)):
                cos, sin = (rope_t[:, n, :, :].rearrange("p t (h f) -> p t h f", h=1).to_broadcast([P, TT, heads, 16])
                            for n in range(2))
                even, odd = x4[:, :, :, 0::2], x4[:, :, :, 1::2]
                r = [t[:, :, 0:heads, :] for t in rot]
                step.mark(dve.tensor_tensor(r[0], even, cos, ALU.mult))
                step.mark(dve.tensor_tensor(r[1], odd, sin, ALU.mult))
                step.mark(dve.tensor_tensor(r[2], even, sin, ALU.mult))
                step(dve.tensor_tensor(r[3], odd, cos, ALU.mult))
                step.mark(dve.tensor_tensor(even, r[0], r[1], ALU.subtract))
                step(dve.tensor_tensor(odd, r[2], r[3], ALU.add))
            for h in range(HEADS):
                dve.tensor_copy(k_tok[:, :, h, NOPE:QK], mla_tok[:, :, KR:416]).then_inc(s["dve_rope"], 1)
            for g in range(8):
                if g == 0:
                    dve.wait_ge(s["dve_rope"], HEADS)
                dve.wait_ge(s["pe_qT"], g + 1)
                dve.tensor_copy(qT[:, g // 2, (g % 2) * 512:(g % 2) * 512 + 512], psum[0:QK, (g % 4) * 512:(g % 4) * 512 + 512])\
                   .then_inc(s["dve_qT"], 1)
            dve.wait_ge(s["act_kT"], 12)
            with dve.Fori(0, HEADS) as h:
                step.enter(h, 2 * TT)

                def row_max(q):
                    dve.wait_ge(s["pe_qk"], h * TT + q + 1)
                    step(dve.tensor_reduce(neg_max[:, q:q + 1], psum[:, (q % 2) * 1536:(q % 2) * 1536 + KEYS], AX.X, ALU.max))
                    dve.tensor_scalar(neg_max[:, q:q + 1], neg_max[:, q:q + 1], -MLA_SCALE, None, ALU.mult)\
                       .then_inc(s["dve_mx"], 1)

                def output(q):
                    dve.wait_ge(s["pe_pv"], h * TT + q + 1)
                    step(dve.reciprocal(row_inv[:, q:q + 1], row_sum[:, q:q + 1]))
                    dve.tensor_scalar(oa_tok[:, q, bass.ds(h * VD, VD)], bank(7, 0, VD),
                                      row_inv[:, q:q + 1], None, ALU.mult).then_inc(s["dve_o"], 1)

                row_max(0)
                for q in range(TT):
                    if q >= 1:
                        output(q - 1)
                    dve.wait_ge(s["pe_pv"], h * TT + q)
                    dve.wait_ge(s["pe_t"], h * 3 * TT + 3 * q + 1)
                    dve.tensor_copy(probT[:, 0:4, :], bank(6)).then_inc(s["dve_pt"], 1)
                    if q + 1 < TT:
                        row_max(q + 1)
                    dve.wait_ge(s["pe_t"], h * 3 * TT + 3 * q + 3)
                    dve.tensor_copy(probT[:, 8:10, :], bank(6, 0, 256)).then_inc(s["dve_pt"], 1)
                output(TT - 1)
            step.leave(HEADS, 2 * TT)
            ada_column(3)
            for g in range(10):
                dve.wait_ge(s["pe_nqk"], g + 1)
                dst, lo, w = na_group(g)
                dve.tensor_copy(dst[0:64, (g % 2) * 2 + 1, lo:lo + w], psum[64:128, (g % 4) * 512:(g % 4) * 512 + w])\
                   .then_inc(s["dve_nqk"], 1)
            for b in range(8):
                dve.wait_ge(s["pe_bb"], b + 1)
                dve.tensor_copy(
                    rel_bias.rearrange("p h (r k) -> p (h r) k", k=64)[:, :, 8 * b:8 * b + 8],
                    bank(b, 0, 448).rearrange("p (k r) -> p r k", k=8)).then_inc(s["dve_bb"], 1)
            dve.wait_ge(s["dve_bb"], 8)
            with dve.Fori(0, HEADS) as h:
                step.enter(h, 1 + 4 * TT)
                mask = row_mask.rearrange("p a b -> p (a b)").rearrange("p (a w) -> p a w", a=1)
                step(dve.tensor_tensor(inner_bias.rearrange("p (a w) -> p a w", a=1), rel_bias[:, bass.ds(h, 1), 128:768],
                                       mask, ALU.add))

                def row_max(q):
                    first, n, col = NA_TILES[q]
                    dve.wait_ge(s["pe_nqk2"], h * TT + q + 1)
                    dve.wait_ge(s["pe_nt"], h * 2 * TT + 2 * max(q - 1, 0))
                    local = nprob[:, q % 2, 0:n].rearrange("p (a w) -> p a w", a=1)
                    scores = psum[:, (q % 2) * 1024:(q % 2) * 1024 + n + C]
                    bias = inner_bias.rearrange("p (a w) -> p a w", a=1) if col is None else \
                        rel_bias[:, bass.ds(h, 1), col:col + n]
                    step.mark(dve.scalar_tensor_tensor(out=local, in0=scores[:, 0:n].rearrange("p (a w) -> p a w", a=1),
                                                       scalar=NA_SCALE, in1=bias, op0=ALU.mult, op1=ALU.add))
                    step(dve.tensor_scalar(nprob[:, q % 2, n:n + C], scores[:, n:n + C], NA_SCALE, None, ALU.mult))
                    step(dve.tensor_reduce(neg_max[:, q:q + 1], nprob[:, q % 2, 0:n + C], AX.X, ALU.max))
                    dve.tensor_scalar(neg_max[:, q:q + 1], neg_max[:, q:q + 1], -1.0, None, ALU.mult)\
                       .then_inc(s["dve_nmx"], 1)

                def output(q):
                    dve.wait_ge(s["pe_npv"], h * TT + q + 1)
                    step(dve.reciprocal(row_inv[:, q:q + 1], row_sum[:, q:q + 1]))
                    dve.tensor_scalar(od_tok[:, q, bass.ds(h * VD, VD)], bank(6 + q % 2, 0, VD),
                                      row_inv[:, q:q + 1], None, ALU.mult).then_inc(s["dve_no"], 1)

                row_max(0)
                for q in range(TT):
                    if q + 1 < TT:
                        row_max(q + 1)
                    if q >= 1:
                        output(q - 1)
                output(TT - 1)
            step.leave(HEADS, 1 + 4 * TT)
            dve.wait_ge(s["dve_ada2"], 4)
            dve.scalar_tensor_tensor(out=scale2, in0=scale2, scalar=1.0, in1=vec[:, V_N2:V_N2 + 8], op0=ALU.add,
                                     op1=ALU.mult).then_inc(s["dve_ada2"], 2)
            dve.wait_ge(s["pe_odT"], 4)
            dve.tensor_copy(cond_rows, cond[:, :, 0:1].to_broadcast([P, KT, P])).then_inc(s["dve_cond"], 1)
            dve.wait_ge(s["in_res"], 32)
            for n in range(4):
                dve.wait_ge(s["pe_res"], n + 1)
                dst = (res_gate1, res_gate2)[n // 2][:, (n % 2) * 512:(n % 2) * 512 + 512]
                dve.tensor_tensor(dst, dst, bank(4 + n), ALU.add).then_inc(s["dve_res"], 1)
            with dve.Fori(0, KT // 2) as i:
                step.enter(i, 12)
                for m in range(16):
                    n, half = (m // 2) % 4, m % 2
                    dst = merged[:, bass.ds(i * 2 + m // 8, 1), half * 512:half * 512 + 512]
                    g, p = (t.rearrange("p (a w) -> p a w", a=1) for t in (gate_sb[:, m % 2, :], bank(4 + m % 4)))
                    dve.wait_ge(s["pe_gate"], i * 16 + m + 1)
                    dve.wait_ge(s["act_gate"], i * 16 + m + 1)
                    if n == 0:
                        dve.tensor_tensor(dst, g, p, ALU.mult).then_inc(s["dve_gate"], 1)
                    else:
                        add = gated.rearrange("p (a w) -> p a w", a=1)
                        dve.wait_ge(s["dve_gate"], i * 16 + m)
                        step(dve.tensor_tensor(add, g, p, ALU.mult))
                        dve.tensor_tensor(dst, dst, add, ALU.add).then_inc(s["dve_gate"], 1)
            step.leave(KT // 2, 12)
            dve.wait_ge(s["in_x1"], 16)
            for m in range(16):
                half, i = m // TT, m % TT
                lo = half * 512
                dve.wait_ge(s["pe_out"], m + 1)
                dve.wait_ge(s["dve_x1"], m)
                step(dve.tensor_tensor(gated, bank(m % 8), res_gate1[:, lo:lo + 512], ALU.mult))
                dve.tensor_tensor(x1[:, i, lo:lo + 512], x1[:, i, lo:lo + 512], gated, ALU.add).then_inc(s["dve_x1"], 1)
            for g in range(2):
                dve.wait_ge(s["act_ssq2"], 4 * g + 4)
                dve.tensor_scalar(ssq[:, 4 * g:4 * g + 4], ssq[:, 4 * g:4 * g + 4], 1.0 / D, EPS, ALU.mult, ALU.add)\
                   .then_inc(s["dve_ms2"], 1)
                dve.wait_ge(s["act_rt2"], g + 1)
                step(dve.reciprocal(rstd[:, 4 * g:4 * g + 4], rstd[:, 4 * g:4 * g + 4]))
                for i in range(4 * g, 4 * g + 4):
                    dve.tensor_scalar(x1n[:, i, :], x1[:, i, :], rstd[:, i:i + 1], None, ALU.mult)\
                       .then_inc(s["dve_x1n"], 1)

            def column(t):
                return t.rearrange("p (t a) -> p t a", a=1)

            def first_equal(hot, values, top):
                seen = column(rc[7])
                step(dve.tensor_tensor(hot, values, column(top).to_broadcast([P, TT, 4]), ALU.is_equal))
                step(dve.tensor_copy(seen, hot[:, :, 0:1]))
                for j in range(1, 4):
                    step(dve.tensor_tensor(hot[:, :, j:j + 1], hot[:, :, j:j + 1], seen, ALU.is_gt))
                    if j < 3:
                        step(dve.tensor_tensor(seen, seen, hot[:, :, j:j + 1], ALU.max))

            dve.wait_ge(s["in_router"], 64)
            dve.wait_ge(s["pe_route"], 1)
            step(dve.tensor_tensor(logits, bank(4, 0, 160).rearrange("p (t n) -> p t n", n=20),
                                   wr_bias.rearrange("p (a n) -> p a n", a=1).to_broadcast([P, TT, 20]), ALU.add))
            group_logit = logits[:, :, 0:4]
            step(dve.tensor_reduce(rc[0], group_logit, AX.X, ALU.max))
            dve.tensor_tensor(group_exp, group_logit, column(rc[0]).to_broadcast([P, TT, 4]), ALU.subtract)\
               .then_inc(s["dve_route"], 1)
            first_equal(group_hot, group_logit, rc[0])
            picked = pick.rearrange("p t (g e) -> p t g e", g=4)
            step(dve.tensor_tensor(picked, logits[:, :, 4:20].rearrange("p t (g e) -> p t g e", g=4),
                                   group_hot.rearrange("p t (g a) -> p t g a", a=1).to_broadcast([P, TT, 4, 4]), ALU.mult))
            step(dve.tensor_reduce(expert_logit, picked.rearrange("p t g e -> p t e g"), AX.X, ALU.add))
            step(dve.tensor_reduce(rc[1], expert_logit, AX.X, ALU.max))
            first_equal(expert_hot, expert_logit, rc[1])
            step(dve.scalar_tensor_tensor(out=expert_logit, in0=expert_hot, scalar=MASK, in1=expert_logit, op0=ALU.mult,
                                          op1=ALU.add))
            step(dve.tensor_reduce(rc[2], expert_logit, AX.X, ALU.max))
            first_equal(second_hot, expert_logit, rc[2])
            dve.tensor_tensor(rc[3], rc[2], rc[1], ALU.subtract).then_inc(s["dve_route"], 1)
            dve.wait_ge(s["act_route"], 2)
            step(dve.tensor_reduce(rc[4], group_exp, AX.X, ALU.add))
            step(dve.tensor_scalar(rc[5], rc[3], 1.0, None, ALU.add))
            step(dve.tensor_tensor(rc[5], rc[5], rc[4], ALU.mult))
            step(dve.reciprocal(rc[5], rc[5]))
            step(dve.tensor_tensor(rc[6], rc[5], rc[3], ALU.mult))
            step(dve.tensor_tensor(expert_hot, expert_hot, column(rc[5]).to_broadcast([P, TT, 4]), ALU.mult))
            step(dve.tensor_tensor(second_hot, second_hot, column(rc[6]).to_broadcast([P, TT, 4]), ALU.mult))
            step(dve.tensor_tensor(expert_hot, expert_hot, second_hot, ALU.add))
            step(dve.tensor_tensor(route.rearrange("p t (g e) -> p t g e", g=4),
                                   group_hot.rearrange("p t (g a) -> p t g a", a=1).to_broadcast([P, TT, 4, 4]),
                                   expert_hot.rearrange("p t (a e) -> p t a e", a=1).to_broadcast([P, TT, 4, 4]), ALU.mult))
            dve.wait_ge(s["pe_hT2"], 2 * KT)
            step(dve.memset(moe, 0.0))
            with dve.Fori(0, EXPERTS // 2) as i:
                for m in range(2):
                    for c4 in range(4):
                        f, half = c4 // 2, c4 % 2
                        n = 4 * m + c4
                        if c4 == 0:
                            dve.wait_ge(s["pe_down"], i * 32 + 16 * m)
                        dve.wait_ge(s["act_silu"], i * 8 + n + 1)
                        dve.wait_ge(s["pe_au"], i * 8 + n + 1)
                        dve.tensor_tensor(actT[:, f, half * 512:half * 512 + 512], silu[:, n % 2, :], bank(2 * (n % 2) + 1),
                                          ALU.mult).then_inc(s["dve_act"], 1)
                    for c16 in range(16):
                        t, half = c16 // 2, c16 % 2
                        n = 16 * m + c16
                        dst = moe[:, t, half * 512:half * 512 + 512]
                        dve.wait_ge(s["dve_moe"], i * 32 + 16 * m)
                        dve.wait_ge(s["pe_down"], i * 32 + n + 1)
                        dve.scalar_tensor_tensor(out=dst, in0=bank(4 + c16 % 4), scalar=route[:, t, bass.ds(i * 2 + m, 1)], in1=dst,
                                                 op0=ALU.mult, op1=ALU.add).then_inc(s["dve_moe"], 1)
            dve.wait_ge(s["dve_moe"], 16 * EXPERTS)
            for i in range(TT):
                step(dve.tensor_tensor(moe[:, i, :], moe[:, i, :], res_gate2, ALU.mult))
                dve.tensor_tensor(x1[:, i, :], x1[:, i, :], moe[:, i, :], ALU.add).then_inc(s["dve_moe"], 1)
            dve.wait_ge(s["in_final"], 16)
            for i in range(TT):
                dve.wait_ge(s["act_fin"], i + 1)
                dve.tensor_scalar(ssq[:, i:i + 1], ssq[:, i:i + 1], 1.0 / D, EPS, ALU.mult, ALU.add).then_inc(s["dve_fms"], 1)
                dve.wait_ge(s["act_frt"], i + 1)
                step(dve.reciprocal(rstd[:, i:i + 1], rstd[:, i:i + 1]))
                dve.scalar_tensor_tensor(out=x1[:, i, :], in0=x1[:, i, :], scalar=rstd[:, i:i + 1], in1=final_gain,
                                         op0=ALU.mult, op1=ALU.mult).then_inc(s["dve_fin"], 1)

        @block.tensor
        def _(pe):
            def mm(dst, lhsT, rhs, first, last):
                return pe.matmul(dst, lhsT, rhs, start=first, stop=last)

            pe.wait_ge(s["pool_const"], 3)
            pe.wait_ge(s["in_vec"], 16 * 11)
            pe.transpose(bank(7, 0, P), staged, ident[:, :]).then_inc(s["pe_vec"], 1)
            pe.wait_ge(s["in_feat"], 48)
            for layer in range(2):
                for half in range(2):
                    lo = half * 512
                    dst = psum[0:64, layer * 1024 + lo:layer * 1024 + lo + 512]
                    if layer == 1:
                        pe.wait_ge(s["act_sin"], 1)
                    mm(dst, w1_sb if layer == 0 else w2_sb, (feat if layer == 0 else hid)[:, lo:lo + 512], True, True)\
                        .then_inc(s["pe_sin"], 1)
            pe.wait_ge(s["act_sin"], 2)
            pe.wait_ge(s["in_w3"], 16)
            pe.wait_ge(s["dve_vec"], 1)
            for i in range(TT):
                if i >= 2:
                    pe.wait_ge(s["dve_filt"], i - 1)
                b = 4 + 2 * (i % 2)
                mm(bank(b), hid[:, i * P:i * P + P], w3_sb[:, 0:512], True, True)
                mm(bank(b + 1), hid[:, i * P:i * P + P], w3_sb[:, 512:1024], True, True).then_inc(s["pe_filt"], 1)
            pe.wait_ge(s["dve_filt"], TT)
            for g in range(16):
                j, part = g // 2, g % 2
                n = K_SPEC[j // 2]
                if g % 4 == 0:
                    arrived(pe, n)
                if g >= 4:
                    pe.wait_ge(s["act_spec"], g - 3)
                table = slot(n, 2, TT, 2, P)
                for i in range(TT):
                    last = mm(bank(g % 4), table[:, j % 2, i, part, :], (fsum, fdif)[part][:, i, :], i == 0, i == TT - 1)
                last.then_inc(s["pe_spec"], 1)
            pe.wait_ge(s["pool_sq"], 4 * TT - 1)
            for n in range(4):
                last = mm(bank(4, n, n + 1), sq_acc[:, n * P:n * P + P], ones[:, 0:1], True, True)
            last.then_inc(s["pe_fnorm"], 1)
            pe.wait_ge(s["act_cond"], 1)
            for n in range(4):
                arrived(pe, K_ADA1[n])
                w = slot(K_ADA1[n], KT, 512)
                for m in range(4):
                    cb = 2 * (4 * n + m)
                    for t in range(KT):
                        last = mm(bank(5, cb, cb + 2), w[:, t, m * P:m * P + P], cond[:, t, :], t == 0, t == KT - 1)
                last.then_inc(s["pe_ada"], 1)
            pe.wait_ge(s["dve_xn"], AT)
            pe.wait_ge(s["act_spec"], 16)
            for n in range(3 * KT):
                kt, g = n // 3, n % 3
                if n >= 4:
                    pe.wait_ge(s["act_hT"], n - 3)
                for i in range(4 if g < 2 else CT):
                    src = x_sb[:, 4 * g + i, :] if g < 2 else x_ctx[:, i, :]
                    last = pe.transpose(bank(n % 4, i * P, i * P + P), src[:, kt * P:kt * P + P], ident[:, :])
                last.then_inc(s["pe_xT"], 1)
            pe.wait_ge(s["act_hT"], 3 * KT)
            pe.wait_ge(s["dve_mod"], 1)
            for g in range(12):
                ct, half = g // 2, g % 2
                n = K_HY[ct // 4]
                arrived(pe, n)
                if g >= 4:
                    pe.wait_ge(s["act_hy"], g - 3)
                w = slot(n, KT, 512 if ct < 4 else 256)
                for k in range(KT):
                    last = mm(bank(4 + g % 4), w[:, k, (ct % 4) * P:(ct % 4) * P + P],
                              hT[:, k, half * 512:half * 512 + 512], k == 0, k == KT - 1)
                last.then_inc(s["pe_hy"], 1)
            pe.wait_ge(s["act_hy"], 12)

            def ada_column(n):
                arrived(pe, K_ADA2[n])
                w = slot(K_ADA2[n], KT, 512)
                for m in range(4):
                    for t in range(KT):
                        last = mm(bank((4, 4, 7, 7)[n], 2 * m, 2 * m + 2), w[:, t, m * P:m * P + P], cond[:, t, :],
                                  t == 0, t == KT - 1)
                last.then_inc(s["pe_ada2"], 1)

            for order in range(2):
                pe.wait_ge(s["dve_fold"], 4 * order + 4)
                if order == 1:
                    pe.wait_ge(s["act_inv"], 4)
                for tt in range(4):
                    for n in range(2):
                        for ct in range(2):
                            last = pe.transpose(bank(tt, (2 * n + ct) * P, (2 * n + ct + 1) * P),
                                                folded[:, n, ct, tt * P:tt * P + P], ident[:, :])
                    last.then_inc(s["pe_fold"], 1)
                pe.wait_ge(s["act_fold"], 4 * order + 4)
                for j in range(KT):
                    n = K_CONV[order][0][j // 4]
                    arrived(pe, n)
                    table = slot(n, 4, 4, 2, P)
                    if 8 * order + j >= 4:
                        pe.wait_ge(s["dve_spec"], 8 * order + j - 3)
                    if order == 1 and j == 0:
                        pe.wait_ge(s["dve_ada2"], 1)
                    for m in range(2):
                        src = m if j < 4 else 1 - m
                        for tt in range(4):
                            last = mm(bank(4 + j % 4, m * BW, m * BW + BW), table[:, j % 4, tt, m, :],
                                      folded_t[:, tt, src, :], tt == 0, tt == 3)
                    last.then_inc(s["pe_fwd"], 1)
                for j in range(KT):
                    n = K_CONV[order][1][j // 4]
                    arrived(pe, n)
                    table = slot(n, 4, 2, 512)
                    pe.wait_ge(s["dve_spec"], 8 * order + j + 1)
                    for ct in range(2):
                        for m in range(2):
                            ab = m if j < 4 else 1 - m
                            last = mm(bank(2 * ct + ab), conv_spec[:, j, m, ct * P:ct * P + P], table[:, j % 4, m, :],
                                      j == 0, j == KT - 1)
                    if j % 4 == 3:
                        last.then_inc(s["pe_inv"], 1)
                ada_column(order)
            pe.wait_ge(s["act_inv"], 8)
            pe.wait_ge(s["dve_ada2"], 2)
            arrived(pe, K_FN)
            w = slot(K_FN, KT, BW)
            for g in range(4):
                for k in range(KT):
                    last = mm(bank(g), w[:, k, (g // 2) * P:(g // 2) * P + P],
                              hT[:, k, (g % 2) * 512:(g % 2) * 512 + 512], k == 0, k == KT - 1)
                last.then_inc(s["pe_fn"], 1)
            pe.wait_ge(s["act_fn"], 4)
            pe.wait_ge(s["in_pack"], 16)
            for i in range(TT):
                if i >= 4:
                    pe.wait_ge(s["act_chan"], i - 3)
                for ct in range(2):
                    last = mm(bank(4 + i % 4, ct * 256, ct * 256 + 256), fnT[:, ct, i * P:i * P + P], chan_basis,
                              True, True)
                last.then_inc(s["pe_chan"], 1)
            pe.wait_ge(s["act_chan"], TT)
            for part in range(2):
                arrived(pe, K_TOK[part])
                table = slot(K_TOK[part], TT, 512)
                for ct in range(2):
                    for i in range(TT):
                        last = mm(bank(4 * part + ct), chan_mixed[:, i, ct, part, :], table[:, i, :], i == 0, i == TT - 1)
                    if part == 0:
                        for i in range(TT):
                            last = mm(bank(2, ct, ct + 1), chan_mixed[:, i, ct, 0, :], alternate, i == 0, i == TT - 1)
                last.then_inc(s["pe_tok"], 1)
            ada_column(2)
            arrived(pe, K_MLA)
            pe.wait_ge(s["dve_oc"], 2)
            w = slot(K_MLA, KT, 416)
            for i in range(AT):
                if i >= 4:
                    pe.wait_ge(s["dve_mla"], i - 3)
                lo = 0 if i < TT else 256
                for k in range(KT):
                    last = mm(bank(i % 4, lo, 416), hT[:, k, i * P:i * P + P], w[:, k, lo:416], k == 0, k == KT - 1)
                last.then_inc(s["pe_mla"], 1)
            pe.wait_ge(s["dve_mn"], 2 + TT + AT)
            for g in range(7):
                src = mla_tok[:, :, (g // 2) * P:(g // 2) * P + P] if g < 4 else mla_tok[:, :, 256:384]
                t0 = 4 * (g % 2 if g < 4 else g - 4)
                for i in range(4 if g < 6 else CT):
                    last = pe.transpose(bank(g, i * P, i * P + P), src[:, t0 + i, :], ident[:, :])
                last.then_inc(s["pe_mT"], 1)
            pe.wait_ge(s["act_mT"], 7)
            pe.wait_ge(s["in_uq"], 32)
            pe.wait_ge(s["dve_ada2"], 3)
            for i in range(AT):
                if i < TT:
                    if i >= 4:
                        pe.wait_ge(s["dve_uq"], i - 3)
                    for k in range(2):
                        last = mm(bank(i % 4, 0, 384), cqT[:, k, i * P:i * P + P], w_uq[:, k, :], k == 0, k == 1)
                    last.then_inc(s["pe_uq"], 1)
                if i >= 4:
                    pe.wait_ge(s["act_ukv"], 2 * (i - 3))
                mm(bank(4 + i % 4), ckvT[:, i * P:i * P + P], w_ukv, True, True).then_inc(s["pe_ukv"], 1)
            pe.wait_ge(s["dve_rope"], HEADS)
            for g in range(8):
                if g >= 4:
                    pe.wait_ge(s["dve_qT"], g - 3)
                for i in range(4):
                    last = pe.transpose(psum[0:QK, (g % 4) * 512 + i * P:(g % 4) * 512 + i * P + P],
                                        q_tok[:, 4 * (g % 2) + i, g // 2, :], ident[:, :])
                last.then_inc(s["pe_qT"], 1)
            pe.wait_ge(s["act_ukv"], 2 * AT)
            for g in range(12):
                if g >= 4:
                    pe.wait_ge(s["act_kT"], g - 3)
                for i in range(4 if g % 3 < 2 else CT):
                    last = pe.transpose(psum[0:QK, (4 + g % 4) * 512 + i * P:(4 + g % 4) * 512 + i * P + P],
                                        k_tok[:, 4 * (g % 3) + i, g // 3, :], ident[:, :])
                last.then_inc(s["pe_kT"], 1)
            pe.wait_ge(s["act_kT"], 12)
            pe.wait_ge(s["dve_qT"], 8)
            with pe.Fori(0, HEADS) as h:
                def scores(q):
                    pe.wait_ge(s["pool_q"], h * TT + q + 1)
                    if q >= 2:
                        pe.wait_ge(s["act_p"], h * TT + q - 1)
                    base = (q % 2) * 1536
                    for lo, hi in ((0, 512), (512, 1024), (1024, 1280)):
                        last = mm(psum[:, base + lo:base + hi], q_now[:, q % 2, :], kT[:, bass.ds(h, 1), lo:hi], True, True)
                    last.then_inc(s["pe_qk"], 1)

                def values(q):
                    pe.wait_ge(s["dve_pt"], h * 2 * TT + 2 * q + 2)
                    pe.wait_ge(s["act_pt"], h * TT + q + 1)
                    for i in range(AT):
                        last = mm(bank(7, 0, VD), probT[:, i, :],
                                  v_tok[:, i, bass.ds(h * VD, VD)], i == 0, i == AT - 1)
                    last.then_inc(s["pe_pv"], 1)

                scores(0)
                for q in range(TT):
                    if q + 1 < TT:
                        scores(q + 1)
                    if q >= 1:
                        values(q - 1)
                    pe.wait_ge(s["act_p"], h * TT + q + 1)
                    for r in range(3):
                        if r == 0:
                            pe.wait_ge(s["dve_pt"], h * 2 * TT + 2 * q)
                        elif r == 1:
                            pe.wait_ge(s["dve_o"], h * TT + q)
                        else:
                            pe.wait_ge(s["dve_pt"], h * 2 * TT + 2 * q + 1)
                        for i in range(4 * r, min(4 * r + 4, AT)):
                            last = pe.transpose(bank(6 + r % 2, (i % 4) * P, (i % 4) * P + P),
                                                prob[:, q % 2, i * P:i * P + P], ident[:, :])
                        last.then_inc(s["pe_t"], 1)
                values(TT - 1)
            pe.wait_ge(s["dve_o"], HEADS * TT)
            for g in range(4):
                for i in range(4):
                    last = pe.transpose(bank(g, i * P, i * P + P), oa_tok[:, 4 * (g % 2) + i, (g // 2) * P:(g // 2) * P + P],
                                        ident[:, :])
                last.then_inc(s["pe_oaT"], 1)
            ada_column(3)
            pe.wait_ge(s["act_oaT"], 4)
            pe.wait_ge(s["dve_ada2"], 4)
            arrived(pe, K_NQK)
            w = slot(K_NQK, KT, 512)
            for g in range(10):
                if g >= 4:
                    pe.wait_ge(s["act_nqk"], g - 3)
                    pe.wait_ge(s["dve_nqk"], g - 3)
                _, lo, n = na_group(g)
                col = (g % 2) * P + (0 if g < 4 else BW)
                for k in range(KT):
                    last = mm(bank(g % 4, 0, n), w[:, k, col:col + P], hT[:, k, lo:lo + n], k == 0, k == KT - 1)
                last.then_inc(s["pe_nqk"], 1)
            arrived(pe, K_NV)
            w = slot(K_NV, KT, BW)
            for i in range(AT):
                if i >= 4:
                    pe.wait_ge(s["act_nv"], i - 3)
                for k in range(KT):
                    last = mm(bank(4 + i % 4, 0, BW), hT[:, k, i * P:i * P + P], w[:, k, :], k == 0, k == KT - 1)
                last.then_inc(s["pe_nv"], 1)
            pe.wait_ge(s["in_rpb"], 16 * 8)
            pe.wait_ge(s["act_nqk"], 10)
            pe.wait_ge(s["dve_nqk"], 10)
            pe.wait_ge(s["act_nv"], AT)
            for kc in range(64):
                if kc % 32 == 0:
                    arrived(pe, K_REL[kc // 32])
                table = slot(K_REL[kc // 32], 32, P, rows=64)
                last = mm(bank(kc // 8, (kc % 8) * 56, (kc % 8) * 56 + 56), table[:, kc % 32, :],
                          rpb_t.rearrange("p h r -> p (h r)"), True, True)
                if kc % 8 == 7:
                    last.then_inc(s["pe_bb"], 1)
            pe.wait_ge(s["dve_bb"], 8)
            pe.wait_ge(s["pool_npad"], 2)
            with pe.Fori(0, HEADS) as h:
                def scores(q):
                    first, n, _ = NA_TILES[q]
                    pe.wait_ge(s["pool_nq"], h * TT + q + 1)
                    if q >= 2:
                        pe.wait_ge(s["dve_nmx"], h * TT + q - 1)
                    base = (q % 2) * 1024
                    for lo, hi, key in [(0, 512, first * P)] + ([(512, 640, first * P + 512)] if n == 640 else []) + \
                            [(n, n + C, T)]:
                        last = mm(psum[:, base + lo:base + hi], nq_now[:, q % 2, :],
                                  nkT[:, bass.ds(h, 1), key:key + hi - lo], True, True)
                    last.then_inc(s["pe_nqk2"], 1)

                def values(q):
                    first, n, _ = NA_TILES[q]
                    pe.wait_ge(s["act_npt"], h * 2 * TT + 2 * q + 2)
                    pe.wait_ge(s["dve_no"], h * TT + max(q - 1, 0))
                    tiles = [first + i for i in range(n // P)] + [TT, TT + 1]
                    for i, t in enumerate(tiles):
                        last = mm(bank(6 + q % 2, 0, VD), nprobT[:, i, :],
                                  nv_tok[:, t, bass.ds(h * VD, VD)], i == 0, i == len(tiles) - 1)
                    last.then_inc(s["pe_npv"], 1)

                scores(0)
                for q in range(TT):
                    if q + 1 < TT:
                        scores(q + 1)
                    if q >= 1:
                        values(q - 1)
                    n = (NA_TILES[q][1] + C) // P
                    pe.wait_ge(s["act_np"], h * TT + q + 1)
                    pe.wait_ge(s["act_npt"], h * 2 * TT + 2 * q)
                    for r in range(2):
                        for i in range(4 * r, min(4 * r + 4, n)):
                            last = pe.transpose(bank(4 + r, (i % 4) * P, (i % 4) * P + P),
                                                nprob[:, q % 2, i * P:i * P + P], ident[:, :])
                        last.then_inc(s["pe_nt"], 1)
                values(TT - 1)
            pe.wait_ge(s["dve_no"], HEADS * TT)
            for g in range(4):
                for i in range(4):
                    last = pe.transpose(bank(g, i * P, i * P + P), od_tok[:, 4 * (g % 2) + i, (g // 2) * P:(g // 2) * P + P],
                                        ident[:, :])
                last.then_inc(s["pe_odT"], 1)
            pe.wait_ge(s["dve_cond"], 1)
            for n in range(4):
                arrived(pe, K_RES[n])
                w = slot(K_RES[n], KT, 512)
                for t in range(KT):
                    last = mm(bank(4 + n), cond_rows[:, t, :], w[:, t, :], t == 0, t == KT - 1)
                last.then_inc(s["pe_res"], 1)
            pe.wait_ge(s["dve_res"], 4)
            pe.wait_ge(s["act_odT"], 4)
            with pe.Fori(0, KT // 2) as i:
                for m in range(16):
                    slot_n, n, half = m // 8, (m // 2) % 4, m % 2
                    if m % 8 == 0:
                        pe.wait_ge(in_gate[slot_n], i * 80 + 80)
                    for name in ("act_gate", "dve_gate"):
                        if m >= 4:
                            pe.wait_ge(s[name], i * 16 + m - 3)
                        else:
                            pe.wait_ge(s[name], i * 16)
                    for k in range(KT):
                        last = mm(bank(m % 4), gate_slots[slot_n][:, k, n, :], hT[:, k, half * 512:half * 512 + 512],
                                  k == 0, k == KT - 1)
                    last.then_inc(s["pe_gg"], 1)
                    for k in range(2):
                        last = mm(bank(4 + m % 4), wb[:, slot_n, 2 * n + k, :], oT[n][:, k, half * 512:half * 512 + 512],
                                  k == 0, k == 1)
                    last.then_inc(s["pe_gate"], 1)
            pe.wait_ge(s["dve_gate"], 64)
            for m in range(16):
                half, t = m // TT, m % TT
                if t == 0:
                    pe.wait_ge(s["in_w_out"], 16 * half + 16)
                if m >= 8:
                    pe.wait_ge(s["dve_x1"], m - 7)
                for k in range(KT):
                    last = mm(bank(m % 8), merged[:, k, t * P:t * P + P], w_out_slots[half][:, k, :], k == 0, k == KT - 1)
                last.then_inc(s["pe_out"], 1)
            pe.wait_ge(s["dve_x1"], 16)
            for n in range(2 * KT):
                g, kt = n // KT, n % KT
                pe.wait_ge(s["dve_x1n"], 4 * g + 4)
                if n >= 4:
                    pe.wait_ge(s["act_hT2"], n - 3)
                for i in range(4):
                    last = pe.transpose(bank(n % 4, i * P, i * P + P), x1n[:, 4 * g + i, kt * P:kt * P + P], ident[:, :])
                last.then_inc(s["pe_hT2"], 1)
            pe.wait_ge(s["act_hT2"], 2 * KT)
            pe.wait_ge(s["in_router"], 64)
            for t in range(TT):
                for k in range(KT):
                    last = mm(bank(4, 20 * t, 20 * t + 20), h2T[:, k, t * P:t * P + P], wr[:, k, :], k == 0, k == KT - 1)
            last.then_inc(s["pe_route"], 1)
            pe.wait_ge(s["dve_route"], 1)
            with pe.Fori(0, EXPERTS // 2) as i:
                for m in range(2):
                    pe.wait_ge(in_expert[m], i * 48 + 48)
                    for c4 in range(4):
                        f, half = c4 // 2, c4 % 2
                        n = 4 * m + c4
                        pe.wait_ge(s["dve_act"], i * 8 + max(n - 1, 0))
                        for u in range(2):
                            for k in range(KT):
                                last = mm(bank(2 * (n % 2) + u), expert_slots[m][:, u, k, f * P:f * P + P],
                                          h2T[:, k, half * 512:half * 512 + 512], k == 0, k == KT - 1)
                        last.then_inc(s["pe_au"], 1)
                    for c16 in range(16):
                        t, half = c16 // 2, c16 % 2
                        n = 16 * m + c16
                        if c16 == 0:
                            pe.wait_ge(s["dve_act"], i * 8 + 4 * m + 4)
                        pe.wait_ge(s["dve_moe"], i * 32 + max(n - 3, 0))
                        for f in range(2):
                            last = mm(bank(4 + c16 % 4), actT[:, f, t * P:t * P + P], w_down[:, m, f, half * 512:half * 512 + 512],
                                      f == 0, f == 1)
                        last.then_inc(s["pe_down"], 1)


def _tables():
    import numpy as np
    P, T, pi = 128, 1024, np.pi
    f32 = np.float32
    tb = {}
    t = np.linspace(0.0, 1.0, T, dtype=f32)
    bands = np.linspace(1e-4, 15, 16, dtype=f32)
    ang = (f32(2.0 * pi / T) * np.arange(T, dtype=f32)[:, None] * bands).astype(f32)
    tb["features"] = np.concatenate([t[:, None], np.cos(ang), -np.sin(ang)], axis=1).T
    dl = np.linspace(np.log(1e-2) / 1.5, np.log(1e-2) / 0.3, 256)
    win = np.exp(-np.linspace(0, 1, T)[:, None] * np.abs(dl))
    back = win.copy()
    back[0] = 0.0
    tb["window"] = np.stack([win, back], 1).reshape(8, P, 2, 256).transpose(1, 0, 2, 3)
    k = np.concatenate([np.arange(0, T, 2), np.arange(1, T, 2)])
    a = pi * (((2 * k[None, :] + 1) * np.arange(T)[:, None]) % (4 * T)) / (2 * T)
    g = np.stack([np.cos(a), -np.sin(a)], 1)
    tb["filter_basis"] = g.reshape(8, P, 2, 8, P).transpose(1, 3, 0, 2, 4)
    th = pi * (((2 * k[None, :] + 1) * (2 * np.arange(512)[:, None] + 1)) % (8 * T)) / (4 * T)
    cas = np.stack([np.cos(th) + np.sin(th), np.cos(th) - np.sin(th)], 1)
    tb["forward_basis"] = cas.reshape(4, P, 2, 8, P).transpose(1, 3, 0, 2, 4)
    tb["inverse_basis"] = (cas / (2 * T)).transpose(2, 1, 0).reshape(8, P, 2, 512).transpose(1, 0, 2, 3)
    b = 2 * pi * ((np.arange(T)[:, None] * np.arange(512)[None, :]) % T) / T
    tb["token_basis"] = np.stack([np.cos(b), -np.sin(b)], 0).reshape(2, 8, P, 512).transpose(2, 0, 1, 3)
    c = 2 * pi * ((np.arange(64)[:, None] * np.arange(64)[None, :]) % 64) / 64
    chan = np.zeros((P, 2, P))
    for n in range(2):
        chan[n * 64:n * 64 + 64, 0, n * 64:n * 64 + 64] = np.cos(c) / 256
        chan[n * 64:n * 64 + 64, 1, n * 64:n * 64 + 64] = np.sin(c) / 256
    tok = np.arange(T)
    inv = (f32(10000.0) ** (-np.arange(8, dtype=f32) / f32(8))).astype(f32)
    ra = np.concatenate([(tok // 64).astype(f32)[:, None] * inv, (tok % 64).astype(f32)[:, None] * inv], 1)
    rope = np.stack([np.cos(ra), np.sin(ra)], 1).reshape(8, P, 2, 16).transpose(1, 2, 0, 3)
    rows = np.full((P, 10, 64), -1e30)
    rows[:64, 0:8] = 0
    rows[64:, 1:9] = 0
    qc, kc = np.arange(64)[:, None], np.arange(64)[None, :]
    start = np.clip(qc - 8, 0, 48)
    ok = (kc >= start) & (kc < start + 16)
    sel = np.zeros((2, 32, 64, 2, 64))
    for r in range(2):
        for q in range(64):
            for kk in range(64):
                if ok[q, kk]:
                    sel[r, kk - q + 15, kk, r, q] = 1
                else:
                    sel[r, 31, kk, r, q] = 1
    tb["relative_columns"] = sel.reshape(64, 64 * P)
    alt = (1 - 2 * (np.arange(P) % 2))[:, None]
    tb["pack"] = np.concatenate([x.reshape(P, -1) for x in (rope, rows, chan, alt)], 1)
    return {n: np.ascontiguousarray(v, dtype=f32) for n, v in tb.items()}


_INS = ['x', 'c', 'ctx', 'c_ctx', 'ada_w', 'ada_b', 'norm1_g', 'norm2_g', 'w_in', 'mla_q_norm', 'mla_w_uq',
        'mla_kv_norm', 'mla_w_ukv', 'hy_short_w', 'hy_w1', 'hy_b1', 'hy_freq1', 'hy_w2', 'hy_b2', 'hy_freq2',
        'hy_w3', 'hy_bias', 'na_rpb', 'w_branch', 'w_out', 'moe_w_group', 'moe_b_group', 'moe_w_expert',
        'moe_b_expert', 'moe_w_gate', 'moe_w_up', 'moe_w_down', 'final_norm_g']
_OUTS = [((1, 1024, 1024), 'float32')]


def kernel(**inputs):
    import numpy as _np
    import concourse.bacc as _bacc
    from concourse import mybir as _mybir
    from concourse.bass_utils import run_bass_kernel_spmd as _run

    nc = _bacc.Bacc("TRN2", target_bir_lowering=False, num_devices=1)
    arrays, args = {}, {}
    for name, a in [(n, inputs[n]) for n in _INS] + list(_tables().items()):
        a = _np.ascontiguousarray(a)
        arrays[f"in_{name}_dram"] = a
        args[name] = nc.dram_tensor(f"in_{name}_dram", a.shape, _mybir.dt.from_np(a.dtype), kind="ExternalInput").ap()
    for i, (shape, dtype) in enumerate(_OUTS):
        dt = _mybir.dt.from_np(_np.dtype(dtype))
        args["out"] = nc.dram_tensor(f"out_{i}_dram", shape, dt, kind="ExternalOutput").ap()
    hybrid_flow_backbone(nc, **args)
    r = _run(nc, [arrays], core_ids=[0])
    return r.results[0]["out_0_dram"]
```

```python
import concourse.bass as bass
from concourse import mybir
from contextlib import ExitStack

F32 = mybir.dt.float32
I32 = mybir.dt.int32
ALU = mybir.AluOpType
ACT = mybir.ActivationFunctionType
AX = mybir.AxisListType

P = 128
D = 1024
KT = D // P
T = 1024
TT = T // P
C = 256
CT = C // P
AT = TT + CT
BW = 256
HEADS = 4
NOPE, ROPE, VD = 64, 32, 64
QK = NOPE + ROPE
KEYS = T + C
MLA_SCALE = float(QK) ** -0.5
NA_SCALE = 64.0 ** -0.5
EPS = 1e-6
MASK = -1e30
PI = 3.14159265
TURN = 6.283185307179586
ROUND = 1.5 * 2.0 ** 23
EXPERTS, HID = 16, 256
CQ, KR, HY, FN, NQ, NV, GATE, IN_END = 0, 384, 416, 1184, 1440, 1952, 2208, 6304
MAX_TILES = 32
FREE = 4
SLOT = 4096
V_ADAB, V_N1, V_N2, V_QN, V_KVN, V_TAP, V_HB, V_B1, V_F1, V_B2, V_F2, V_END = 0, 48, 56, 64, 66, 67, 85, 89, 90, 91, 92, 93


class Steps:

    def __init__(self, eng, sem):
        self.eng, self.sem, self.base, self.n = eng, sem, 0, 0

    def __call__(self, ins):
        self.mark(ins)
        self.eng.wait_ge(self.sem, self.base + self.n)

    def mark(self, ins):
        ins.then_inc(self.sem, 1)
        self.n += 1

    def sync(self):
        self.eng.wait_ge(self.sem, self.base + self.n)

    def enter(self, i, per):
        self.before = self.base + self.n
        self.base, self.n = self.before + i * per, 0

    def leave(self, rounds, per):
        assert self.n == per, (self.n, per)
        self.base, self.n = self.before + rounds * per, 0


def hybrid_flow_backbone(nc, out, x, c, ctx, c_ctx, ada_w, ada_b, norm1_g, norm2_g, w_in, mla_q_norm, mla_w_uq,
                         mla_kv_norm, mla_w_ukv, hy_short_w, hy_w1, hy_b1, hy_freq1, hy_w2, hy_b2, hy_freq2,
                         hy_w3, hy_bias, na_rpb, w_branch, w_out, moe_w_group, moe_b_group, moe_w_expert,
                         moe_b_expert, moe_w_gate, moe_w_up, moe_w_down, final_norm_g,
                         features, window, filter_basis, forward_basis, inverse_basis, token_basis,
                         relative_columns, pack, routing_tab):
    stack = ExitStack()
    with stack:
        def sb(name, shape, dt=F32):
            return stack.enter_context(nc.sbuf_tensor(name, shape, dt))

        def sem(name):
            return stack.enter_context(nc.semaphore(name))

        def cut(t, at, *shape, rows=P):
            size = 1
            for s in shape:
                size *= s
            v = t[0:rows, at:at + size]
            if len(shape) == 1:
                return v
            names = "abcde"[:len(shape)]
            return v.rearrange(f"p ({' '.join(names)}) -> p {' '.join(names)}", **dict(zip(names, shape)))

        normed = sb("normed", [P, 10240])
        branches = sb("branches", [P, 8192])
        ring = sb("ring", [P, 3 * SLOT])
        arena = sb("arena", [P, 20700])
        pk = sb("pk", [P, 1153])
        ident = sb("ident", [P, P])
        ones = sb("ones", [P, 2])
        vec = sb("vec", [P, V_END])
        small = sb("small", [P, 256])
        psum = stack.enter_context(nc.psum_tensor("psum", [P, 4096], F32))

        def bank(b, lo=0, hi=512):
            return psum[:, b * 512 + lo:b * 512 + hi]

        def slot(n, *shape, rows=P):
            return cut(ring, (n % 3) * SLOT, *shape, rows=rows)

        rope_t = cut(pk, 0, 2, TT, 16)
        row_mask = cut(pk, 256, 10, 64)
        chan_basis = cut(pk, 896, 2 * P)
        alternate = pk[:, 1152:1153]

        scale1 = cut(small, 0, 2, KT)
        shift1 = cut(small, 16, 2, KT)
        scale2 = cut(small, 32, KT)
        shift2 = cut(small, 40, KT)
        cond = cut(small, 48, KT, 2)
        cond_raw = cut(small, 64, 2, KT)
        ssq = cut(small, 80, 32)
        rstd = cut(small, 112, 32)
        filter_norm = cut(small, 144, 4)
        neg_max = cut(small, 148, 8)
        row_sum = cut(small, 156, 8)
        row_inv = cut(small, 164, 8)

        window_sb = cut(normed, 0, TT, 2, BW)
        feat = cut(normed, 4096, T, rows=33)
        arg = cut(normed, 5120, T, rows=64)
        turn = cut(normed, 6144, T, rows=64)
        hid = cut(normed, 7168, T, rows=64)
        w3_sb = cut(normed, 8192, T, rows=64)
        w1_sb = cut(normed, 9216, 64, rows=33)
        w2_sb = cut(normed, 9280, 64, rows=64)
        staged = cut(normed, 9344, P)
        spec = cut(arena, 0, 2, KT, 512)
        fsum = cut(arena, 8192, TT, 512)
        fdif = cut(arena, 12288, TT, 512)
        x_ctx = cut(arena, 16400, CT, D)
        fir_f = cut(arena, 18448, 512)
        fir_b = cut(arena, 18960, 512)
        sq_acc = cut(arena, 19472, 512)
        sq_tmp = cut(arena, 19984, 512)
        x_sb = cut(branches, 0, TT, D)
        hT = cut(normed, 0, KT, KEYS)
        conv = cut(arena, 8192, 6, T)
        raw = cut(arena, 14336, 2, T + 2)
        folded_t = cut(arena, 14336, 4, 2, BW)
        prod_r = cut(arena, 16400, 2, BW)
        prod_i = cut(arena, 16912, 2, BW)
        mix = cut(arena, 17424, T)
        conv_spec = cut(branches, 4096, KT, 2, BW)
        folded = cut(branches, 0, 2, 2, 512)
        halves = cut(branches, 0, 2, 2, 512)
        oT = [cut(branches, n * 2048, 2, T) for n in range(4)]
        fnT = cut(arena, 0, 2, T)
        chan_mixed = cut(arena, 2048, TT, 2, 2, P)
        sine_part = cut(arena, 6144, 2, 512)

        mla_tok = cut(arena, 0, AT, 416)
        cqT = cut(arena, 4160, 2, T)
        ckvT = cut(arena, 6208, KEYS)
        q_tok = cut(arena, 7488, TT, HEADS, QK)
        k_tok = cut(arena, 10560, AT, HEADS, QK)
        v_tok = cut(arena, 14400, AT, HEADS * VD)
        qT = cut(arena, 0, HEADS, T, rows=QK)
        kT = cut(arena, 4160, HEADS, KEYS, rows=QK)
        prob = cut(arena, 10560, 2, KEYS)
        probT = cut(arena, 13120, AT, P)
        w_uq = cut(arena, 16960, 2, HEADS * QK)
        w_ukv = cut(arena, 17728, HEADS * (NOPE + VD))
        q_now = cut(arena, 18240, 2, P, rows=QK)
        rot = [cut(arena, 18496 + 512 * n, TT, HEADS, 16) for n in range(4)]
        oa_tok = cut(branches, 0, TT, BW)
        nqT = cut(arena, 0, HEADS, T, rows=64)
        nkT = cut(arena, 4096, HEADS, KEYS)
        nv_tok = cut(arena, 9216, AT, BW)
        rel_bias = cut(arena, 11776, HEADS, 14 * 64)
        inner_bias = cut(arena, 15360, 640)
        nprob = cut(arena, 16000, 2, 896)
        nprobT = cut(arena, 17792, 7, P)
        nq_now = cut(arena, 18688, 2, P)
        rpb_t = cut(small, 176, HEADS, 14, rows=64)
        od_tok = cut(branches, 6144, TT, BW)
        NA_TILES = [(0, 512, 384), (0, 512, 256)] + [(q - 2, 640, None) for q in range(2, 6)] + \
                   [(4, 512, 128), (4, 512, 0)]
        merged = cut(arena, 0, KT, T)
        cond_rows = cut(arena, 0, KT, P)
        wb = cut(arena, 8192, 2, 8, P)
        gate_sb = cut(arena, 15360, 2, 512)
        gated = cut(arena, 12288, 512)
        final_gain = cut(arena, 16384, D)
        res_gate1 = cut(arena, 17408, D)
        res_gate2 = cut(arena, 18432, D)
        x1 = cut(normed, 0, TT, D)
        x1n = cut(branches, 0, TT, D)
        h2T = cut(arena, 0, KT, T)
        square2 = cut(normed, 8192, D)
        wr = cut(arena, 19456, KT, 20)
        wr_bias = cut(arena, 19616, 20)
        logits = cut(arena, 19640, TT, 20)
        route = cut(arena, 19800, TT, EXPERTS)
        pick = cut(arena, 19928, TT, 16)
        group_hot, expert_hot, second_hot, expert_logit = (cut(arena, 20056 + 32 * n, TT, 4) for n in range(4))
        rc = [cut(arena, 20184 + 8 * n, TT) for n in range(8)]
        group_exp = cut(arena, 20248, TT, 4)
        first_of, second_of, both_of, slot_of, tile_off, masked = (cut(arena, 12288 + 128 * n, TT, EXPERTS) for n in range(6))
        count, tiles, upto, base_of, one_row = (cut(arena, 13056 + 16 * n, EXPERTS) for n in range(5))
        slots_f, slot_tile, slot_row = (cut(arena, 13136 + 16 * n, 2, TT) for n in range(3))
        ended = cut(arena, 13200, 34, EXPERTS)
        ended_sum = cut(arena, 13744, 34)
        weight_t = cut(arena, 13778, 32)
        tab = cut(arena, 13810, 296)
        column_no, token_no, before = tab[:, 0:128], tab[:, 160:168], tab[:, 168:296]
        all_ones = cut(arena, 14106, P)
        pairs_f = cut(arena, 14234, 2)
        row_hot = cut(arena, 0, 2, TT, P)
        tile_hot = cut(arena, 2048, 2, TT, 2, 32)
        ints = sb("ints", [P, 96], I32)
        token_of = ints[:, 0:34]
        expert_of = ints[:, 34:68]
        pair_count = ints[0:1, 68:69]
        slots_i = ints[:, 69:85].rearrange("p (c t) -> p c t", c=2)
        token_now = ints[:, 85:87]
        w_down = cut(arena, 8192, 2, 2, D)
        slot_x = cut(branches, 0, 2, D)
        slot_y = cut(branches, 2048, 2, D)
        slot_hT = cut(branches, 4096, 2, KT, P)
        act_tok = cut(branches, 6144, 2, HID)
        actT = cut(branches, 6656, 2, HID)
        silu = cut(branches, 7168, 2, HID)
        parts = cut(arena, 3072, 2, 2, D)
        rows_dram = nc.dram_tensor("normed_rows", [T, D], F32, kind="Internal").ap()
        slots_dram = nc.dram_tensor("expert_rows", [MAX_TILES * P, D], F32, kind="Internal").ap()

        s = {n: sem(n) for n in (
            "in_small", "in_x", "pool_const", "pool_pad", "dve_chain", "act_chain", "dve_zero",
            "pe_vec", "dve_vec", "act_cond", "pe_sin", "dve_arg", "act_sin", "pe_filt", "dve_filt", "pool_sq",
            "pe_spec", "act_spec", "pe_fnorm", "pe_ada", "act_ssq", "dve_xn", "pe_xT", "act_hT",
            "pe_hy", "act_hy", "dve_conv", "dve_fold", "pe_fold", "act_fold", "pe_fwd", "dve_spec",
            "pe_inv", "act_inv", "dve_z", "pe_fn", "act_fn", "pe_chan", "act_chan", "pe_tok", "act_tok", "dve_oc",
            "in_uq", "pe_mla", "dve_mla", "act_msq", "act_mrt", "dve_mn", "pe_mT", "act_mT", "pe_uq", "dve_uq", "pe_ukv",
            "act_ukv", "dve_rope", "pe_qT", "dve_qT", "pe_kT", "act_kT", "pool_q", "pe_qk", "dve_mx", "act_p", "pe_t", "dve_pt",
            "act_pt", "pe_pv", "dve_o", "pe_oaT", "act_oaT", "pe_nqk", "act_nqk", "dve_nqk", "pe_nv", "act_nv", "in_rpb", "pool_rpb",
            "pe_bb", "dve_bb", "pool_nq", "pe_nqk2", "dve_nmx", "act_np", "pe_nt", "act_npt", "pe_npv", "dve_no", "pe_odT", "act_odT",
            "pool_npad",
            "pe_ada2", "dve_ada2", "pe_res", "dve_res", "in_res", "dve_cond", "pe_gg", "pe_gate", "act_gate", "dve_gate",
            "in_w_out", "in_x1", "pe_out", "dve_x1", "act_ssq2", "act_rt2", "dve_ms2", "dve_x1n", "pe_hT2", "act_hT2",
            "in_router", "pe_route", "act_route", "dve_route", "pe_au", "act_silu", "dve_moe", "act_fin",
            "in_tab", "pool_idx", "pool_ones", "dve_both", "pe_count", "dve_hot", "pe_table", "dve_table", "pe_x", "act_h", "dve_h",
            "dve_mul", "pe_actT", "dve_actT", "pe_down", "dve_y",
            "dve_fin", "dve_fms", "act_frt",
            "stored", "in_vec", "in_feat", "dve_mod")}
        in_gate = [sem(f"in_gate{n}") for n in range(2)]
        rows_stored = sem("rows_stored")
        in_slots = [sem(f"in_slots{n}") for n in range(2)]
        in_down = [sem(f"in_down{n}") for n in range(2)]
        y_stored = [sem(f"y_stored{n}") for n in range(2)]
        in_parts = [sem(f"in_parts{n}") for n in range(2)]
        in_expert = [sem(f"in_expert{n}") for n in range(2)]
        in_ring = [sem(f"in_ring{n}") for n in range(3)]
        block = stack.enter_context(nc.Block())

        w_in_k = w_in[0].rearrange("(t p) n -> p t n", p=P)
        ada_k = ada_w[0].rearrange("(p t) n -> p t n", t=KT)

        chunks = []

        def chunk(src, shape, done, value):
            n = len(chunks)
            chunks.append((src, slot(n, *shape), done, value))
            return n

        K_SPEC = [chunk(filter_basis[:, 2 * n:2 * n + 2], (2, TT, 2, P), "pe_spec", 4 * n + 4) for n in range(4)]
        K_ADA1 = [chunk(ada_k[:, :, n * 512:n * 512 + 512], (KT, 512), "pe_ada", n + 1) for n in range(4)]
        K_HY = [chunk(w_in_k[:, :, HY:HY + 512], (KT, 512), "pe_hy", 8),
                chunk(w_in_k[:, :, HY + 512:FN], (KT, 256), "pe_hy", 12)]
        K_CONV = []
        K_ADA2 = []

        def ada_columns(n):
            K_ADA2.append(chunk(ada_k[:, :, (6 + n) * 512:(7 + n) * 512], (KT, 512), "pe_ada2", n + 1))

        for n in range(2):
            K_CONV.append((
                [chunk(forward_basis[:, 4 * m:4 * m + 4], (4, 4, 2, P), "pe_fwd", 8 * n + 4 * m + 4) for m in range(2)],
                [chunk(inverse_basis[:, 4 * m:4 * m + 4], (4, 2, 512), "pe_inv", 2 * n + m + 1) for m in range(2)]))
            ada_columns(n)
        K_FN = chunk(w_in_k[:, :, FN:NQ], (KT, BW), "pe_fn", 4)
        K_TOK = [chunk(token_basis[:, m], (TT, 512), "pe_tok", m + 1) for m in range(2)]

        ada_columns(2)
        K_MLA = chunk(w_in_k[:, :, CQ:HY], (KT, 416), "pe_mla", AT)
        ada_columns(3)
        K_NQK = chunk(w_in_k[:, :, NQ:NV], (KT, 512), "pe_nqk", 10)
        K_NV = chunk(w_in_k[:, :, NV:GATE], (KT, BW), "pe_nv", AT)
        K_REL = []
        for n in range(2):
            K_REL.append(len(chunks))
            chunks.append((relative_columns[:, n * SLOT:n * SLOT + SLOT], slot(len(chunks), 32, P, rows=64).rearrange(
                "p a b -> p (a b)"), "pe_bb", 4 * n + 4))
        K_RES = [chunk(ada_k[:, :, n * 512:n * 512 + 512], (KT, 512), "pe_res", m + 1)
                 for m, n in enumerate((4, 5, 10, 11))]
        G0 = len(chunks)
        gate_slots = [slot(G0 + n, KT, 4, P) for n in range(2)]
        w_out_slots = [slot(G0 + 2, KT, 512), slot(G0, KT, 512)]
        expert_slots = cut(ring, 0, 2, KT, 2 * HID)
        def arrived(eng, n):
            eng.wait_ge(in_ring[n % 3], 16 * (n // 3 + 1))

        def na_group(g):
            block_of = g // 2
            if block_of < 2:
                return nqT, block_of * 512, 512
            return nkT, (block_of - 2) * 512, 512 if block_of < 4 else C
        @block.sync
        def _(sp):
            def load(dst, src, signal):
                sp.dma_start(dst, src).then_inc(s[signal], 16)

            sp.wait_ge(s["dve_zero"], 1)
            row = 0
            for src, n in ((ada_b, 48), (norm1_g, 8), (norm2_g, 8), (mla_q_norm, 2), (mla_kv_norm, 1),
                           (hy_short_w, 18), (hy_bias, 4)):
                flat = src[0] if len(src.shape) == 2 else src[0].rearrange("a n -> (a n)")
                load(staged[row:row + n, :], flat.rearrange("(r q) -> r q", q=P), "in_vec")
                row += n
            for src in (hy_b1, hy_freq1, hy_b2, hy_freq2):
                load(staged[row:row + 1, 0:64], src, "in_vec")
                row += 1
            load(w1_sb, hy_w1[0], "in_feat")
            load(w2_sb, hy_w2[0], "in_feat")
            load(feat, features, "in_feat")
            load(w3_sb, hy_w3[0], "in_feat")
            load(window_sb, window, "in_feat")
            load(cond_raw[:, 0, :], c[0].rearrange("(p t) -> p t", t=KT), "in_small")
            load(cond_raw[:, 1, :], c_ctx.rearrange("(p t) -> p t", t=KT), "in_small")
            sp.wait_ge(s["pool_rpb"], 1)
            with nc.allow_non_contiguous_dma(reason="a small table, transposed"):
                for r in range(2):
                    for h in range(HEADS):
                        load(rpb_t[32 * r:32 * r + 31, h, :], na_rpb[0, h, 1 - r:15 - r, :].rearrange("d c -> c d"), "in_rpb")
            for n, (src, dst, _, _) in enumerate(chunks):
                if n == 1:
                    load(x_sb, x[0].rearrange("(t p) d -> p t d", p=P), "in_x")
                    load(x_ctx, ctx[0].rearrange("(t p) d -> p t d", p=P), "in_x")
                    load(pk[:, :], pack, "in_x")
                if n >= 3:
                    sp.wait_ge(s[chunks[n - 3][2]], chunks[n - 3][3])
                sp.dma_start(dst, src).then_inc(in_ring[n % 3], 16)
                if n == K_MLA:
                    sp.wait_ge(s["pe_tok"], 2)
                    sp.wait_ge(s["dve_oc"], 2)
                    load(w_uq, mla_w_uq[0].rearrange("(t p) n -> p t n", p=P), "in_uq")
                    load(w_ukv, mla_w_ukv[0], "in_uq")

            sp.wait_ge(s["pe_odT"], 4)
            for dst, lo in ((res_gate1, 2048), (res_gate2, 5120)):
                load(dst, ada_b[0:1, lo:lo + D].to_broadcast([P, D]), "in_res")
            load(final_gain, final_norm_g.rearrange("(a d) -> a d", a=1).to_broadcast([P, D]), "in_res")
            load(wr[:, :, 0:4], moe_w_group[0].rearrange("(t p) n -> p t n", p=P), "in_router")
            load(wr[:, :, 4:20], moe_w_expert[0].rearrange("(t p) n -> p t n", p=P), "in_router")
            load(wr_bias[:, 0:4], moe_b_group[0:1, :].to_broadcast([P, 4]), "in_router")
            load(wr_bias[:, 4:20], moe_b_expert[0:1, :].to_broadcast([P, 16]), "in_router")

            def load_gate(d, m):
                for n in range(4):
                    sp.dma_start(gate_slots[m][:, :, n, :], w_in_k[:, :, bass.ds(d * P + GATE + n * D, P)])\
                      .then_inc(in_gate[m], 16)
                sp.dma_start(wb[:, m, :, :], w_branch[0].rearrange("n (t p) d -> p (n t) d", p=P)[:, :, bass.ds(d * P, P)])\
                  .then_inc(in_gate[m], 16)

            for m in range(2):
                sp.wait_ge(s[chunks[G0 + m - 3][2]], chunks[G0 + m - 3][3])
                load_gate(m, m)
            sp.wait_ge(s[chunks[G0 - 1][2]], chunks[G0 - 1][3])
            w_out_k = w_out[0].rearrange("(t p) n -> p t n", p=P)
            load(w_out_slots[0], w_out_k[:, :, 0:512], "in_w_out")
            with sp.Fori(0, 3) as i:
                for m in range(2):
                    sp.wait_ge(s["pe_gate"], i * 16 + 8 * (m + 1))
                    load_gate(i * 2 + m + 2, m)
            sp.wait_ge(s["pe_gate"], 56)
            sp.wait_ge(s["in_w_out"], 16)
            load(w_out_slots[1], w_out_k[:, :, 512:1024], "in_w_out")
            sp.wait_ge(s["pe_gate"], 64)
            load(x1, x[0].rearrange("(t p) d -> p t d", p=P), "in_x1")

            load(tab, routing_tab, "in_tab")
            for n in range(2):
                sp.dma_start(slots_dram[(2 + n) * T:(3 + n) * T, :], x[0]).then_inc(rows_stored, 16)
            for i in range(TT):
                sp.wait_ge(s["dve_x1n"], i + 1)
                sp.dma_start(rows_dram[i * P:i * P + P, :], x1n[:, i, :]).then_inc(rows_stored, 16)

            def load_gate_up(j, m):
                e = sp.value_load(expert_of[0:1, bass.ds(j, 1)], min_val=0, max_val=EXPERTS - 1)
                for n, w in enumerate((moe_w_gate, moe_w_up)):
                    sp.dma_start(expert_slots[:, m, :, n * HID:n * HID + HID],
                                 w[0, bass.ds(e, 1)].rearrange("e (t p) f -> p (e t) f", p=P)).then_inc(in_expert[m], 16)
                return e

            def load_down(e, m):
                sp.dma_start(w_down[:, m, :, :], moe_w_down[0, bass.ds(e, 1)].rearrange("e (t p) d -> p (e t) d", p=P))\
                  .then_inc(in_down[m], 16)

            sp.wait_ge(s["dve_table"], 1)
            sp.wait_ge(s["pe_out"], 16)
            sp.wait_ge(rows_stored, 16 * (TT + 2))
            for m in range(2):
                sp.sem_inc(y_stored[m], 16)
                load_down(load_gate_up(m, m), m)
            pairs = sp.value_load(pair_count, min_val=8, max_val=16)

            def store(j, m):
                sp.wait_ge(s["dve_y"], j * 2 + 2 + FREE)
                sp.dma_start(slots_dram[bass.ds(j * P, P), :], slot_y[:, m, :]).then_inc(y_stored[m], 16)

            with sp.Fori(0, pairs - 1) as i:
                for m in range(2):
                    sp.wait_ge(s["pe_au"], i * 2 + m + 1 + FREE)
                    e = load_gate_up(i * 2 + m + 2, m)
                    sp.wait_ge(s["pe_down"], i * 4 + 2 * m + 2 + FREE)
                    load_down(e, m)
                    store(i * 2 + m, m)
            for m in range(2):
                store(pairs * 2 + (m - 2), m)
            for i in range(TT):
                sp.wait_ge(s["dve_fin"], i + 1)
                sp.dma_start(out[0, i * P:i * P + P, :], x1[:, i, :]).then_inc(s["stored"], 16)
            sp.wait_ge(s["stored"], 16 * TT)

        @block.gpsimd
        def _(pool):
            pool.memset(ident[:, :], 0.0).then_inc(s["pool_const"], 1)
            pool.memset(rpb_t, MASK).then_inc(s["pool_rpb"], 1)
            pool.memset(ones[:, :], 1.0).then_inc(s["pool_const"], 1)
            pool.wait_ge(s["pool_const"], 2)
            pool.affine_select(out=ident[:, :], in_=ident[:, :], compare_op=ALU.not_equal, fill=1.0, base=0,
                               pattern=[[-1, P]], channel_multiplier=1).then_inc(s["pool_const"], 1)
            step = Steps(pool, s["pool_sq"])
            for i in range(TT):
                pool.wait_ge(s["dve_filt"], i + 1)
                for f in (fsum, fdif):
                    if i == 0 and f is fsum:
                        step(pool.tensor_tensor(sq_acc, f[:, i, :], f[:, i, :], ALU.mult))
                        continue
                    step(pool.tensor_tensor(sq_tmp, f[:, i, :], f[:, i, :], ALU.mult))
                    step(pool.tensor_tensor(sq_acc, sq_acc, sq_tmp, ALU.add))
            pool.wait_ge(s["pe_spec"], 16)
            pool.memset(raw[:, :, 0:1], 0.0).then_inc(s["pool_pad"], 1)
            pool.memset(raw[:, :, T + 1:T + 2], 0.0).then_inc(s["pool_pad"], 1)
            pool.wait_ge(s["dve_qT"], 8)
            with pool.Fori(0, HEADS) as h:
                for q in range(TT):
                    if q >= 2:
                        pool.wait_ge(s["pe_qk"], h * TT + q - 1)
                    pool.tensor_copy(q_now[:, q % 2, :].rearrange("p (a w) -> p a w", a=1),
                                     qT[:, bass.ds(h, 1), q * P:q * P + P]).then_inc(s["pool_q"], 1)
                pool.wait_ge(s["pe_qk"], h * TT + TT)
            pool.wait_ge(s["pe_oaT"], 4)
            pool.memset(nkT[64:128, :, :], 0.0).then_inc(s["pool_npad"], 1)
            pool.memset(nq_now[64:128, :, :], 0.0).then_inc(s["pool_npad"], 1)
            pool.wait_ge(s["act_nqk"], 10)
            pool.wait_ge(s["dve_nqk"], 10)
            with pool.Fori(0, HEADS) as h:
                for q in range(TT):
                    if q >= 2:
                        pool.wait_ge(s["pe_nqk2"], h * TT + q - 1)
                    pool.tensor_copy(nq_now[0:64, q % 2, :].rearrange("p (a w) -> p a w", a=1),
                                     nqT[:, bass.ds(h, 1), q * P:q * P + P]).then_inc(s["pool_nq"], 1)
                pool.wait_ge(s["pe_nqk2"], h * TT + TT)
            pool.wait_ge(s["pe_odT"], 4)
            pool.memset(all_ones, 1.0).then_inc(s["pool_ones"], 1)
            pool.wait_ge(s["dve_table"], 1)
            pool.wait_ge(rows_stored, 16 * (TT + 2))

            def gather(j, m):
                pool.tensor_copy(token_now[:, m:m + 1], token_of[:, bass.ds(j, 1)]).then_inc(s["pool_idx"], 1)
                pool.wait_ge(s["pool_idx"], j * 2 + 1)
                pool.sem_inc(s["pool_idx"], 1)
                pool.indirect_dma_start(slot_x[:, m, :], None, rows_dram, bass.IndirectOffsetOnAxis(token_now[:, m:m + 1], 0))\
                    .then_inc(in_slots[m], 16)

            gather(0, 0)
            pairs = pool.value_load(pair_count, min_val=8, max_val=16)
            with pool.Fori(0, pairs) as i:
                for m in range(2):
                    pool.wait_ge(s["pe_x"], i * 2 + m + FREE)
                    gather(i * 2 + m + 1, 1 - m)
            for m in range(2):
                pool.wait_ge(y_stored[m], pairs * 16 + 16)
            pool.sem_inc(s["pool_idx"], 1)
            for i in range(TT):
                if i >= 2:
                    pool.wait_ge(s["dve_moe"], i - 1)
                for n in range(2):
                    pool.indirect_dma_start(parts[:, i % 2, n, :], None, slots_dram,
                                            bass.IndirectOffsetOnAxis(slots_i[:, n, i:i + 1], 0)).then_inc(in_parts[i % 2], 16)

        @block.scalar
        def _(act):
            step = Steps(act, s["act_chain"])
            act.sem_inc(s["act_gate"], FREE)
            for layer in range(2):
                act.wait_ge(s["dve_arg"], layer + 1)
                if layer == 1:
                    act.wait_ge(s["pe_sin"], 4)
                act.activation(hid, arg, ACT.Sin).then_inc(s["act_sin"], 1)
            act.wait_ge(s["in_small"], 32)
            act.activation(cond.rearrange("p t v -> p v t"), cond_raw, ACT.Silu).then_inc(s["act_cond"], 1)
            act.wait_ge(s["in_x"], 48)
            scratch = cut(normed, 4096, D)
            for i in range(AT):
                src = x_sb[:, i, :] if i < TT else x_ctx[:, i - TT, :]
                step.mark(act.activation(scratch, src, ACT.Square, accum_out=ssq[:, i:i + 1]))
                step.sync()
            act.wait_ge(s["dve_vec"], 2)
            act.activation(rstd[:, 0:AT], ssq[:, 0:AT], ACT.Sqrt).then_inc(s["act_ssq"], 1)
            for g in range(16):
                act.wait_ge(s["pe_spec"], g + 1)
                act.activation(spec[:, g % 2, g // 2, :], bank(g % 4), ACT.Copy).then_inc(s["act_spec"], 1)
            act.wait_ge(s["dve_vec"], 3)
            act.activation(filter_norm, filter_norm, ACT.Sqrt).then_inc(s["act_ssq"], 1)
            act.wait_ge(s["dve_mod"], 1)
            act.wait_ge(s["dve_xn"], AT)
            for n in range(3 * KT):
                kt, g = n // 3, n % 3
                w = 512 if g < 2 else C
                act.wait_ge(s["pe_xT"], n + 1)
                act.activation(hT[:, kt, g * 512:g * 512 + w], bank(n % 4, 0, w), ACT.Identity,
                               bias=shift1[:, g // 2, kt:kt + 1], scale=scale1[:, g // 2, kt:kt + 1])\
                   .then_inc(s["act_hT"], 1)
            act.wait_ge(s["pool_pad"], 2)
            for g in range(12):
                ct, half = g // 2, g % 2
                if half == 0 and ct >= 2:
                    act.wait_ge(s["dve_conv"], ct - 1)
                act.wait_ge(s["pe_hy"], g + 1)
                act.activation(raw[:, ct % 2, 1 + half * 512:513 + half * 512], bank(4 + g % 4), ACT.Copy)\
                   .then_inc(s["act_hy"], 1)
            for order in range(2):
                for tt in range(4):
                    if order == 0 and tt == 0:
                        act.wait_ge(s["dve_conv"], 6)
                    act.wait_ge(s["pe_fold"], 4 * order + tt + 1)
                    act.activation(folded_t[:, tt, :, :], bank(tt), ACT.Copy).then_inc(s["act_fold"], 1)
                act.wait_ge(s["pe_inv"], 2 * order + 2)
                for ct in range(2):
                    for ab in range(2):
                        act.activation(halves[:, ct, ab, :], bank(2 * ct + ab), ACT.Copy,
                                       scale=filter_norm[:, 2 * order + ct:2 * order + ct + 1])\
                           .then_inc(s["act_inv"], 1)
            act.wait_ge(s["dve_z"], 4)
            for g in range(4):
                act.wait_ge(s["pe_fn"], g + 1)
                act.activation(fnT[:, g // 2, (g % 2) * 512:(g % 2) * 512 + 512], bank(g), ACT.Copy)\
                   .then_inc(s["act_fn"], 1)
            for i in range(TT):
                act.wait_ge(s["pe_chan"], i + 1)
                act.activation(chan_mixed[:, i, :, :, :], bank(4 + i % 4), ACT.Copy).then_inc(s["act_chan"], 1)
            act.wait_ge(s["pe_tok"], 2)
            for ct in range(2):
                act.activation(sine_part[:, ct, :], bank(4 + ct), ACT.Copy).then_inc(s["act_tok"], 1)
            square = q_tok[:, 0, :, :].rearrange("p h f -> p (h f)")
            sums = Steps(act, s["act_msq"])
            for i in range(AT):
                act.wait_ge(s["dve_mla"], i + 1)
                if i < TT:
                    sums(act.activation(square[:, 0:256], mla_tok[:, i, 0:256], ACT.Square, accum_out=ssq[:, i:i + 1]))
                sums(act.activation(square[:, 0:128], mla_tok[:, i, 256:384], ACT.Square,
                                    accum_out=ssq[:, 8 + i:9 + i]))
            act.wait_ge(s["dve_mn"], 2)
            act.activation(rstd[:, 0:18], ssq[:, 0:18], ACT.Sqrt).then_inc(s["act_mrt"], 1)
            for g in range(7):
                act.wait_ge(s["pe_mT"], g + 1)
                if g < 4:
                    act.activation(cqT[:, g // 2, (g % 2) * 512:(g % 2) * 512 + 512], bank(g), ACT.Copy,
                                   scale=vec[:, V_QN + g // 2:V_QN + g // 2 + 1]).then_inc(s["act_mT"], 1)
                else:
                    w = 512 if g < 6 else C
                    act.activation(ckvT[:, (g - 4) * 512:(g - 4) * 512 + w], bank(g, 0, w), ACT.Copy,
                                   scale=vec[:, V_KVN:V_KVN + 1]).then_inc(s["act_mT"], 1)
            for i in range(AT):
                act.wait_ge(s["pe_ukv"], i + 1)
                kv = bank(4 + i % 4).rearrange("p (h f) -> p h f", h=HEADS)
                act.activation(k_tok[:, i, :, 0:NOPE], kv[:, :, 0:NOPE], ACT.Copy).then_inc(s["act_ukv"], 1)
                act.activation(v_tok[:, i, :].rearrange("p (h f) -> p h f", h=HEADS), kv[:, :, NOPE:], ACT.Copy)\
                   .then_inc(s["act_ukv"], 1)
            for g in range(12):
                w = 512 if g % 3 < 2 else C
                act.wait_ge(s["pe_kT"], g + 1)
                if g == 0:
                    act.wait_ge(s["pe_qT"], 8)
                act.activation(kT[:, g // 3, (g % 3) * 512:(g % 3) * 512 + w], psum[0:QK, (4 + g % 4) * 512:(4 + g % 4) * 512 + w],
                               ACT.Copy).then_inc(s["act_kT"], 1)
            act.wait_ge(s["pe_kT"], 12)
            with act.Fori(0, HEADS) as h:
                def exponentials(q):
                    act.wait_ge(s["dve_mx"], h * TT + q + 1)
                    if q >= 2:
                        act.wait_ge(s["pe_t"], h * 3 * TT + 3 * (q - 1))
                    act.activation(prob[:, q % 2, :], psum[:, (q % 2) * 1536:(q % 2) * 1536 + KEYS], ACT.Exp,
                                   bias=neg_max[:, q:q + 1], scale=MLA_SCALE, accum_out=row_sum[:, q:q + 1])\
                       .then_inc(s["act_p"], 1)

                exponentials(0)
                for q in range(TT):
                    if q >= 1:
                        act.wait_ge(s["pe_pv"], h * TT + q)
                    act.wait_ge(s["pe_t"], h * 3 * TT + 3 * q + 2)
                    act.activation(probT[:, 4:8, :], bank(7), ACT.Copy).then_inc(s["act_pt"], 1)
                    if q + 1 < TT:
                        exponentials(q + 1)
                act.wait_ge(s["pe_pv"], h * TT + TT)
            for g in range(4):
                act.wait_ge(s["pe_oaT"], 4)
                act.activation(oT[0][:, g // 2, (g % 2) * 512:(g % 2) * 512 + 512], bank(g), ACT.Copy)\
                   .then_inc(s["act_oaT"], 1)
            for g in range(10):
                act.wait_ge(s["pe_nqk"], g + 1)
                dst, lo, w = na_group(g)
                act.activation(dst[0:64, (g % 2) * 2, lo:lo + w], psum[0:64, (g % 4) * 512:(g % 4) * 512 + w], ACT.Copy)\
                   .then_inc(s["act_nqk"], 1)
            for i in range(AT):
                act.wait_ge(s["pe_nv"], i + 1)
                act.activation(nv_tok[:, i, :], bank(4 + i % 4, 0, BW), ACT.Copy).then_inc(s["act_nv"], 1)
            with act.Fori(0, HEADS) as h:
                def exponentials(q):
                    n = NA_TILES[q][1] + C
                    act.wait_ge(s["dve_nmx"], h * TT + q + 1)
                    act.activation(nprob[:, q % 2, 0:n], nprob[:, q % 2, 0:n], ACT.Exp, bias=neg_max[:, q:q + 1],
                                   accum_out=row_sum[:, q:q + 1]).then_inc(s["act_np"], 1)

                exponentials(0)
                for q in range(TT):
                    n = (NA_TILES[q][1] + C) // P
                    if q >= 1:
                        act.wait_ge(s["pe_npv"], h * TT + q)
                    for r in range(2):
                        act.wait_ge(s["pe_nt"], h * 2 * TT + 2 * q + r + 1)
                        w = min(4, n - 4 * r)
                        act.activation(nprobT[:, 4 * r:4 * r + w, :], bank(4 + r, 0, w * P), ACT.Copy)\
                           .then_inc(s["act_npt"], 1)
                    if q + 1 < TT:
                        exponentials(q + 1)
                act.wait_ge(s["pe_npv"], h * TT + TT)
            for g in range(4):
                act.wait_ge(s["pe_odT"], 4)
                act.activation(oT[3][:, g // 2, (g % 2) * 512:(g % 2) * 512 + 512], bank(g), ACT.Copy)\
                   .then_inc(s["act_odT"], 1)
            with act.Fori(0, KT // 2) as i:
                for m in range(16):
                    act.wait_ge(s["dve_gate"], i * 16 + m + FREE - 1)
                    act.wait_ge(s["pe_gg"], i * 16 + m + 1)
                    act.activation(gate_sb[:, m % 2, :], bank(m % 4), ACT.Sigmoid).then_inc(s["act_gate"], 1)
            sums = Steps(act, s["act_ssq2"])
            for g in range(2):
                for i in range(4 * g, 4 * g + 4):
                    act.wait_ge(s["dve_x1"], TT + i + 1)
                    sums(act.activation(square2, x1[:, i, :], ACT.Square, accum_out=ssq[:, i:i + 1]))
                act.wait_ge(s["dve_ms2"], g + 1)
                act.activation(rstd[:, 4 * g:4 * g + 4], ssq[:, 4 * g:4 * g + 4], ACT.Sqrt).then_inc(s["act_rt2"], 1)
            act.wait_ge(s["dve_ada2"], 6)
            for n in range(2 * KT):
                g, kt = n // KT, n % KT
                act.wait_ge(s["pe_hT2"], n + 1)
                act.activation(h2T[:, kt, g * 512:g * 512 + 512], bank(n % 4), ACT.Identity,
                               bias=shift2[:, kt:kt + 1], scale=scale2[:, kt:kt + 1]).then_inc(s["act_hT2"], 1)
            act.wait_ge(s["dve_route"], 1)
            act.activation(group_exp, group_exp, ACT.Exp).then_inc(s["act_route"], 1)
            act.wait_ge(s["dve_route"], 2)
            act.activation(rc[3], rc[3], ACT.Exp).then_inc(s["act_route"], 1)
            act.wait_ge(s["dve_table"], 1)
            pairs = act.value_load(pair_count, min_val=8, max_val=16)

            def modulate(j, m):
                act.wait_ge(s["pe_au"], j + FREE - 1)
                act.wait_ge(s["pe_x"], j + 1 + FREE)
                for kt in range(4):
                    act.activation(slot_hT[:, m, kt, :], bank(2, kt * P, kt * P + P), ACT.Identity,
                                   bias=shift2[:, kt:kt + 1], scale=scale2[:, kt:kt + 1]).then_inc(s["act_h"], 1)

            modulate(0, 0)
            with act.Fori(0, pairs) as i:
                for m in range(2):
                    act.wait_ge(s["dve_mul"], i * 2 + m - 1 + FREE)
                    act.wait_ge(s["pe_au"], i * 2 + m + 1 + FREE)
                    act.activation(silu[:, m, :], bank(m, 0, HID), ACT.Silu).then_inc(s["act_silu"], 1)
                    modulate(i * 2 + m + 1, 1 - m)
            sums = Steps(act, s["act_fin"])
            for i in range(TT):
                act.wait_ge(s["dve_moe"], i + 1)
                sums(act.activation(square2, x1[:, i, :], ACT.Square, accum_out=ssq[:, i:i + 1]))
                act.wait_ge(s["dve_fms"], i + 1)
                act.activation(rstd[:, i:i + 1], ssq[:, i:i + 1], ACT.Sqrt).then_inc(s["act_frt"], 1)

        @block.vector
        def _(dve):
            step = Steps(dve, s["dve_chain"])
            for name in ("dve_mul", "dve_actT", "dve_y"):
                dve.sem_inc(s[name], FREE)
            dve.sem_inc(s["dve_gate"], FREE)
            dve.memset(staged, 0.0).then_inc(s["dve_zero"], 1)
            dve.wait_ge(s["pe_vec"], 1)
            dve.tensor_copy(vec[:, :], bank(7, 0, V_END)).then_inc(s["dve_vec"], 1)
            dve.wait_ge(s["dve_vec"], 1)
            for layer, (b, f) in enumerate(((V_B1, V_F1), (V_B2, V_F2))):
                dve.wait_ge(s["pe_sin"], 2 * layer + 2)
                if layer == 1:
                    dve.wait_ge(s["act_sin"], 1)
                step(dve.tensor_scalar(arg, psum[0:64, layer * 1024:layer * 1024 + 1024], vec[0:64, b:b + 1],
                                       vec[0:64, f:f + 1], ALU.add, ALU.mult))
                step(dve.tensor_scalar(turn, arg, 1.0 / TURN, ROUND, ALU.mult, ALU.add))
                step(dve.tensor_scalar(turn, turn, -ROUND, -TURN, ALU.add, ALU.mult))
                step(dve.tensor_tensor(arg, arg, turn, ALU.add))
                dve.tensor_scalar(arg, arg, PI, -PI, ALU.min, ALU.max).then_inc(s["dve_arg"], 1)
            dve.wait_ge(s["in_feat"], 80)
            for i in range(TT):
                dve.wait_ge(s["pe_filt"], i + 1)
                b = 4 + 2 * (i % 2)
                for dst, n in ((fir_f, 0), (fir_b, 1)):
                    step.mark(dve.tensor_tensor(
                        dst.rearrange("p (o w) -> p o w", o=2), bank(b + n).rearrange("p (o w) -> p o w", o=2),
                        window_sb[:, i, n:n + 1, :].to_broadcast([P, 2, BW]), ALU.mult))
                step.sync()
                step.mark(dve.tensor_tensor(fsum[:, i, :], fir_f, fir_b, ALU.add))
                dve.tensor_tensor(fdif[:, i, :], fir_f, fir_b, ALU.subtract).then_inc(s["dve_filt"], 1)
                dve.wait_ge(s["dve_filt"], i + 1)
                step.sync()
            dve.wait_ge(s["act_chain"], AT)
            dve.tensor_scalar(ssq[:, 0:AT], ssq[:, 0:AT], 1.0 / D, EPS, ALU.mult, ALU.add).then_inc(s["dve_vec"], 1)
            dve.wait_ge(s["act_ssq"], 1)
            step(dve.reciprocal(rstd[:, 0:AT], rstd[:, 0:AT]))
            for i in range(AT):
                row = x_sb[:, i, :] if i < TT else x_ctx[:, i - TT, :]
                dve.tensor_scalar(row, row, rstd[:, i:i + 1], None, ALU.mult).then_inc(s["dve_xn"], 1)
            dve.wait_ge(s["pe_fnorm"], 1)
            dve.tensor_scalar(filter_norm, bank(4, 0, 4), 0.5, EPS, ALU.mult, ALU.add).then_inc(s["dve_vec"], 1)
            dve.wait_ge(s["act_ssq"], 2)
            step(dve.reciprocal(filter_norm, filter_norm))
            dve.wait_ge(s["pe_ada"], 4)
            for v in range(2):
                m = bank(5, 0, 32).rearrange("p (b v) -> p b v", v=2)
                step(dve.tensor_tensor(shift1[:, v, :], m[:, 0:8, v], vec[:, 0:8], ALU.add))
                step(dve.tensor_tensor(scale1[:, v, :], m[:, 8:16, v], vec[:, 8:16], ALU.add))
                ins = dve.scalar_tensor_tensor(out=scale1[:, v, :], in0=scale1[:, v, :], scalar=1.0,
                                               in1=vec[:, V_N1:V_N1 + 8], op0=ALU.add, op1=ALU.mult)
                if v == 0:
                    step(ins)
                else:
                    ins.then_inc(s["dve_mod"], 1)
            for ct in range(6):
                dve.wait_ge(s["act_hy"], 2 * ct + 2)
                tap = [vec[:, V_TAP + 6 * j + ct:V_TAP + 6 * j + ct + 1] for j in range(3)]
                u = raw[:, ct % 2, :]
                step(dve.tensor_scalar(conv[:, ct, :], u[:, 1:T + 1], tap[1], None, ALU.mult))
                step(dve.scalar_tensor_tensor(out=conv[:, ct, :], in0=u[:, 0:T], scalar=tap[0],
                                              in1=conv[:, ct, :], op0=ALU.mult, op1=ALU.add))
                dve.scalar_tensor_tensor(out=conv[:, ct, :], in0=u[:, 2:T + 2], scalar=tap[2],
                                         in1=conv[:, ct, :], op0=ALU.mult, op1=ALU.add)\
                   .then_inc(s["dve_conv"], 1)
            dve.wait_ge(s["dve_conv"], 6)
            def ada_column(n):
                dst = (shift2, scale2)[n // 2][:, 4 * (n % 2):4 * (n % 2) + 4]
                b = V_ADAB + 24 + 4 * n
                dve.wait_ge(s["pe_ada2"], n + 1)
                dve.tensor_tensor(dst, bank((4, 4, 7, 7)[n], 0, 8).rearrange("p (m v) -> p m v", v=2)[:, :, 0],
                                  vec[:, b:b + 4], ALU.add).then_inc(s["dve_ada2"], 1)

            for order in range(2):
                if order == 1:
                    dve.wait_ge(s["dve_z"], 2)
                for ct in range(2):
                    z = conv[:, ct, :]
                    for n, op in enumerate((ALU.add, ALU.subtract)):
                        dve.tensor_tensor(folded[:, n, ct, :], z[:, 0:512], z[:, T - 1:511:-1], op)\
                           .then_inc(s["dve_fold"], 1)
                for j in range(KT):
                    re, im = (spec[:, n, j:j + 1, order * BW:order * BW + BW].to_broadcast([P, 2, BW]) for n in range(2))
                    u = bank(4 + j % 4).rearrange("p (n w) -> p n w", n=2)
                    if j == 0 and order == 0:
                        dve.wait_ge(s["act_spec"], 16)
                    dve.wait_ge(s["pe_fwd"], 8 * order + j + 1)
                    step.mark(dve.tensor_tensor(prod_r, u, re, ALU.mult))
                    step(dve.tensor_tensor(prod_i, u, im, ALU.mult))
                    step.mark(dve.tensor_tensor(conv_spec[:, j, 0, :], prod_r[:, 0, :], prod_i[:, 1, :], ALU.subtract))
                    dve.tensor_tensor(conv_spec[:, j, 1, :], prod_r[:, 1, :], prod_i[:, 0, :], ALU.add)\
                       .then_inc(s["dve_spec"], 1)
                    dve.wait_ge(s["dve_spec"], 8 * order + j + 1)
                    step.sync()
                ada_column(order)
                dve.wait_ge(s["act_inv"], 4 * order + 4)
                for ct in range(2):
                    a, b = halves[:, ct, 0, :], halves[:, ct, 1, :]
                    step.mark(dve.tensor_tensor(mix[:, 0:512], a, b, ALU.add))
                    step(dve.tensor_tensor(mix[:, T - 1:511:-1], a, b, ALU.subtract))
                    h = V_HB + 2 * order + ct
                    step(dve.scalar_tensor_tensor(out=mix, in0=conv[:, ct, :], scalar=vec[:, h:h + 1], in1=mix,
                                                  op0=ALU.mult, op1=ALU.add))
                    dst = conv[:, ct, :] if order == 0 else oT[1][:, ct, :]
                    dve.tensor_tensor(dst, mix, conv[:, 2 + 2 * order + ct, :], ALU.mult).then_inc(s["dve_z"], 1)
                    dve.wait_ge(s["dve_z"], 2 * order + ct + 1)
            dve.wait_ge(s["act_tok"], 2)
            for ct in range(2):
                o = oT[2][:, ct, :]
                sn = sine_part[:, ct, :]
                step.mark(dve.tensor_tensor(o[:, 0:512], bank(ct), sn, ALU.add))
                step.mark(dve.tensor_tensor(o[:, T - 1:512:-1], bank(ct, 1, 512), sn[:, 1:512], ALU.subtract))
                dve.tensor_copy(o[:, 512:513], bank(2, ct, ct + 1)).then_inc(s["dve_oc"], 1)
            step.sync()
            ada_column(2)
            for i in range(AT):
                lo = 0 if i < TT else 256
                dve.wait_ge(s["pe_mla"], i + 1)
                dve.tensor_copy(mla_tok[:, i, lo:416], bank(i % 4, lo, 416)).then_inc(s["dve_mla"], 1)
            dve.wait_ge(s["act_msq"], 2 * TT + CT)
            norms = Steps(dve, s["dve_mn"])
            norms.mark(dve.tensor_scalar(ssq[:, 0:8], ssq[:, 0:8], 1.0 / 256, EPS, ALU.mult, ALU.add))
            norms.mark(dve.tensor_scalar(ssq[:, 8:18], ssq[:, 8:18], 1.0 / 128, EPS, ALU.mult, ALU.add))
            dve.wait_ge(s["act_mrt"], 1)
            dve.wait_ge(s["dve_mla"], AT)
            step(dve.reciprocal(rstd[:, 0:18], rstd[:, 0:18]))
            for i in range(TT):
                norms.mark(dve.tensor_scalar(mla_tok[:, i, 0:256], mla_tok[:, i, 0:256], rstd[:, i:i + 1], None, ALU.mult))
            for i in range(AT):
                norms.mark(dve.tensor_scalar(mla_tok[:, i, 256:384], mla_tok[:, i, 256:384], rstd[:, 8 + i:9 + i], None,
                                             ALU.mult))
            for i in range(TT):
                dve.wait_ge(s["pe_uq"], i + 1)
                dve.tensor_copy(q_tok[:, i, :, :], bank(i % 4, 0, 384)).then_inc(s["dve_uq"], 1)
            dve.wait_ge(s["dve_uq"], TT)
            kr = mla_tok[:, 0:TT, KR:416].rearrange("p t (h f) -> p t h f", h=1)
            for x4, heads in ((q_tok[:, :, :, NOPE:QK], HEADS), (kr, 1)):
                cos, sin = (rope_t[:, n, :, :].rearrange("p t (h f) -> p t h f", h=1).to_broadcast([P, TT, heads, 16])
                            for n in range(2))
                even, odd = x4[:, :, :, 0::2], x4[:, :, :, 1::2]
                r = [t[:, :, 0:heads, :] for t in rot]
                step.mark(dve.tensor_tensor(r[0], even, cos, ALU.mult))
                step.mark(dve.tensor_tensor(r[1], odd, sin, ALU.mult))
                step.mark(dve.tensor_tensor(r[2], even, sin, ALU.mult))
                step(dve.tensor_tensor(r[3], odd, cos, ALU.mult))
                step.mark(dve.tensor_tensor(even, r[0], r[1], ALU.subtract))
                step(dve.tensor_tensor(odd, r[2], r[3], ALU.add))
            for h in range(HEADS):
                dve.tensor_copy(k_tok[:, :, h, NOPE:QK], mla_tok[:, :, KR:416]).then_inc(s["dve_rope"], 1)
            for g in range(8):
                if g == 0:
                    dve.wait_ge(s["dve_rope"], HEADS)
                dve.wait_ge(s["pe_qT"], g + 1)
                dve.tensor_copy(qT[:, g // 2, (g % 2) * 512:(g % 2) * 512 + 512], psum[0:QK, (g % 4) * 512:(g % 4) * 512 + 512])\
                   .then_inc(s["dve_qT"], 1)
            dve.wait_ge(s["act_kT"], 12)
            with dve.Fori(0, HEADS) as h:
                step.enter(h, 2 * TT)

                def row_max(q):
                    dve.wait_ge(s["pe_qk"], h * TT + q + 1)
                    step(dve.tensor_reduce(neg_max[:, q:q + 1], psum[:, (q % 2) * 1536:(q % 2) * 1536 + KEYS], AX.X, ALU.max))
                    dve.tensor_scalar(neg_max[:, q:q + 1], neg_max[:, q:q + 1], -MLA_SCALE, None, ALU.mult)\
                       .then_inc(s["dve_mx"], 1)

                def output(q):
                    dve.wait_ge(s["pe_pv"], h * TT + q + 1)
                    step(dve.reciprocal(row_inv[:, q:q + 1], row_sum[:, q:q + 1]))
                    dve.tensor_scalar(oa_tok[:, q, bass.ds(h * VD, VD)], bank(7, 0, VD),
                                      row_inv[:, q:q + 1], None, ALU.mult).then_inc(s["dve_o"], 1)

                row_max(0)
                for q in range(TT):
                    if q >= 1:
                        output(q - 1)
                    if q >= 1:
                        dve.wait_ge(s["pe_pv"], h * TT + q)
                    dve.wait_ge(s["pe_t"], h * 3 * TT + 3 * q + 1)
                    dve.tensor_copy(probT[:, 0:4, :], bank(6)).then_inc(s["dve_pt"], 1)
                    if q + 1 < TT:
                        row_max(q + 1)
                    dve.wait_ge(s["pe_t"], h * 3 * TT + 3 * q + 3)
                    dve.tensor_copy(probT[:, 8:10, :], bank(6, 0, 256)).then_inc(s["dve_pt"], 1)
                output(TT - 1)
            step.leave(HEADS, 2 * TT)
            ada_column(3)
            for g in range(10):
                dve.wait_ge(s["pe_nqk"], g + 1)
                dst, lo, w = na_group(g)
                dve.tensor_copy(dst[0:64, (g % 2) * 2 + 1, lo:lo + w], psum[64:128, (g % 4) * 512:(g % 4) * 512 + w])\
                   .then_inc(s["dve_nqk"], 1)
            for b in range(8):
                dve.wait_ge(s["pe_bb"], b + 1)
                dve.tensor_copy(
                    rel_bias.rearrange("p h (r k) -> p (h r) k", k=64)[:, :, 8 * b:8 * b + 8],
                    bank(b, 0, 448).rearrange("p (k r) -> p r k", k=8)).then_inc(s["dve_bb"], 1)
            dve.wait_ge(s["dve_bb"], 8)
            with dve.Fori(0, HEADS) as h:
                step.enter(h, 1 + 4 * TT)
                mask = row_mask.rearrange("p a b -> p (a b)").rearrange("p (a w) -> p a w", a=1)
                step(dve.tensor_tensor(inner_bias.rearrange("p (a w) -> p a w", a=1), rel_bias[:, bass.ds(h, 1), 128:768],
                                       mask, ALU.add))

                def row_max(q):
                    first, n, col = NA_TILES[q]
                    dve.wait_ge(s["pe_nqk2"], h * TT + q + 1)
                    if q >= 2:
                        dve.wait_ge(s["pe_nt"], h * 2 * TT + 2 * (q - 1))
                    local = nprob[:, q % 2, 0:n].rearrange("p (a w) -> p a w", a=1)
                    scores = psum[:, (q % 2) * 1024:(q % 2) * 1024 + n + C]
                    bias = inner_bias.rearrange("p (a w) -> p a w", a=1) if col is None else \
                        rel_bias[:, bass.ds(h, 1), col:col + n]
                    step.mark(dve.scalar_tensor_tensor(out=local, in0=scores[:, 0:n].rearrange("p (a w) -> p a w", a=1),
                                                       scalar=NA_SCALE, in1=bias, op0=ALU.mult, op1=ALU.add))
                    step(dve.tensor_scalar(nprob[:, q % 2, n:n + C], scores[:, n:n + C], NA_SCALE, None, ALU.mult))
                    step(dve.tensor_reduce(neg_max[:, q:q + 1], nprob[:, q % 2, 0:n + C], AX.X, ALU.max))
                    dve.tensor_scalar(neg_max[:, q:q + 1], neg_max[:, q:q + 1], -1.0, None, ALU.mult)\
                       .then_inc(s["dve_nmx"], 1)

                def output(q):
                    dve.wait_ge(s["pe_npv"], h * TT + q + 1)
                    step(dve.reciprocal(row_inv[:, q:q + 1], row_sum[:, q:q + 1]))
                    dve.tensor_scalar(od_tok[:, q, bass.ds(h * VD, VD)], bank(6 + q % 2, 0, VD),
                                      row_inv[:, q:q + 1], None, ALU.mult).then_inc(s["dve_no"], 1)

                row_max(0)
                for q in range(TT):
                    if q + 1 < TT:
                        row_max(q + 1)
                    if q >= 1:
                        output(q - 1)
                output(TT - 1)
            step.leave(HEADS, 1 + 4 * TT)
            dve.wait_ge(s["dve_ada2"], 4)
            dve.scalar_tensor_tensor(out=scale2, in0=scale2, scalar=1.0, in1=vec[:, V_N2:V_N2 + 8], op0=ALU.add,
                                     op1=ALU.mult).then_inc(s["dve_ada2"], 2)
            dve.wait_ge(s["pe_odT"], 4)
            dve.tensor_copy(cond_rows, cond[:, :, 0:1].to_broadcast([P, KT, P])).then_inc(s["dve_cond"], 1)
            dve.wait_ge(s["in_res"], 48)
            for n in range(4):
                dve.wait_ge(s["pe_res"], n + 1)
                dst = (res_gate1, res_gate2)[n // 2][:, (n % 2) * 512:(n % 2) * 512 + 512]
                dve.tensor_tensor(dst, dst, bank(4 + n), ALU.add).then_inc(s["dve_res"], 1)
            with dve.Fori(0, KT // 2) as i:
                step.enter(i, 12)
                for m in range(16):
                    n, half = (m // 2) % 4, m % 2
                    dst = merged[:, bass.ds(i * 2 + m // 8, 1), half * 512:half * 512 + 512]
                    g, p = (t.rearrange("p (a w) -> p a w", a=1) for t in (gate_sb[:, m % 2, :], bank(4 + m % 4)))
                    dve.wait_ge(s["pe_gate"], i * 16 + m + 1)
                    dve.wait_ge(s["act_gate"], i * 16 + m + FREE + 1)
                    if n == 0:
                        dve.tensor_tensor(dst, g, p, ALU.mult).then_inc(s["dve_gate"], 1)
                    else:
                        add = gated.rearrange("p (a w) -> p a w", a=1)
                        dve.wait_ge(s["dve_gate"], i * 16 + m + FREE)
                        step(dve.tensor_tensor(add, g, p, ALU.mult))
                        dve.tensor_tensor(dst, dst, add, ALU.add).then_inc(s["dve_gate"], 1)
            step.leave(KT // 2, 12)
            dve.wait_ge(s["in_x1"], 16)
            for m in range(16):
                half, i = m // TT, m % TT
                lo = half * 512
                dve.wait_ge(s["pe_out"], m + 1)
                dve.wait_ge(s["dve_x1"], m)
                step(dve.tensor_tensor(gated, bank(m % 8), res_gate1[:, lo:lo + 512], ALU.mult))
                dve.tensor_tensor(x1[:, i, lo:lo + 512], x1[:, i, lo:lo + 512], gated, ALU.add).then_inc(s["dve_x1"], 1)
            for g in range(2):
                dve.wait_ge(s["act_ssq2"], 4 * g + 4)
                dve.tensor_scalar(ssq[:, 4 * g:4 * g + 4], ssq[:, 4 * g:4 * g + 4], 1.0 / D, EPS, ALU.mult, ALU.add)\
                   .then_inc(s["dve_ms2"], 1)
                dve.wait_ge(s["act_rt2"], g + 1)
                step(dve.reciprocal(rstd[:, 4 * g:4 * g + 4], rstd[:, 4 * g:4 * g + 4]))
                for i in range(4 * g, 4 * g + 4):
                    dve.tensor_scalar(x1n[:, i, :], x1[:, i, :], rstd[:, i:i + 1], None, ALU.mult)\
                       .then_inc(s["dve_x1n"], 1)

            def column(t):
                return t.rearrange("p (t a) -> p t a", a=1)

            def first_equal(hot, values, top):
                seen = column(rc[7])
                step(dve.tensor_tensor(hot, values, column(top).to_broadcast([P, TT, 4]), ALU.is_equal))
                step(dve.tensor_copy(seen, hot[:, :, 0:1]))
                for j in range(1, 4):
                    step(dve.tensor_tensor(hot[:, :, j:j + 1], hot[:, :, j:j + 1], seen, ALU.is_gt))
                    if j < 3:
                        step(dve.tensor_tensor(seen, seen, hot[:, :, j:j + 1], ALU.max))

            dve.wait_ge(s["in_router"], 64)
            dve.wait_ge(s["pe_route"], 1)
            step(dve.tensor_tensor(logits, bank(4, 0, 160).rearrange("p (t n) -> p t n", n=20),
                                   wr_bias.rearrange("p (a n) -> p a n", a=1).to_broadcast([P, TT, 20]), ALU.add))
            group_logit = logits[:, :, 0:4]
            step(dve.tensor_reduce(rc[0], group_logit, AX.X, ALU.max))
            dve.tensor_tensor(group_exp, group_logit, column(rc[0]).to_broadcast([P, TT, 4]), ALU.subtract)\
               .then_inc(s["dve_route"], 1)
            first_equal(group_hot, group_logit, rc[0])
            picked = pick.rearrange("p t (g e) -> p t g e", g=4)
            step(dve.tensor_tensor(picked, logits[:, :, 4:20].rearrange("p t (g e) -> p t g e", g=4),
                                   group_hot.rearrange("p t (g a) -> p t g a", a=1).to_broadcast([P, TT, 4, 4]), ALU.mult))
            step(dve.tensor_reduce(expert_logit, picked.rearrange("p t g e -> p t e g"), AX.X, ALU.add))
            step(dve.tensor_reduce(rc[1], expert_logit, AX.X, ALU.max))
            first_equal(expert_hot, expert_logit, rc[1])
            step(dve.scalar_tensor_tensor(out=expert_logit, in0=expert_hot, scalar=MASK, in1=expert_logit, op0=ALU.mult,
                                          op1=ALU.add))
            step(dve.tensor_reduce(rc[2], expert_logit, AX.X, ALU.max))
            first_equal(second_hot, expert_logit, rc[2])
            dve.tensor_tensor(rc[3], rc[2], rc[1], ALU.subtract).then_inc(s["dve_route"], 1)
            dve.wait_ge(s["act_route"], 2)
            step(dve.tensor_reduce(rc[4], group_exp, AX.X, ALU.add))
            step(dve.tensor_scalar(rc[5], rc[3], 1.0, None, ALU.add))
            step(dve.tensor_tensor(rc[5], rc[5], rc[4], ALU.mult))
            step(dve.reciprocal(rc[5], rc[5]))
            step(dve.tensor_tensor(rc[6], rc[5], rc[3], ALU.mult))

            def outer(dst, experts):
                return dve.tensor_tensor(dst.rearrange("p t (g e) -> p t g e", g=4),
                                         group_hot.rearrange("p t (g a) -> p t g a", a=1).to_broadcast([P, TT, 4, 4]),
                                         experts.rearrange("p t (a e) -> p t a e", a=1).to_broadcast([P, TT, 4, 4]), ALU.mult)

            step(outer(first_of, expert_hot))
            step(outer(second_of, second_hot))
            dve.tensor_tensor(both_of, first_of, second_of, ALU.add).then_inc(s["dve_both"], 1)
            dve.wait_ge(s["pe_count"], 1)
            inside = bank(5, 0, P).rearrange("p (t e) -> p t e", t=TT)
            total = bank(5, P, 2 * P).rearrange("p (t e) -> p t e", t=TT)
            step(dve.memset(tile_off[:, 0, :], 0.0))
            for t in range(1, TT):
                step(dve.tensor_tensor(tile_off[:, t, :], tile_off[:, t - 1, :], total[:, t - 1, :], ALU.add))
            step(dve.tensor_tensor(count, tile_off[:, TT - 1, :], total[:, TT - 1, :], ALU.add))

            def round_to_integer(t):
                step(dve.tensor_scalar(t, t, ROUND, None, ALU.add))
                step(dve.tensor_scalar(t, t, -ROUND, None, ALU.add))

            step(dve.tensor_scalar(tiles, count, 1.0 / P, (P - 1.0) / P - 0.5 + 0.5 / P, ALU.mult, ALU.add))
            round_to_integer(tiles)
            step(dve.memset(one_row, 1.0))
            step(dve.tensor_tensor_scan(upto, one_row, tiles, 0.0, ALU.mult, ALU.add))
            step(dve.tensor_tensor(base_of, upto, tiles, ALU.subtract))
            step(dve.tensor_scalar(base_of, base_of, float(P), None, ALU.mult))
            step(dve.tensor_tensor(slot_of, inside, tile_off, ALU.add))
            step(dve.tensor_tensor(slot_of, slot_of, base_of.rearrange("p (a e) -> p a e", a=1).to_broadcast([P, TT, EXPERTS]),
                                   ALU.add))
            for n, hot in enumerate((first_of, second_of)):
                step(dve.tensor_tensor(masked, hot, slot_of, ALU.mult))
                step(dve.tensor_reduce(slots_f[:, n, :], masked, AX.X, ALU.add))
            step(dve.tensor_scalar(slot_tile, slots_f, 1.0 / P, -0.5 + 0.5 / P, ALU.mult, ALU.add))
            round_to_integer(slot_tile)
            step(dve.scalar_tensor_tensor(out=slot_row, in0=slot_tile, scalar=-float(P), in1=slots_f, op0=ALU.mult, op1=ALU.add))
            dve.wait_ge(s["pe_route"], 1)
            for n in range(2):
                step(dve.tensor_tensor(row_hot[:, n, :, :], column_no.rearrange("p (a k) -> p a k", a=1).to_broadcast([P, TT, P]),
                                       column(slot_row[:, n, :]).to_broadcast([P, TT, P]), ALU.is_equal))
                hot = tile_hot[:, n, :, 1, :]
                step(dve.tensor_tensor(hot, column_no[:, 0:32].rearrange("p (a k) -> p a k", a=1).to_broadcast([P, TT, 32]),
                                       column(slot_tile[:, n, :]).to_broadcast([P, TT, 32]), ALU.is_equal))
                step(dve.tensor_tensor(tile_hot[:, n, :, 0, :], hot, column(token_no).to_broadcast([P, TT, 32]), ALU.mult))
                dve.tensor_tensor(hot, hot, column(rc[5 + n]).to_broadcast([P, TT, 32]), ALU.mult).then_inc(s["dve_hot"], 1)
            step(dve.tensor_tensor(ended, upto.rearrange("p (a e) -> p a e", a=1).to_broadcast([P, 34, EXPERTS]),
                                   column_no[:, 0:34].rearrange("p (k a) -> p k a", a=1).to_broadcast([P, 34, EXPERTS]),
                                   ALU.is_le))
            step(dve.tensor_reduce(ended_sum, ended, AX.X, ALU.add))
            step(dve.tensor_scalar(expert_of, ended_sum, EXPERTS - 1.0, None, ALU.min))
            step(dve.tensor_scalar(pairs_f[:, 0:1], upto[:, EXPERTS - 1:EXPERTS], 0.5, 0.25, ALU.mult, ALU.add))
            round_to_integer(pairs_f[:, 0:1])
            step(dve.tensor_copy(pair_count, pairs_f[0:1, 0:1]))
            step(dve.tensor_copy(slots_i, slots_f))
            step(dve.memset(token_of, 0))
            dve.wait_ge(s["pe_table"], 1)
            step(dve.tensor_copy(weight_t, bank(6, 32, 64)))
            dve.tensor_copy(token_of[:, 0:32], bank(6, 0, 32)).then_inc(s["dve_table"], 1)
            dve.wait_ge(s["dve_table"], 1)
            pairs = dve.value_load(pair_count, min_val=8, max_val=16)

            def modulate(j, m):
                dve.wait_ge(s["pe_au"], j + FREE - 1)
                dve.wait_ge(s["pe_x"], j + 1 + FREE)
                for kt in range(4, KT):
                    dve.tensor_scalar(slot_hT[:, m, kt, :], bank(3, (kt - 4) * P, (kt - 3) * P), scale2[:, kt:kt + 1],
                                      shift2[:, kt:kt + 1], ALU.mult, ALU.add).then_inc(s["dve_h"], 1)

            modulate(0, 0)
            with dve.Fori(0, pairs) as i:
                for m in range(2):
                    dve.wait_ge(s["pe_actT"], i * 2 + m - 1 + FREE)
                    dve.wait_ge(s["act_silu"], i * 2 + m + 1)
                    dve.tensor_tensor(act_tok[:, m, :], silu[:, m, :], bank(m, HID, 2 * HID), ALU.mult)\
                       .then_inc(s["dve_mul"], 1)
                    modulate(i * 2 + m + 1, 1 - m)
                    dve.wait_ge(s["pe_down"], i * 4 + 2 * m - 2 + FREE)
                    dve.wait_ge(s["pe_actT"], i * 2 + m + 1 + FREE)
                    dve.tensor_copy(actT[:, m, :], bank(4 + m, 0, HID)).then_inc(s["dve_actT"], 1)
                    dve.wait_ge(y_stored[m], i * 16 + 16)
                    for half in range(2):
                        dve.wait_ge(s["pe_down"], i * 4 + 2 * m + half + 1 + FREE)
                        lo = half * 512
                        dve.scalar_tensor_tensor(out=slot_y[:, m, lo:lo + 512], in0=bank(6 + half),
                                                 scalar=weight_t[:, bass.ds(i * 2 + m, 1)], in1=res_gate2[:, lo:lo + 512],
                                                 op0=ALU.mult, op1=ALU.mult).then_inc(s["dve_y"], 1)
            def residual(i):
                dve.wait_ge(in_parts[i % 2], 32 * (i // 2 + 1))
                step(dve.tensor_tensor(x1[:, i, :], x1[:, i, :], parts[:, i % 2, 0, :], ALU.add))
                dve.tensor_tensor(x1[:, i, :], x1[:, i, :], parts[:, i % 2, 1, :], ALU.add).then_inc(s["dve_moe"], 1)

            residual(0)
            dve.wait_ge(s["in_res"], 48)
            for i in range(TT):
                if i + 1 < TT:
                    residual(i + 1)
                dve.wait_ge(s["act_fin"], i + 1)
                dve.tensor_scalar(ssq[:, i:i + 1], ssq[:, i:i + 1], 1.0 / D, EPS, ALU.mult, ALU.add).then_inc(s["dve_fms"], 1)
                dve.wait_ge(s["act_frt"], i + 1)
                step(dve.reciprocal(rstd[:, i:i + 1], rstd[:, i:i + 1]))
                dve.scalar_tensor_tensor(out=x1[:, i, :], in0=x1[:, i, :], scalar=rstd[:, i:i + 1], in1=final_gain,
                                         op0=ALU.mult, op1=ALU.mult).then_inc(s["dve_fin"], 1)

        @block.tensor
        def _(pe):
            def mm(dst, lhsT, rhs, first, last):
                return pe.matmul(dst, lhsT, rhs, start=first, stop=last)

            for name in ("pe_au", "pe_x", "pe_actT", "pe_down"):
                pe.sem_inc(s[name], FREE)
            pe.wait_ge(s["pool_const"], 3)
            pe.wait_ge(s["in_vec"], 16 * 11)
            pe.transpose(bank(7, 0, P), staged, ident[:, :]).then_inc(s["pe_vec"], 1)
            pe.wait_ge(s["in_feat"], 80)
            for layer in range(2):
                for half in range(2):
                    lo = half * 512
                    dst = psum[0:64, layer * 1024 + lo:layer * 1024 + lo + 512]
                    if layer == 1:
                        pe.wait_ge(s["act_sin"], 1)
                    mm(dst, w1_sb if layer == 0 else w2_sb, (feat if layer == 0 else hid)[:, lo:lo + 512], True, True)\
                        .then_inc(s["pe_sin"], 1)
            pe.wait_ge(s["act_sin"], 2)
            pe.wait_ge(s["dve_vec"], 1)
            for i in range(TT):
                if i >= 2:
                    pe.wait_ge(s["dve_filt"], i - 1)
                b = 4 + 2 * (i % 2)
                mm(bank(b), hid[:, i * P:i * P + P], w3_sb[:, 0:512], True, True)
                mm(bank(b + 1), hid[:, i * P:i * P + P], w3_sb[:, 512:1024], True, True).then_inc(s["pe_filt"], 1)
            pe.wait_ge(s["dve_filt"], TT)
            for g in range(16):
                j, part = g // 2, g % 2
                n = K_SPEC[j // 2]
                if g % 4 == 0:
                    arrived(pe, n)
                if g >= 4:
                    pe.wait_ge(s["act_spec"], g - 3)
                table = slot(n, 2, TT, 2, P)
                for i in range(TT):
                    last = mm(bank(g % 4), table[:, j % 2, i, part, :], (fsum, fdif)[part][:, i, :], i == 0, i == TT - 1)
                last.then_inc(s["pe_spec"], 1)
            pe.wait_ge(s["pool_sq"], 4 * TT - 1)
            for n in range(4):
                last = mm(bank(4, n, n + 1), sq_acc[:, n * P:n * P + P], ones[:, 0:1], True, True)
            last.then_inc(s["pe_fnorm"], 1)
            pe.wait_ge(s["act_cond"], 1)
            for n in range(4):
                arrived(pe, K_ADA1[n])
                w = slot(K_ADA1[n], KT, 512)
                for m in range(4):
                    cb = 2 * (4 * n + m)
                    for t in range(KT):
                        last = mm(bank(5, cb, cb + 2), w[:, t, m * P:m * P + P], cond[:, t, :], t == 0, t == KT - 1)
                last.then_inc(s["pe_ada"], 1)
            pe.wait_ge(s["dve_xn"], AT)
            pe.wait_ge(s["act_spec"], 16)
            for n in range(3 * KT):
                kt, g = n // 3, n % 3
                if n >= 4:
                    pe.wait_ge(s["act_hT"], n - 3)
                for i in range(4 if g < 2 else CT):
                    src = x_sb[:, 4 * g + i, :] if g < 2 else x_ctx[:, i, :]
                    last = pe.transpose(bank(n % 4, i * P, i * P + P), src[:, kt * P:kt * P + P], ident[:, :])
                last.then_inc(s["pe_xT"], 1)
            pe.wait_ge(s["act_hT"], 3 * KT)
            pe.wait_ge(s["dve_mod"], 1)
            for g in range(12):
                ct, half = g // 2, g % 2
                n = K_HY[ct // 4]
                arrived(pe, n)
                if g >= 4:
                    pe.wait_ge(s["act_hy"], g - 3)
                w = slot(n, KT, 512 if ct < 4 else 256)
                for k in range(KT):
                    last = mm(bank(4 + g % 4), w[:, k, (ct % 4) * P:(ct % 4) * P + P],
                              hT[:, k, half * 512:half * 512 + 512], k == 0, k == KT - 1)
                last.then_inc(s["pe_hy"], 1)
            pe.wait_ge(s["act_hy"], 12)

            def ada_column(n):
                arrived(pe, K_ADA2[n])
                w = slot(K_ADA2[n], KT, 512)
                for m in range(4):
                    for t in range(KT):
                        last = mm(bank((4, 4, 7, 7)[n], 2 * m, 2 * m + 2), w[:, t, m * P:m * P + P], cond[:, t, :],
                                  t == 0, t == KT - 1)
                last.then_inc(s["pe_ada2"], 1)

            for order in range(2):
                pe.wait_ge(s["dve_fold"], 4 * order + 4)
                if order == 1:
                    pe.wait_ge(s["act_inv"], 4)
                for tt in range(4):
                    for n in range(2):
                        for ct in range(2):
                            last = pe.transpose(bank(tt, (2 * n + ct) * P, (2 * n + ct + 1) * P),
                                                folded[:, n, ct, tt * P:tt * P + P], ident[:, :])
                    last.then_inc(s["pe_fold"], 1)
                pe.wait_ge(s["act_fold"], 4 * order + 4)
                for j in range(KT):
                    n = K_CONV[order][0][j // 4]
                    arrived(pe, n)
                    table = slot(n, 4, 4, 2, P)
                    if 8 * order + j >= 4:
                        pe.wait_ge(s["dve_spec"], 8 * order + j - 3)
                    if order == 1 and j == 0:
                        pe.wait_ge(s["dve_ada2"], 1)
                    for m in range(2):
                        src = m if j < 4 else 1 - m
                        for tt in range(4):
                            last = mm(bank(4 + j % 4, m * BW, m * BW + BW), table[:, j % 4, tt, m, :],
                                      folded_t[:, tt, src, :], tt == 0, tt == 3)
                    last.then_inc(s["pe_fwd"], 1)
                for j in range(KT):
                    n = K_CONV[order][1][j // 4]
                    arrived(pe, n)
                    table = slot(n, 4, 2, 512)
                    pe.wait_ge(s["dve_spec"], 8 * order + j + 1)
                    for ct in range(2):
                        for m in range(2):
                            ab = m if j < 4 else 1 - m
                            last = mm(bank(2 * ct + ab), conv_spec[:, j, m, ct * P:ct * P + P], table[:, j % 4, m, :],
                                      j == 0, j == KT - 1)
                    if j % 4 == 3:
                        last.then_inc(s["pe_inv"], 1)
                ada_column(order)
            pe.wait_ge(s["act_inv"], 8)
            pe.wait_ge(s["dve_ada2"], 2)
            arrived(pe, K_FN)
            w = slot(K_FN, KT, BW)
            for g in range(4):
                for k in range(KT):
                    last = mm(bank(g), w[:, k, (g // 2) * P:(g // 2) * P + P],
                              hT[:, k, (g % 2) * 512:(g % 2) * 512 + 512], k == 0, k == KT - 1)
                last.then_inc(s["pe_fn"], 1)
            pe.wait_ge(s["act_fn"], 4)
            pe.wait_ge(s["in_x"], 48)
            for i in range(TT):
                if i >= 4:
                    pe.wait_ge(s["act_chan"], i - 3)
                for ct in range(2):
                    last = mm(bank(4 + i % 4, ct * 256, ct * 256 + 256), fnT[:, ct, i * P:i * P + P], chan_basis,
                              True, True)
                last.then_inc(s["pe_chan"], 1)
            pe.wait_ge(s["act_chan"], TT)
            for part in range(2):
                arrived(pe, K_TOK[part])
                table = slot(K_TOK[part], TT, 512)
                for ct in range(2):
                    for i in range(TT):
                        last = mm(bank(4 * part + ct), chan_mixed[:, i, ct, part, :], table[:, i, :], i == 0, i == TT - 1)
                    if part == 0:
                        for i in range(TT):
                            last = mm(bank(2, ct, ct + 1), chan_mixed[:, i, ct, 0, :], alternate, i == 0, i == TT - 1)
                last.then_inc(s["pe_tok"], 1)
            ada_column(2)
            arrived(pe, K_MLA)
            pe.wait_ge(s["dve_oc"], 2)
            w = slot(K_MLA, KT, 416)
            for i in range(AT):
                if i >= 4:
                    pe.wait_ge(s["dve_mla"], i - 3)
                lo = 0 if i < TT else 256
                for k in range(KT):
                    last = mm(bank(i % 4, lo, 416), hT[:, k, i * P:i * P + P], w[:, k, lo:416], k == 0, k == KT - 1)
                last.then_inc(s["pe_mla"], 1)
            pe.wait_ge(s["dve_mn"], 2 + TT + AT)
            for g in range(7):
                src = mla_tok[:, :, (g // 2) * P:(g // 2) * P + P] if g < 4 else mla_tok[:, :, 256:384]
                t0 = 4 * (g % 2 if g < 4 else g - 4)
                for i in range(4 if g < 6 else CT):
                    last = pe.transpose(bank(g, i * P, i * P + P), src[:, t0 + i, :], ident[:, :])
                last.then_inc(s["pe_mT"], 1)
            pe.wait_ge(s["act_mT"], 7)
            pe.wait_ge(s["in_uq"], 32)
            pe.wait_ge(s["dve_ada2"], 3)
            for i in range(AT):
                if i < TT:
                    if i >= 4:
                        pe.wait_ge(s["dve_uq"], i - 3)
                    for k in range(2):
                        last = mm(bank(i % 4, 0, 384), cqT[:, k, i * P:i * P + P], w_uq[:, k, :], k == 0, k == 1)
                    last.then_inc(s["pe_uq"], 1)
                if i >= 4:
                    pe.wait_ge(s["act_ukv"], 2 * (i - 3))
                mm(bank(4 + i % 4), ckvT[:, i * P:i * P + P], w_ukv, True, True).then_inc(s["pe_ukv"], 1)
            pe.wait_ge(s["dve_rope"], HEADS)
            for g in range(8):
                if g >= 4:
                    pe.wait_ge(s["dve_qT"], g - 3)
                for i in range(4):
                    last = pe.transpose(psum[0:QK, (g % 4) * 512 + i * P:(g % 4) * 512 + i * P + P],
                                        q_tok[:, 4 * (g % 2) + i, g // 2, :], ident[:, :])
                last.then_inc(s["pe_qT"], 1)
            pe.wait_ge(s["act_ukv"], 2 * AT)
            for g in range(12):
                if g >= 4:
                    pe.wait_ge(s["act_kT"], g - 3)
                for i in range(4 if g % 3 < 2 else CT):
                    last = pe.transpose(psum[0:QK, (4 + g % 4) * 512 + i * P:(4 + g % 4) * 512 + i * P + P],
                                        k_tok[:, 4 * (g % 3) + i, g // 3, :], ident[:, :])
                last.then_inc(s["pe_kT"], 1)
            pe.wait_ge(s["act_kT"], 12)
            pe.wait_ge(s["dve_qT"], 8)
            with pe.Fori(0, HEADS) as h:
                def scores(q):
                    pe.wait_ge(s["pool_q"], h * TT + q + 1)
                    if q >= 2:
                        pe.wait_ge(s["act_p"], h * TT + q - 1)
                    base = (q % 2) * 1536
                    for lo, hi in ((0, 512), (512, 1024), (1024, 1280)):
                        last = mm(psum[:, base + lo:base + hi], q_now[:, q % 2, :], kT[:, bass.ds(h, 1), lo:hi], True, True)
                    last.then_inc(s["pe_qk"], 1)

                def values(q):
                    pe.wait_ge(s["dve_pt"], h * 2 * TT + 2 * q + 2)
                    pe.wait_ge(s["act_pt"], h * TT + q + 1)
                    for i in range(AT):
                        last = mm(bank(7, 0, VD), probT[:, i, :],
                                  v_tok[:, i, bass.ds(h * VD, VD)], i == 0, i == AT - 1)
                    last.then_inc(s["pe_pv"], 1)

                scores(0)
                for q in range(TT):
                    if q + 1 < TT:
                        scores(q + 1)
                    if q >= 1:
                        values(q - 1)
                    pe.wait_ge(s["act_p"], h * TT + q + 1)
                    for r in range(3):
                        if r == 0 and q >= 1:
                            pe.wait_ge(s["dve_pt"], h * 2 * TT + 2 * q)
                        elif r == 1 and q >= 1:
                            pe.wait_ge(s["dve_o"], h * TT + q)
                        elif r == 2:
                            pe.wait_ge(s["dve_pt"], h * 2 * TT + 2 * q + 1)
                        for i in range(4 * r, min(4 * r + 4, AT)):
                            last = pe.transpose(bank(6 + r % 2, (i % 4) * P, (i % 4) * P + P),
                                                prob[:, q % 2, i * P:i * P + P], ident[:, :])
                        last.then_inc(s["pe_t"], 1)
                values(TT - 1)
                pe.wait_ge(s["dve_o"], h * TT + TT)
            for g in range(4):
                for i in range(4):
                    last = pe.transpose(bank(g, i * P, i * P + P), oa_tok[:, 4 * (g % 2) + i, (g // 2) * P:(g // 2) * P + P],
                                        ident[:, :])
                last.then_inc(s["pe_oaT"], 1)
            ada_column(3)
            pe.wait_ge(s["act_oaT"], 4)
            pe.wait_ge(s["dve_ada2"], 4)
            arrived(pe, K_NQK)
            w = slot(K_NQK, KT, 512)
            for g in range(10):
                if g >= 4:
                    pe.wait_ge(s["act_nqk"], g - 3)
                    pe.wait_ge(s["dve_nqk"], g - 3)
                _, lo, n = na_group(g)
                col = (g % 2) * P + (0 if g < 4 else BW)
                for k in range(KT):
                    last = mm(bank(g % 4, 0, n), w[:, k, col:col + P], hT[:, k, lo:lo + n], k == 0, k == KT - 1)
                last.then_inc(s["pe_nqk"], 1)
            arrived(pe, K_NV)
            w = slot(K_NV, KT, BW)
            for i in range(AT):
                if i >= 4:
                    pe.wait_ge(s["act_nv"], i - 3)
                for k in range(KT):
                    last = mm(bank(4 + i % 4, 0, BW), hT[:, k, i * P:i * P + P], w[:, k, :], k == 0, k == KT - 1)
                last.then_inc(s["pe_nv"], 1)
            pe.wait_ge(s["in_rpb"], 16 * 8)
            pe.wait_ge(s["act_nqk"], 10)
            pe.wait_ge(s["dve_nqk"], 10)
            pe.wait_ge(s["act_nv"], AT)
            for kc in range(64):
                if kc % 32 == 0:
                    arrived(pe, K_REL[kc // 32])
                table = slot(K_REL[kc // 32], 32, P, rows=64)
                last = mm(bank(kc // 8, (kc % 8) * 56, (kc % 8) * 56 + 56), table[:, kc % 32, :],
                          rpb_t.rearrange("p h r -> p (h r)"), True, True)
                if kc % 8 == 7:
                    last.then_inc(s["pe_bb"], 1)
            pe.wait_ge(s["dve_bb"], 8)
            pe.wait_ge(s["pool_npad"], 2)
            with pe.Fori(0, HEADS) as h:
                def scores(q):
                    first, n, _ = NA_TILES[q]
                    pe.wait_ge(s["pool_nq"], h * TT + q + 1)
                    if q >= 2:
                        pe.wait_ge(s["dve_nmx"], h * TT + q - 1)
                    base = (q % 2) * 1024
                    for lo, hi, key in [(0, 512, first * P)] + ([(512, 640, first * P + 512)] if n == 640 else []) + \
                            [(n, n + C, T)]:
                        last = mm(psum[:, base + lo:base + hi], nq_now[:, q % 2, :],
                                  nkT[:, bass.ds(h, 1), key:key + hi - lo], True, True)
                    last.then_inc(s["pe_nqk2"], 1)

                def values(q):
                    first, n, _ = NA_TILES[q]
                    pe.wait_ge(s["act_npt"], h * 2 * TT + 2 * q + 2)
                    if q >= 2:
                        pe.wait_ge(s["dve_no"], h * TT + q - 1)
                    tiles = [first + i for i in range(n // P)] + [TT, TT + 1]
                    for i, t in enumerate(tiles):
                        last = mm(bank(6 + q % 2, 0, VD), nprobT[:, i, :],
                                  nv_tok[:, t, bass.ds(h * VD, VD)], i == 0, i == len(tiles) - 1)
                    last.then_inc(s["pe_npv"], 1)

                scores(0)
                for q in range(TT):
                    if q + 1 < TT:
                        scores(q + 1)
                    if q >= 1:
                        values(q - 1)
                    n = (NA_TILES[q][1] + C) // P
                    pe.wait_ge(s["act_np"], h * TT + q + 1)
                    if q >= 1:
                        pe.wait_ge(s["act_npt"], h * 2 * TT + 2 * q)
                    for r in range(2):
                        for i in range(4 * r, min(4 * r + 4, n)):
                            last = pe.transpose(bank(4 + r, (i % 4) * P, (i % 4) * P + P),
                                                nprob[:, q % 2, i * P:i * P + P], ident[:, :])
                        last.then_inc(s["pe_nt"], 1)
                values(TT - 1)
                pe.wait_ge(s["dve_no"], h * TT + TT)
            for g in range(4):
                for i in range(4):
                    last = pe.transpose(bank(g, i * P, i * P + P), od_tok[:, 4 * (g % 2) + i, (g // 2) * P:(g // 2) * P + P],
                                        ident[:, :])
                last.then_inc(s["pe_odT"], 1)
            pe.wait_ge(s["dve_cond"], 1)
            for n in range(4):
                arrived(pe, K_RES[n])
                w = slot(K_RES[n], KT, 512)
                for t in range(KT):
                    last = mm(bank(4 + n), cond_rows[:, t, :], w[:, t, :], t == 0, t == KT - 1)
                last.then_inc(s["pe_res"], 1)
            pe.wait_ge(s["dve_res"], 4)
            pe.wait_ge(s["act_odT"], 4)
            with pe.Fori(0, KT // 2) as i:
                for m in range(16):
                    slot_n, n, half = m // 8, (m // 2) % 4, m % 2
                    if m % 8 == 0:
                        pe.wait_ge(in_gate[slot_n], i * 80 + 80)
                    for name in ("act_gate", "dve_gate"):
                        pe.wait_ge(s[name], i * 16 + m + FREE - 3)
                    for k in range(KT):
                        last = mm(bank(m % 4), gate_slots[slot_n][:, k, n, :], hT[:, k, half * 512:half * 512 + 512],
                                  k == 0, k == KT - 1)
                    last.then_inc(s["pe_gg"], 1)
                    for k in range(2):
                        last = mm(bank(4 + m % 4), wb[:, slot_n, 2 * n + k, :], oT[n][:, k, half * 512:half * 512 + 512],
                                  k == 0, k == 1)
                    last.then_inc(s["pe_gate"], 1)
            pe.wait_ge(s["dve_gate"], 64 + FREE)
            for m in range(16):
                half, t = m // TT, m % TT
                if t == 0:
                    pe.wait_ge(s["in_w_out"], 16 * half + 16)
                if m >= 8:
                    pe.wait_ge(s["dve_x1"], m - 7)
                for k in range(KT):
                    last = mm(bank(m % 8), merged[:, k, t * P:t * P + P], w_out_slots[half][:, k, :], k == 0, k == KT - 1)
                last.then_inc(s["pe_out"], 1)
            pe.wait_ge(s["dve_x1"], 16)
            for n in range(2 * KT):
                g, kt = n // KT, n % KT
                pe.wait_ge(s["dve_x1n"], 4 * g + 4)
                if n >= 4:
                    pe.wait_ge(s["act_hT2"], n - 3)
                for i in range(4):
                    last = pe.transpose(bank(n % 4, i * P, i * P + P), x1n[:, 4 * g + i, kt * P:kt * P + P], ident[:, :])
                last.then_inc(s["pe_hT2"], 1)
            pe.wait_ge(s["act_hT2"], 2 * KT)
            pe.wait_ge(s["in_router"], 64)
            for t in range(TT):
                for k in range(KT):
                    last = mm(bank(4, 20 * t, 20 * t + 20), h2T[:, k, t * P:t * P + P], wr[:, k, :], k == 0, k == KT - 1)
            last.then_inc(s["pe_route"], 1)
            pe.wait_ge(s["in_tab"], 16)
            pe.wait_ge(s["pool_ones"], 1)
            pe.wait_ge(s["dve_both"], 1)
            both = both_of.rearrange("p t e -> p (t e)")
            mm(bank(5, 0, P), before, both, True, True)
            mm(bank(5, P, 2 * P), all_ones, both, True, True).then_inc(s["pe_count"], 1)
            pe.wait_ge(s["dve_hot"], 2)
            for n in range(2):
                for t in range(TT):
                    last = mm(bank(6, 0, 64), row_hot[:, n, t, :], tile_hot[:, n, t, :, :].rearrange("p a b -> p (a b)"),
                              n == 0 and t == 0, n == 1 and t == TT - 1)
            last.then_inc(s["pe_table"], 1)
            pe.wait_ge(s["dve_table"], 1)
            pairs = pe.value_load(pair_count, min_val=8, max_val=16)

            def rows(m):
                for kt in range(KT):
                    last = pe.transpose(bank(2 + kt // 4, (kt % 4) * P, (kt % 4) * P + P), slot_x[:, m, kt * P:kt * P + P],
                                        ident[:, :])
                last.then_inc(s["pe_x"], 1)

            pe.wait_ge(in_slots[0], 16)
            rows(0)
            with pe.Fori(0, pairs) as i:
                for m in range(2):
                    pe.wait_ge(in_expert[m], i * 32 + 32)
                    pe.wait_ge(s["act_h"], i * 8 + 4 * m + 4)
                    pe.wait_ge(s["dve_h"], i * 8 + 4 * m + 4)
                    pe.wait_ge(s["dve_mul"], i * 2 + m - 1 + FREE)
                    for k in range(KT):
                        last = mm(bank(m), slot_hT[:, m, k, :], expert_slots[:, m, k, :], k == 0, k == KT - 1)
                    last.then_inc(s["pe_au"], 1)
                    pe.wait_ge(in_slots[1 - m], i * 16 + 16 + 16 * m)
                    rows(1 - m)
                    pe.wait_ge(s["dve_mul"], i * 2 + m + 1 + FREE)
                    pe.wait_ge(s["dve_actT"], i * 2 + m - 1 + FREE)
                    for f in range(2):
                        last = pe.transpose(bank(4 + m, f * P, f * P + P), act_tok[:, m, f * P:f * P + P], ident[:, :])
                    last.then_inc(s["pe_actT"], 1)
                    pe.wait_ge(in_down[m], i * 16 + 16)
                    pe.wait_ge(s["dve_actT"], i * 2 + m + 1 + FREE)
                    for half in range(2):
                        pe.wait_ge(s["dve_y"], i * 4 + 2 * m + half - 1 + FREE)
                        for f in range(2):
                            last = mm(bank(6 + half), actT[:, m, f * P:f * P + P], w_down[:, m, f, half * 512:half * 512 + 512],
                                      f == 0, f == 1)
                        last.then_inc(s["pe_down"], 1)


def _tables():
    import numpy as np
    P, T, pi = 128, 1024, np.pi
    f32 = np.float32
    tb = {}
    t = np.linspace(0.0, 1.0, T, dtype=f32)
    bands = np.linspace(1e-4, 15, 16, dtype=f32)
    ang = (f32(2.0 * pi / T) * np.arange(T, dtype=f32)[:, None] * bands).astype(f32)
    tb["features"] = np.concatenate([t[:, None], np.cos(ang), -np.sin(ang)], axis=1).T
    dl = np.linspace(np.log(1e-2) / 1.5, np.log(1e-2) / 0.3, 256)
    win = np.exp(-np.linspace(0, 1, T)[:, None] * np.abs(dl))
    back = win.copy()
    back[0] = 0.0
    tb["window"] = np.stack([win, back], 1).reshape(8, P, 2, 256).transpose(1, 0, 2, 3)
    k = np.concatenate([np.arange(0, T, 2), np.arange(1, T, 2)])
    a = pi * (((2 * k[None, :] + 1) * np.arange(T)[:, None]) % (4 * T)) / (2 * T)
    g = np.stack([np.cos(a), -np.sin(a)], 1)
    tb["filter_basis"] = g.reshape(8, P, 2, 8, P).transpose(1, 3, 0, 2, 4)
    th = pi * (((2 * k[None, :] + 1) * (2 * np.arange(512)[:, None] + 1)) % (8 * T)) / (4 * T)
    cas = np.stack([np.cos(th) + np.sin(th), np.cos(th) - np.sin(th)], 1)
    tb["forward_basis"] = cas.reshape(4, P, 2, 8, P).transpose(1, 3, 0, 2, 4)
    tb["inverse_basis"] = (cas / (2 * T)).transpose(2, 1, 0).reshape(8, P, 2, 512).transpose(1, 0, 2, 3)
    b = 2 * pi * ((np.arange(T)[:, None] * np.arange(512)[None, :]) % T) / T
    tb["token_basis"] = np.stack([np.cos(b), -np.sin(b)], 0).reshape(2, 8, P, 512).transpose(2, 0, 1, 3)
    c = 2 * pi * ((np.arange(64)[:, None] * np.arange(64)[None, :]) % 64) / 64
    chan = np.zeros((P, 2, P))
    for n in range(2):
        chan[n * 64:n * 64 + 64, 0, n * 64:n * 64 + 64] = np.cos(c) / 256
        chan[n * 64:n * 64 + 64, 1, n * 64:n * 64 + 64] = np.sin(c) / 256
    tok = np.arange(T)
    inv = (f32(10000.0) ** (-np.arange(8, dtype=f32) / f32(8))).astype(f32)
    ra = np.concatenate([(tok // 64).astype(f32)[:, None] * inv, (tok % 64).astype(f32)[:, None] * inv], 1)
    rope = np.stack([np.cos(ra), np.sin(ra)], 1).reshape(8, P, 2, 16).transpose(1, 2, 0, 3)
    rows = np.full((P, 10, 64), -1e30)
    rows[:64, 0:8] = 0
    rows[64:, 1:9] = 0
    qc, kc = np.arange(64)[:, None], np.arange(64)[None, :]
    start = np.clip(qc - 8, 0, 48)
    ok = (kc >= start) & (kc < start + 16)
    sel = np.zeros((2, 32, 64, 2, 64))
    for r in range(2):
        for q in range(64):
            for kk in range(64):
                if ok[q, kk]:
                    sel[r, kk - q + 15, kk, r, q] = 1
                else:
                    sel[r, 31, kk, r, q] = 1
    tb["relative_columns"] = sel.reshape(64, 64 * P)
    alt = (1 - 2 * (np.arange(P) % 2))[:, None]
    tb["pack"] = np.concatenate([x.reshape(P, -1) for x in (rope, rows, chan, alt)], 1)
    col = np.tile(np.arange(160), (P, 1))
    tb["routing_tab"] = np.concatenate([col, np.arange(T).reshape(8, P).T, np.triu(np.ones((P, P)), 1)], 1)
    return {n: np.ascontiguousarray(v, dtype=f32) for n, v in tb.items()}


_INS = ['x', 'c', 'ctx', 'c_ctx', 'ada_w', 'ada_b', 'norm1_g', 'norm2_g', 'w_in', 'mla_q_norm', 'mla_w_uq',
        'mla_kv_norm', 'mla_w_ukv', 'hy_short_w', 'hy_w1', 'hy_b1', 'hy_freq1', 'hy_w2', 'hy_b2', 'hy_freq2',
        'hy_w3', 'hy_bias', 'na_rpb', 'w_branch', 'w_out', 'moe_w_group', 'moe_b_group', 'moe_w_expert',
        'moe_b_expert', 'moe_w_gate', 'moe_w_up', 'moe_w_down', 'final_norm_g']
_OUTS = [((1, 1024, 1024), 'float32')]


def kernel(**inputs):
    import numpy as _np
    import concourse.bacc as _bacc
    from concourse import mybir as _mybir
    from concourse.bass_utils import run_bass_kernel_spmd as _run

    nc = _bacc.Bacc("TRN2", target_bir_lowering=False, num_devices=1)
    arrays, args = {}, {}
    for name, a in [(n, inputs[n]) for n in _INS] + list(_tables().items()):
        a = _np.ascontiguousarray(a)
        arrays[f"in_{name}_dram"] = a
        args[name] = nc.dram_tensor(f"in_{name}_dram", a.shape, _mybir.dt.from_np(a.dtype), kind="ExternalInput").ap()
    for i, (shape, dtype) in enumerate(_OUTS):
        dt = _mybir.dt.from_np(_np.dtype(dtype))
        args["out"] = nc.dram_tensor(f"out_{i}_dram", shape, dt, kind="ExternalOutput").ap()
    hybrid_flow_backbone(nc, **args)
    r = _run(nc, [arrays], core_ids=[0])
    return r.results[0]["out_0_dram"]
```

```python
import concourse.bass as bass
from concourse import mybir
from contextlib import ExitStack

F32 = mybir.dt.float32
I32 = mybir.dt.int32
F32R = mybir.dt.float32r
ALU = mybir.AluOpType
ACT = mybir.ActivationFunctionType
AX = mybir.AxisListType

P = 128
D = 1024
KT = D // P
T = 1024
TT = T // P
C = 256
CT = C // P
AT = TT + CT
BW = 256
HEADS = 4
NOPE, ROPE, VD = 64, 32, 64
QK = NOPE + ROPE
KEYS = T + C
MLA_SCALE = float(QK) ** -0.5
NA_SCALE = 64.0 ** -0.5
EPS = 1e-6
MASK = -1e30
PI = 3.14159265
TURN = 6.283185307179586
ROUND = 1.5 * 2.0 ** 23
EXPERTS, HID = 16, 256
CQ, KR, HY, FN, NQ, NV, GATE, IN_END = 0, 384, 416, 1184, 1440, 1952, 2208, 6304
MAX_TILES = 32
UPPER = -(1 << 12)
FREE = 6
SLOT = 4096
V_ADAB, V_N1, V_N2, V_QN, V_KVN, V_TAP, V_HB, V_B1, V_F1, V_B2, V_F2, V_END = 0, 48, 56, 64, 66, 67, 85, 89, 90, 91, 92, 93


class Steps:

    def __init__(self, eng, sem):
        self.eng, self.sem, self.base, self.n = eng, sem, 0, 0

    def __call__(self, ins):
        self.mark(ins)
        self.eng.wait_ge(self.sem, self.base + self.n)

    def mark(self, ins):
        ins.then_inc(self.sem, 1)
        self.n += 1

    def sync(self):
        self.eng.wait_ge(self.sem, self.base + self.n)

    def enter(self, i, per):
        self.before = self.base + self.n
        self.base, self.n = self.before + i * per, 0

    def leave(self, rounds, per):
        assert self.n == per, (self.n, per)
        self.base, self.n = self.before + rounds * per, 0


def hybrid_flow_backbone(nc, out, x, c, ctx, c_ctx, ada_w, ada_b, norm1_g, norm2_g, w_in, mla_q_norm, mla_w_uq,
                         mla_kv_norm, mla_w_ukv, hy_short_w, hy_w1, hy_b1, hy_freq1, hy_w2, hy_b2, hy_freq2,
                         hy_w3, hy_bias, na_rpb, w_branch, w_out, moe_w_group, moe_b_group, moe_w_expert,
                         moe_b_expert, moe_w_gate, moe_w_up, moe_w_down, final_norm_g,
                         features, window, filter_basis, forward_basis, inverse_basis, token_basis,
                         relative_columns, pack, routing_tab):
    stack = ExitStack()
    with stack:
        def sb(name, shape, dt=F32):
            return stack.enter_context(nc.sbuf_tensor(name, shape, dt))

        def sem(name):
            return stack.enter_context(nc.semaphore(name))

        def cut(t, at, *shape, rows=P):
            size = 1
            for s in shape:
                size *= s
            v = t[0:rows, at:at + size]
            if len(shape) == 1:
                return v
            names = "abcde"[:len(shape)]
            return v.rearrange(f"p ({' '.join(names)}) -> p {' '.join(names)}", **dict(zip(names, shape)))

        sizes = {"normed": 10240, "ring": 3 * SLOT, "arena": 20700}
        with ExitStack() as first:
            normed, ring, arena = (first.enter_context(nc.sbuf_tensor(n, [P, w], F32)) for n, w in sizes.items())
        normed_parts, ring_parts, arena_parts = (sb(f"{n}_parts", [P, w], F32R) for n, w in sizes.items())
        branches = sb("branches", [P, 8192])
        pk = sb("pk", [P, 1153])
        ident = sb("ident", [P, P])
        ones = sb("ones", [P, 2])
        vec = sb("vec", [P, V_END])
        small = sb("small", [P, 256])
        psum = stack.enter_context(nc.psum_tensor("psum", [P, 4096], F32))

        def bank(b, lo=0, hi=512):
            return psum[:, b * 512 + lo:b * 512 + hi]

        def slot(n, *shape, rows=P):
            return cut(ring, (n % 3) * SLOT, *shape, rows=rows)

        rope_t = cut(pk, 0, 2, TT, 16)
        row_mask = cut(pk, 256, 10, 64)
        chan_basis = cut(pk, 896, 2 * P)
        alternate = pk[:, 1152:1153]

        scale1 = cut(small, 0, 2, KT)
        shift1 = cut(small, 16, 2, KT)
        scale2 = cut(small, 32, KT)
        shift2 = cut(small, 40, KT)
        cond = cut(small, 48, KT, 2)
        cond_raw = cut(small, 64, 2, KT)
        ssq = cut(small, 80, 32)
        rstd = cut(small, 112, 32)
        filter_norm = cut(small, 144, 4)
        neg_max = cut(small, 148, 8)
        gate_col = cut(small, 232, 4 * 4)
        row_sum = cut(small, 156, 8)
        row_inv = cut(small, 164, 8)

        window_sb = cut(normed, 0, TT, 2, BW)
        feat = cut(normed, 4096, T, rows=33)
        arg = cut(normed, 5120, T, rows=64)
        turn = cut(normed, 6144, T, rows=64)
        hid = cut(normed, 7168, T, rows=64)
        w3_sb = cut(normed, 8192, T, rows=64)
        w1_sb = cut(normed, 9216, 64, rows=33)
        w2_sb = cut(normed, 9280, 64, rows=64)
        staged = cut(normed, 9344, P)
        ada_acc = cut(normed, 5120, 4, 2, 512)
        ada_acc2 = cut(arena, 19472, 2, 512)
        spec = cut(arena, 0, 2, KT, 512)
        fsum = cut(arena, 8192, TT, 512)
        fdif = cut(arena, 12288, TT, 512)
        x_ctx = cut(arena, 16400, CT, D)
        fir_f = cut(arena, 18448, 512)
        fir_b = cut(arena, 18960, 512)
        sq_acc = cut(arena, 19472, 512)
        sq_tmp = cut(arena, 19984, 512)
        x_sb = cut(branches, 0, TT, D)
        hT = cut(normed, 0, KT, KEYS)
        conv = cut(arena, 8192, 6, T)
        raw = cut(arena, 14336, 2, T + 2)
        folded_t = cut(arena, 16400, 4, 2, BW)
        prod_r = cut(arena, 14336, 2, BW)
        prod_i = cut(arena, 14848, 2, BW)
        mix = cut(arena, 15360, T)
        conv_spec = cut(branches, 4096, KT, 2, BW)
        folded = cut(branches, 0, 2, 2, 512)
        halves = cut(branches, 2048, 2, 2, 512)
        oT = [cut(branches, n * 2048, 2, T) for n in range(4)]
        fnT = cut(arena, 0, 2, T)
        chan_mixed = cut(arena, 2048, TT, 2, 2, P)
        sine_part = cut(arena, 6144, 2, 512)

        mla_tok = cut(arena, 0, AT, 416)
        cqT = cut(arena, 4160, 2, T)
        ckvT = cut(arena, 6208, KEYS)
        q_tok = cut(arena, 7488, TT, HEADS, QK)
        k_tok = cut(arena, 10560, AT, HEADS, QK)
        v_tok = cut(arena, 14400, AT, HEADS * VD)
        qT = cut(arena, 0, HEADS, T, rows=QK)
        kT = cut(arena, 4160, HEADS, KEYS, rows=QK)
        prob = cut(arena, 10560, 2, KEYS)
        probT = cut(arena, 13120, AT, P)
        w_uq = cut(arena, 16960, 2, HEADS * QK)
        w_ukv = cut(arena, 17728, HEADS * (NOPE + VD))
        q_now = cut(arena, 18240, 2, P, rows=QK)
        rot = [cut(arena, 18496 + 512 * n, TT, HEADS, 16) for n in range(4)]
        oa_tok = cut(branches, 0, TT, BW)
        nqT = cut(arena, 0, HEADS, T, rows=64)
        nkT = cut(arena, 4096, HEADS, KEYS)
        nv_tok = cut(arena, 9216, AT, BW)
        rel_bias = cut(arena, 11776, HEADS, 14 * 64)
        inner_bias = cut(arena, 15360, 640)
        nprob = cut(arena, 16000, 2, 896)
        nprobT = cut(arena, 17792, 7, P)
        nq_now = cut(arena, 18688, 2, P)
        rpb_t = cut(small, 176, HEADS, 14, rows=64)
        od_tok = cut(branches, 6144, TT, BW)
        NA_TILES = [(0, 512, 384), (0, 512, 256)] + [(q - 2, 640, None) for q in range(2, 6)] + \
                   [(4, 512, 128), (4, 512, 0)]
        hT_upper = cut(normed_parts, 0, KT, KEYS)
        hT_rest = cut(ring_parts, 0, KT, T)
        w_gate = cut(ring, 2 * SLOT, 4, KT, P)
        w_upper = cut(ring_parts, 2 * SLOT, 4, KT, P)
        w_rest = cut(arena_parts, 10240, 2, KT, P)
        w_split = cut(arena, 14848, 4, P)
        hT_split = cut(arena, 18944, 2, 1, 256)
        w_out_first = cut(arena, 12800, KT, 256)
        w_out_last = cut(ring, 0, KT, 768)
        def out_bank(m, n):
            return bank(m % 8 if m < 2 * TT else m % 4, 0, n)

        OUT_PASSES = [(0, w_out_first), (256, w_out_last[:, :, 0:256]), (512, w_out_last[:, :, 256:768])]
        merged = cut(arena, 0, KT, T)
        gate_cols = cut(arena, 0, 4 * 4, P)
        wb = cut(arena, 8192, 2, 8, P)
        gate_sb = cut(arena, 15360, 2, 512)
        gated = cut(arena, 12288, 512)
        final_gain = cut(arena, 16384, D)
        res_gate1 = cut(arena, 17408, D)
        res_gate2 = cut(arena, 18432, D)
        x1 = cut(normed, 0, TT, D)
        x1n = cut(branches, 0, TT, D)
        h2T = cut(arena, 8192, 2, KT, P)
        logits_t = cut(arena, 15360, T, rows=20)
        square2 = cut(normed, 8192, D)
        wr = cut(arena, 19456, KT, 20)
        wr_bias = cut(arena, 19616, 20)
        logits = cut(arena, 19640, TT, 20)
        route = cut(arena, 19800, TT, EXPERTS)
        pick = cut(arena, 19928, TT, 16)
        group_hot, expert_hot, second_hot, expert_logit = (cut(arena, 20056 + 32 * n, TT, 4) for n in range(4))
        rc = [cut(arena, 20184 + 8 * n, TT) for n in range(8)]
        group_exp = cut(arena, 20248, TT, 4)
        first_of, second_of, both_of, slot_of, tile_off, masked = (cut(arena, 12288 + 128 * n, TT, EXPERTS) for n in range(6))
        count, tiles, upto, base_of, one_row = (cut(arena, 13056 + 16 * n, EXPERTS) for n in range(5))
        slots_f, slot_tile, slot_row = (cut(arena, 13136 + 16 * n, 2, TT) for n in range(3))
        ended = cut(arena, 13200, 34, EXPERTS)
        ended_sum = cut(arena, 13744, 34)
        weight_t = cut(arena, 13778, 32)
        tab = cut(arena, 13810, 296)
        column_no, token_no, before = tab[:, 0:128], tab[:, 160:168], tab[:, 168:296]
        all_ones = cut(arena, 14236, P)
        place = cut(arena, 14364, 4)
        pairs_f = cut(arena, 14234, 2)
        row_hot = cut(arena, 0, 2, TT, P)
        tile_hot = cut(arena, 2048, 2, TT, 2, 32)
        ints = sb("ints", [P, 96], I32)
        token_of = ints[:, 0:34]
        expert_of = ints[:, 34:68]
        pair_count = ints[0:1, 68:69]
        slots_i = ints[:, 69:85].rearrange("p (c t) -> p c t", c=2)
        token_now = ints[:, 85:87]
        w_down = cut(arena, 8192, 2, 2, D)
        slot_x = cut(branches, 0, 2, D)
        slot_y = cut(branches, 2048, 2, D)
        slot_hT = cut(branches, 4096, 2, KT, P)
        act_tok = cut(branches, 6144, 2, HID)
        actT = cut(branches, 6656, 2, HID)
        silu = cut(branches, 7168, 2, HID)
        parts = cut(arena, 0, 4, 2, D)
        rows_dram = nc.dram_tensor("normed_rows", [T, D], F32, kind="Internal").ap()
        slots_dram = nc.dram_tensor("expert_rows", [MAX_TILES * P, D], F32, kind="Internal").ap()

        s = {n: sem(n) for n in (
            "in_x", "pool_const", "pool_pad", "dve_chain", "act_chain", "dve_zero",
            "pe_vec", "dve_vec", "act_cond", "pe_sin", "dve_arg", "act_sin", "pe_filt", "dve_filt", "pool_sq",
            "pe_spec", "act_even", "dve_filter", "pe_fnorm", "pe_ada", "act_ssq", "act_xn", "pe_xT", "act_hT",
            "pe_hy", "act_hy", "dve_conv", "dve_fold", "pe_fold", "act_fold", "pe_fwd", "dve_spec",
            "pe_inv", "act_inv", "dve_z", "pe_fn", "act_fn", "pe_chan", "act_chan", "pe_tok", "act_tok", "dve_oc",
            "in_uq", "pe_mla", "dve_mla", "act_msq", "act_mrt", "dve_mn", "pe_mT", "act_mT", "pe_uq", "dve_uq", "pe_ukv",
            "act_ukv", "dve_rope", "pe_qT", "dve_qT", "pe_kT", "act_kT", "pool_q", "pe_qk", "dve_mx", "act_p", "pe_t", "dve_pt",
            "act_pt", "pe_pv", "dve_o", "pe_oaT", "act_oaT", "pe_nqk", "act_nqk", "dve_nqk", "pe_nv", "act_nv", "in_rpb", "pool_rpb",
            "pe_bb", "dve_bb", "pool_nq", "pe_nqk2", "dve_nmx", "act_np", "pe_nt", "act_npt", "pe_npv", "dve_no", "pe_odT", "act_odT",
            "dve_acc", "dve_ada", "pe_res", "dve_res", "in_res", "pe_gg", "pe_gate", "act_gate", "dve_gate",
            "in_w_out", "in_x1", "pe_out", "dve_x1", "act_ssq2", "act_rt2", "dve_ms2", "dve_x1n", "pe_hT2", "act_hT2",
            "in_router", "pe_route", "act_route", "dve_route", "pe_au", "act_silu", "dve_moe",
            "in_tab", "pool_idx", "pe_count", "dve_hot", "pe_table", "dve_table", "pe_x", "act_h", "dve_h",
            "dve_mul", "pe_actT", "dve_actT", "pe_down", "dve_y",
            "dve_fin", "dve_split", "pool_split", "dve_logit", "pe_back", "in_window",
            "stored", "in_vec", "in_feat", "dve_mod")}
        in_gate = [sem(f"in_gate{n}") for n in range(4)]
        rows_stored = sem("rows_stored")
        in_slots = [sem(f"in_slots{n}") for n in range(2)]
        in_down = [sem(f"in_down{n}") for n in range(2)]
        y_stored = [sem(f"y_stored{n}") for n in range(2)]
        in_parts = [sem(f"in_parts{n}") for n in range(2)] + in_slots
        in_expert = [sem(f"in_expert{n}") for n in range(2)]
        in_ring = [sem(f"in_ring{n}") for n in range(3)]
        block = stack.enter_context(nc.Block())

        w_in_k = w_in[0].rearrange("(t p) n -> p t n", p=P)
        ada_k = ada_w[0].rearrange("(p t) n -> p t n", t=KT)

        chunks = []

        def chunk(src, shape, done, value):
            n = len(chunks)
            chunks.append((src, slot(n, *shape), done, value))
            return n

        K_SPEC, K_ADA = [], []

        def ada_chunk(n):
            K_ADA.append(chunk(ada_k[:, :, n * 512:n * 512 + 512], (KT, 512), "dve_acc", len(K_ADA) + 1))

        for n in range(4):
            K_SPEC.append(chunk(filter_basis[:, n], (TT, 2, P), "pe_spec", 2 * n + 2))
            ada_chunk(n)
        K_HY = [chunk(w_in_k[:, :, HY:HY + 512], (KT, 512), "pe_hy", 8),
                chunk(w_in_k[:, :, HY + 512:FN], (KT, 256), "pe_hy", 12)]
        K_CONV = []
        for n in range(2):
            K_CONV.append((
                [chunk(forward_basis[:, 4 * m:4 * m + 4], (4, 4, 2, P), "pe_fwd", 8 * n + 4 * m + 4) for m in range(2)],
                [chunk(inverse_basis[:, 4 * m:4 * m + 4], (4, 2, 512), "pe_inv", 3 * n + 2 * m + 1) for m in range(2)]))
        K_FN = chunk(w_in_k[:, :, FN:NQ], (KT, BW), "pe_fn", 4)
        ada_chunk(6)
        ada_chunk(7)
        K_TOK = [chunk(token_basis[:, 0], (TT, 512), "pe_tok", 1)]
        ada_chunk(8)
        K_TOK.append(chunk(token_basis[:, 1], (TT, 512), "pe_tok", 2))
        ada_chunk(9)
        K_MLA = chunk(w_in_k[:, :, CQ:HY], (KT, 416), "pe_mla", AT)
        ada_chunk(4)
        ada_chunk(5)
        K_NQK = chunk(w_in_k[:, :, NQ:NV], (KT, 512), "pe_nqk", 10)
        ada_chunk(10)
        K_NV = chunk(w_in_k[:, :, NV:GATE], (KT, BW), "pe_nv", AT)
        ada_chunk(11)
        K_REL = []
        for n in range(2):
            K_REL.append(len(chunks))
            chunks.append((relative_columns[:, n * SLOT:n * SLOT + SLOT], slot(len(chunks), 32, P, rows=64).rearrange(
                "p a b -> p (a b)"), "pe_bb", 4 * n + 4))
        expert_slots = cut(ring, 0, 2, KT, 2 * HID)
        def arrived(eng, n):
            eng.wait_ge(in_ring[n % 3], 16 * (n // 3 + 1))

        def na_group(g):
            block_of = g // 2
            if block_of < 2:
                return nqT, block_of * 512, 512
            return nkT, (block_of - 2) * 512, 512 if block_of < 4 else C
        @block.sync
        def _(sp):
            def load(dst, src, signal):
                sp.dma_start(dst, src).then_inc(s[signal], 16)

            sp.wait_ge(s["dve_zero"], 1)
            row = 0
            for src, n in ((ada_b, 48), (norm1_g, 8), (norm2_g, 8), (mla_q_norm, 2), (mla_kv_norm, 1),
                           (hy_short_w, 18), (hy_bias, 4)):
                flat = src[0] if len(src.shape) == 2 else src[0].rearrange("a n -> (a n)")
                load(staged[row:row + n, :], flat.rearrange("(r q) -> r q", q=P), "in_vec")
                row += n
            for src in (hy_b1, hy_freq1, hy_b2, hy_freq2):
                load(staged[row:row + 1, 0:64], src, "in_vec")
                row += 1
            load(w1_sb, hy_w1[0], "in_feat")
            load(w2_sb, hy_w2[0], "in_feat")
            load(feat, features, "in_feat")
            load(cond_raw[:, 0, :], c[0].rearrange("(p t) -> p t", t=KT), "in_feat")
            load(cond_raw[:, 1, :], c_ctx.rearrange("(p t) -> p t", t=KT), "in_feat")
            load(w3_sb, hy_w3[0], "in_window")
            load(window_sb, window, "in_window")
            sp.wait_ge(s["pool_rpb"], 1)
            with nc.allow_non_contiguous_dma(reason="a small table, transposed"):
                for r in range(2):
                    for h in range(HEADS):
                        load(rpb_t[32 * r:32 * r + 31, h, :], na_rpb[0, h, 1 - r:15 - r, :].rearrange("d c -> c d"), "in_rpb")
            for n, (src, dst, _, _) in enumerate(chunks):
                if n == 1:
                    load(x_sb, x[0].rearrange("(t p) d -> p t d", p=P), "in_x")
                    load(x_ctx, ctx[0].rearrange("(t p) d -> p t d", p=P), "in_x")
                    load(pk[:, :], pack, "in_x")
                if n >= 3:
                    sp.wait_ge(s[chunks[n - 3][2]], chunks[n - 3][3])
                sp.dma_start(dst, src).then_inc(in_ring[n % 3], 16)
                if n == K_MLA:
                    sp.wait_ge(s["pe_tok"], 2)
                    sp.wait_ge(s["dve_oc"], 2)
                    load(w_uq, mla_w_uq[0].rearrange("(t p) n -> p t n", p=P), "in_uq")
                    load(w_ukv, mla_w_ukv[0], "in_uq")

            def load_gate(d, n):
                sp.dma_start(w_gate[:, n, :, :], w_in_k[:, :, bass.ds(d * P + GATE + n * D, P)]).then_inc(in_gate[n], 16)

            def load_branch(d, m):
                sp.dma_start(wb[:, m, :, :], w_branch[0].rearrange("n (t p) d -> p (n t) d", p=P)[:, :, bass.ds(d * P, P)])\
                  .then_inc(in_gate[1], 16)

            sp.wait_ge(s["pe_bb"], 8)
            sp.wait_ge(s["dve_acc"], 12)
            for n in range(4):
                load_gate(0, n)
            sp.wait_ge(s["pe_odT"], 4)
            load_branch(0, 0)
            load(final_gain, final_norm_g.rearrange("(a d) -> a d", a=1).to_broadcast([P, D]), "in_res")
            load(wr[:, :, 0:4], moe_w_group[0].rearrange("(t p) n -> p t n", p=P), "in_router")
            load(wr[:, :, 4:20], moe_w_expert[0].rearrange("(t p) n -> p t n", p=P), "in_router")
            load(wr_bias[:, 0:4], moe_b_group[0:1, :].to_broadcast([P, 4]), "in_router")
            load(wr_bias[:, 4:20], moe_b_expert[0:1, :].to_broadcast([P, 16]), "in_router")

            w_out_k = w_out[0].rearrange("(t p) n -> p t n", p=P)
            load(w_out_first, w_out_k[:, :, 0:256], "in_w_out")

            def refill(d, m):
                for n in range(4):
                    sp.wait_ge(s["pe_gate"], d * 8 + (2 * n - 6))
                    load_gate(d, n)
                    if n == 1:
                        load_branch(d, m)

            with sp.Fori(0, 3) as i:
                for m in range(2):
                    refill(i * 2 + (m + 1), 1 - m)
            refill(7, 1)
            sp.wait_ge(s["pe_gate"], 64)
            sp.wait_ge(s["in_w_out"], 16)
            load(w_out_last, w_out_k[:, :, 256:1024], "in_w_out")
            load(x1, x[0].rearrange("(t p) d -> p t d", p=P), "in_x1")
            sp.wait_ge(s["pe_out"], TT)
            load(tab, routing_tab, "in_tab")
            for n in range(2):
                sp.dma_start(slots_dram[(2 + n) * T:(3 + n) * T, :], x[0]).then_inc(rows_stored, 16)
            for i in range(TT):
                sp.wait_ge(s["dve_x1n"], i + 1)
                sp.dma_start(rows_dram[i * P:i * P + P, :], x1n[:, i, :]).then_inc(rows_stored, 16)

            def load_gate_up(j, m):
                e = sp.value_load(expert_of[0:1, bass.ds(j, 1)], min_val=0, max_val=EXPERTS - 1)
                for n, w in enumerate((moe_w_gate, moe_w_up)):
                    sp.dma_start(expert_slots[:, m, :, n * HID:n * HID + HID],
                                 w[0, bass.ds(e, 1)].rearrange("e (t p) f -> p (e t) f", p=P)).then_inc(in_expert[m], 16)
                return e

            def load_down(e, m):
                sp.dma_start(w_down[:, m, :, :], moe_w_down[0, bass.ds(e, 1)].rearrange("e (t p) d -> p (e t) d", p=P))\
                  .then_inc(in_down[m], 16)

            sp.wait_ge(s["dve_table"], 1)
            sp.wait_ge(s["pe_out"], 3 * TT)
            sp.wait_ge(rows_stored, 16 * (TT + 2))
            for m in range(2):
                sp.sem_inc(y_stored[m], 16)
                load_down(load_gate_up(m, m), m)
            pairs = sp.value_load(pair_count, min_val=8, max_val=16)

            def store(j, m):
                sp.wait_ge(s["dve_y"], j * 2 + 2 + FREE)
                sp.dma_start(slots_dram[bass.ds(j * P, P), :], slot_y[:, m, :]).then_inc(y_stored[m], 16)

            with sp.Fori(0, pairs - 1) as i:
                for m in range(2):
                    sp.wait_ge(s["pe_au"], i * 2 + m + 1 + FREE)
                    e = load_gate_up(i * 2 + m + 2, m)
                    sp.wait_ge(s["pe_down"], i * 4 + 2 * m + 2 + FREE)
                    load_down(e, m)
                    store(i * 2 + m, m)
            for m in range(2):
                store(pairs * 2 + (m - 2), m)
            for i in range(TT):
                sp.wait_ge(s["dve_fin"], i + 1)
                sp.dma_start(out[0, i * P:i * P + P, :], x1[:, i, :]).then_inc(s["stored"], 16)
            sp.wait_ge(s["stored"], 16 * TT)

        @block.gpsimd
        def _(pool):
            pool.memset(ident[:, :], 0.0).then_inc(s["pool_const"], 1)
            pool.memset(rpb_t, MASK).then_inc(s["pool_rpb"], 1)
            pool.memset(ones[:, :], 1.0).then_inc(s["pool_const"], 1)
            pool.wait_ge(s["pool_const"], 2)
            pool.affine_select(out=ident[:, :], in_=ident[:, :], compare_op=ALU.not_equal, fill=1.0, base=0,
                               pattern=[[-1, P]], channel_multiplier=1).then_inc(s["pool_const"], 1)
            step = Steps(pool, s["pool_sq"])
            for i in range(TT):
                pool.wait_ge(s["dve_filt"], i + 1)
                for f in (fsum, fdif):
                    if i == 0 and f is fsum:
                        step(pool.tensor_tensor(sq_acc, f[:, i, :], f[:, i, :], ALU.mult))
                        continue
                    step(pool.tensor_tensor(sq_tmp, f[:, i, :], f[:, i, :], ALU.mult))
                    step(pool.tensor_tensor(sq_acc, sq_acc, sq_tmp, ALU.add))
            pool.wait_ge(s["pe_spec"], 8)
            pool.memset(raw[:, :, 0:1], 0.0).then_inc(s["pool_pad"], 1)
            pool.memset(raw[:, :, T + 1:T + 2], 0.0).then_inc(s["pool_pad"], 1)
            pool.wait_ge(s["dve_qT"], 8)
            with pool.Fori(0, HEADS) as h:
                for q in range(TT):
                    if q >= 2:
                        pool.wait_ge(s["pe_qk"], h * TT + q - 1)
                    pool.tensor_copy(q_now[:, q % 2, :].rearrange("p (a w) -> p a w", a=1),
                                     qT[:, bass.ds(h, 1), q * P:q * P + P]).then_inc(s["pool_q"], 1)
                pool.wait_ge(s["pe_qk"], h * TT + TT)
            pool.wait_ge(s["pe_oaT"], 4)
            pool.memset(nkT[64:128, :, :], 0.0).then_inc(s["pool_pad"], 1)
            pool.memset(nq_now[64:128, :, :], 0.0).then_inc(s["pool_pad"], 1)
            pool.wait_ge(s["act_nqk"], 10)
            pool.wait_ge(s["dve_nqk"], 10)

            def part(h, q):
                whole, upper, rest = (t[:, bass.ds(h * 2 + q // 4, 1), (q % 4) * 256:(q % 4) * 256 + 256]
                                      for t in (hT, hT_upper, hT_rest))
                pool.wait_ge(s["dve_split"], h * TT + q + 1)
                pool.sem_inc(s["pool_idx"], 1)
                pool.tensor_tensor(rest, whole, hT_split[:, q % 2, :, :], ALU.subtract).then_inc(s["pool_split"], 1)
                pool.wait_ge(s["pool_split"], h * (2 * TT) + (2 * q + 1))
                pool.sem_inc(s["pool_idx"], 1)
                pool.tensor_tensor(upper, whole, rest.bitcast(F32), ALU.subtract).then_inc(s["pool_split"], 1)

            def near_queries(h, q):
                pool.tensor_copy(nq_now[0:64, q % 2, :].rearrange("p (a w) -> p a w", a=1),
                                 nqT[:, bass.ds(h + q // TT, 1), (q % TT) * P:(q % TT) * P + P]).then_inc(s["pool_nq"], 1)

            def serve(h, end):
                for q in range(TT):
                    if q + 2 < TT or not end:
                        pool.wait_ge(s["pe_nqk2"], h * TT + q + 1)
                        near_queries(h, q + 2)
                    if q >= 1:
                        part(h, q - 1)
                part(h, TT - 1)

            near_queries(0, 0)
            near_queries(0, 1)
            with pool.Fori(0, HEADS - 1) as h:
                serve(h, False)
            serve(HEADS - 1, True)
            pool.wait_ge(s["dve_table"], 1)
            pool.wait_ge(rows_stored, 16 * (TT + 2))

            def gather(j, m):
                pool.tensor_copy(token_now[:, m:m + 1], token_of[:, bass.ds(j, 1)]).then_inc(s["pool_idx"], 1)
                pool.wait_ge(s["pool_idx"], j * 2 + (2 * HEADS * TT + 1))
                pool.sem_inc(s["pool_idx"], 1)
                pool.indirect_dma_start(slot_x[:, m, :], None, rows_dram, bass.IndirectOffsetOnAxis(token_now[:, m:m + 1], 0))\
                    .then_inc(in_slots[m], 16)

            gather(0, 0)
            gather(1, 1)
            pairs = pool.value_load(pair_count, min_val=8, max_val=16)
            with pool.Fori(0, pairs - 1) as i:
                for m in range(2):
                    pool.wait_ge(s["pe_x"], i * 2 + (m + 1 + FREE))
                    gather(i * 2 + (m + 2), m)
            for m in range(2):
                pool.wait_ge(y_stored[m], pairs * 16 + 16)
            pool.sem_inc(s["pool_idx"], 1)
            for i in range(TT):
                if i >= 4:
                    pool.wait_ge(s["dve_moe"], i - 3)
                for n in range(2):
                    pool.indirect_dma_start(parts[:, i % 4, n, :], None, slots_dram,
                                            bass.IndirectOffsetOnAxis(slots_i[:, n, i:i + 1], 0)).then_inc(in_parts[i % 4], 16)

        @block.scalar
        def _(act):
            step = Steps(act, s["act_chain"])
            act.sem_inc(s["act_gate"], FREE)
            for layer in range(2):
                act.wait_ge(s["dve_arg"], layer + 1)
                if layer == 1:
                    act.wait_ge(s["pe_sin"], 4)
                act.activation(hid, arg, ACT.Sin).then_inc(s["act_sin"], 1)
            act.wait_ge(s["in_feat"], 80)
            act.activation(cond.rearrange("p t v -> p v t"), cond_raw, ACT.Silu).then_inc(s["act_cond"], 1)
            act.wait_ge(s["in_x"], 48)
            scratch = cut(normed, 4096, D)
            for i in range(AT):
                src = x_sb[:, i, :] if i < TT else x_ctx[:, i - TT, :]
                step.mark(act.activation(scratch, src, ACT.Square, accum_out=ssq[:, i:i + 1]))
                step.sync()
            act.wait_ge(s["dve_vec"], 2)
            act.activation(rstd[:, 0:AT], ssq[:, 0:AT], ACT.Sqrt).then_inc(s["act_ssq"], 1)
            act.wait_ge(s["dve_vec"], 3)
            for i in range(AT):
                row = x_sb[:, i, :] if i < TT else x_ctx[:, i - TT, :]
                act.activation(row, row, ACT.Copy, scale=rstd[:, i:i + 1]).then_inc(s["act_xn"], 1)
            for g in range(8):
                act.wait_ge(s["pe_spec"], g + 1)
                act.activation(spec[:, g % 2, g // 2, :], bank(2 * (g % 2)), ACT.Copy).then_inc(s["act_even"], 1)
            act.wait_ge(s["dve_vec"], 4)
            act.activation(filter_norm, filter_norm, ACT.Sqrt).then_inc(s["act_ssq"], 1)
            act.wait_ge(s["dve_mod"], 1)
            act.wait_ge(s["act_xn"], AT)
            for n in range(3 * KT):
                kt, g = n // 3, n % 3
                w = 512 if g < 2 else C
                act.wait_ge(s["pe_xT"], n + 1)
                act.activation(hT[:, kt, g * 512:g * 512 + w], bank(n % 4, 0, w), ACT.Identity,
                               bias=shift1[:, g // 2, kt:kt + 1], scale=scale1[:, g // 2, kt:kt + 1])\
                   .then_inc(s["act_hT"], 1)
            act.wait_ge(s["pool_pad"], 2)
            for g in range(12):
                ct, half = g // 2, g % 2
                if half == 0 and ct >= 2:
                    act.wait_ge(s["dve_conv"], ct - 1)
                act.wait_ge(s["pe_hy"], g + 1)
                act.activation(raw[:, ct % 2, 1 + half * 512:513 + half * 512], bank(4 + g % 4), ACT.Copy)\
                   .then_inc(s["act_hy"], 1)
            for order in range(2):
                for tt in range(4):
                    act.wait_ge(s["pe_fold"], 4 * order + tt + 1)
                    act.activation(folded_t[:, tt, :, :], bank(tt), ACT.Copy).then_inc(s["act_fold"], 1)
                for ct in range(2):
                    act.wait_ge(s["pe_inv"], 3 * order + ct + 2)
                    for ab in range(2):
                        act.activation(halves[:, ct, ab, :], bank(2 * ct + ab), ACT.Copy,
                                       scale=filter_norm[:, 2 * order + ct:2 * order + ct + 1])\
                           .then_inc(s["act_inv"], 1)
            act.wait_ge(s["dve_z"], 4)
            for g in range(4):
                act.wait_ge(s["pe_fn"], g + 1)
                act.activation(fnT[:, g // 2, (g % 2) * 512:(g % 2) * 512 + 512], bank(g), ACT.Copy)\
                   .then_inc(s["act_fn"], 1)
            for i in range(TT):
                act.wait_ge(s["pe_chan"], i + 1)
                act.activation(chan_mixed[:, i, :, :, :], bank(4 + i % 4), ACT.Copy).then_inc(s["act_chan"], 1)
            act.wait_ge(s["pe_tok"], 2)
            for ct in range(2):
                act.activation(sine_part[:, ct, :], bank(4 + ct), ACT.Copy).then_inc(s["act_tok"], 1)
            square = q_tok[:, 0, :, :].rearrange("p h f -> p (h f)")
            sums = Steps(act, s["act_msq"])
            for i in range(AT):
                act.wait_ge(s["dve_mla"], i + 1)
                if i < TT:
                    sums(act.activation(square[:, 0:256], mla_tok[:, i, 0:256], ACT.Square, accum_out=ssq[:, i:i + 1]))
                sums(act.activation(square[:, 0:128], mla_tok[:, i, 256:384], ACT.Square,
                                    accum_out=ssq[:, 8 + i:9 + i]))
            act.wait_ge(s["dve_mn"], 2)
            act.activation(rstd[:, 0:18], ssq[:, 0:18], ACT.Sqrt).then_inc(s["act_mrt"], 1)
            for g in range(7):
                act.wait_ge(s["pe_mT"], g + 1)
                if g < 4:
                    act.activation(cqT[:, g // 2, (g % 2) * 512:(g % 2) * 512 + 512], bank(g), ACT.Copy,
                                   scale=vec[:, V_QN + g // 2:V_QN + g // 2 + 1]).then_inc(s["act_mT"], 1)
                else:
                    w = 512 if g < 6 else C
                    act.activation(ckvT[:, (g - 4) * 512:(g - 4) * 512 + w], bank(g, 0, w), ACT.Copy,
                                   scale=vec[:, V_KVN:V_KVN + 1]).then_inc(s["act_mT"], 1)
            for i in range(AT):
                act.wait_ge(s["pe_ukv"], i + 1)
                kv = bank(4 + i % 4).rearrange("p (h f) -> p h f", h=HEADS)
                act.activation(k_tok[:, i, :, 0:NOPE], kv[:, :, 0:NOPE], ACT.Copy).then_inc(s["act_ukv"], 1)
                act.activation(v_tok[:, i, :].rearrange("p (h f) -> p h f", h=HEADS), kv[:, :, NOPE:], ACT.Copy)\
                   .then_inc(s["act_ukv"], 1)
            for g in range(12):
                w = 512 if g % 3 < 2 else C
                act.wait_ge(s["pe_kT"], g + 1)
                if g == 0:
                    act.wait_ge(s["pe_qT"], 8)
                act.activation(kT[:, g // 3, (g % 3) * 512:(g % 3) * 512 + w], psum[0:QK, (4 + g % 4) * 512:(4 + g % 4) * 512 + w],
                               ACT.Copy).then_inc(s["act_kT"], 1)
            act.wait_ge(s["pe_kT"], 12)
            def exponentials(h, q):
                c = q % TT
                act.wait_ge(s["dve_mx"], h * TT + q + 1)
                if q >= 2:
                    act.wait_ge(s["pe_t"], h * 3 * TT + 3 * (q - 1))
                act.activation(prob[:, q % 2, :], psum[:, (q % 2) * 1536:(q % 2) * 1536 + KEYS], ACT.Exp,
                               bias=neg_max[:, c:c + 1], scale=MLA_SCALE, accum_out=row_sum[:, c:c + 1])\
                   .then_inc(s["act_p"], 1)

            def probabilities(h, end):
                for q in range(TT):
                    if q >= 1:
                        act.wait_ge(s["pe_pv"], h * TT + q)
                    act.wait_ge(s["pe_t"], h * 3 * TT + 3 * q + 2)
                    act.activation(probT[:, 4:8, :], bank(7), ACT.Copy).then_inc(s["act_pt"], 1)
                    if q + 1 < TT or not end:
                        exponentials(h, q + 1)
                act.wait_ge(s["pe_pv"], h * TT + TT)

            exponentials(0, 0)
            with act.Fori(0, HEADS - 1) as h:
                probabilities(h, False)
            probabilities(HEADS - 1, True)
            for g in range(4):
                act.wait_ge(s["pe_oaT"], 4)
                act.activation(oT[0][:, g // 2, (g % 2) * 512:(g % 2) * 512 + 512], bank(g), ACT.Copy)\
                   .then_inc(s["act_oaT"], 1)
            for g in range(10):
                act.wait_ge(s["pe_nqk"], g + 1)
                dst, lo, w = na_group(g)
                act.activation(dst[0:64, (g % 2) * 2, lo:lo + w], psum[0:64, (g % 4) * 512:(g % 4) * 512 + w], ACT.Copy)\
                   .then_inc(s["act_nqk"], 1)
            for i in range(AT):
                act.wait_ge(s["pe_nv"], i + 1)
                act.activation(nv_tok[:, i, :], bank(4 + i % 4, 0, BW), ACT.Copy).then_inc(s["act_nv"], 1)
            def near_exponentials(h, q):
                c = q % TT
                n = NA_TILES[c][1] + C
                act.wait_ge(s["dve_nmx"], h * TT + q + 1)
                act.activation(nprob[:, q % 2, 0:n], nprob[:, q % 2, 0:n], ACT.Exp, bias=neg_max[:, c:c + 1],
                               accum_out=row_sum[:, c:c + 1]).then_inc(s["act_np"], 1)

            def near_probabilities(h, end):
                for q in range(TT):
                    n = (NA_TILES[q][1] + C) // P
                    if q >= 1:
                        act.wait_ge(s["pe_npv"], h * TT + q)
                    for r in range(2):
                        act.wait_ge(s["pe_nt"], h * 2 * TT + 2 * q + r + 1)
                        w = min(4, n - 4 * r)
                        act.activation(nprobT[:, 4 * r:4 * r + w, :], bank(4 + r, 0, w * P), ACT.Copy)\
                           .then_inc(s["act_npt"], 1)
                    if q + 1 < TT or not end:
                        near_exponentials(h, q + 1)
                act.wait_ge(s["pe_npv"], h * TT + TT)

            near_exponentials(0, 0)
            with act.Fori(0, HEADS - 1) as h:
                near_probabilities(h, False)
            near_probabilities(HEADS - 1, True)
            for g in range(4):
                act.wait_ge(s["pe_odT"], 4)
                act.activation(oT[3][:, g // 2, (g % 2) * 512:(g % 2) * 512 + 512], bank(g), ACT.Copy)\
                   .then_inc(s["act_odT"], 1)
            with act.Fori(0, KT // 2) as i:
                for m in range(16):
                    act.wait_ge(s["dve_gate"], i * 16 + m + FREE - 1)
                    act.wait_ge(s["pe_gg"], i * 16 + m + 1)
                    act.activation(gate_sb[:, m % 2, :], bank(m % 4), ACT.Sigmoid).then_inc(s["act_gate"], 1)
            def second_rows(i):
                if i >= 2:
                    act.wait_ge(s["pe_route"], i - 1)
                for kt in range(KT):
                    act.wait_ge(s["pe_hT2"], i + 1)
                    act.activation(h2T[:, i % 2, kt, :], bank(4 + kt // 4, (kt % 4) * P, (kt % 4) * P + P), ACT.Identity,
                                   bias=shift2[:, kt:kt + 1], scale=scale2[:, kt:kt + 1]).then_inc(s["act_hT2"], 1)

            act.wait_ge(s["dve_ada"], 17)
            sums = Steps(act, s["act_ssq2"])
            for i in range(TT):
                act.wait_ge(s["dve_x1"], 2 * TT + i + 1)
                sums(act.activation(square2, x1[:, i, :], ACT.Square, accum_out=ssq[:, i:i + 1]))
                act.wait_ge(s["dve_ms2"], i + 1)
                act.activation(rstd[:, i:i + 1], ssq[:, i:i + 1], ACT.Sqrt).then_inc(s["act_rt2"], 1)
                if i >= 1:
                    second_rows(i - 1)
            second_rows(TT - 1)
            act.wait_ge(s["dve_route"], 1)
            act.activation(group_exp, group_exp, ACT.Exp).then_inc(s["act_route"], 1)
            act.wait_ge(s["dve_route"], 2)
            act.activation(rc[3], rc[3], ACT.Exp).then_inc(s["act_route"], 1)
            act.wait_ge(s["dve_table"], 1)
            pairs = act.value_load(pair_count, min_val=8, max_val=16)

            def modulate(j, m):
                act.wait_ge(s["pe_au"], j + (FREE - 1))
                act.wait_ge(s["pe_x"], j + (1 + FREE))
                for kt in range(4):
                    act.activation(slot_hT[:, m, kt, :], bank(2, kt * P, kt * P + P), ACT.Identity,
                                   bias=shift2[:, kt:kt + 1], scale=scale2[:, kt:kt + 1]).then_inc(s["act_h"], 1)

            def half_silu(j, m):
                act.wait_ge(s["dve_mul"], j + (FREE - 1))
                act.wait_ge(s["pe_au"], j + (FREE + 1))
                act.activation(silu[:, m, :], bank(m, 0, HID), ACT.Silu).then_inc(s["act_silu"], 1)

            modulate(0, 0)
            half_silu(0, 0)
            modulate(1, 1)
            with act.Fori(0, pairs - 1) as i:
                for m in range(2):
                    half_silu(i * 2 + (m + 1), 1 - m)
                    modulate(i * 2 + (m + 2), m)
            half_silu(pairs * 2 - 1, 1)
            for i in range(TT):
                act.wait_ge(s["dve_moe"], i + 1)
                sums(act.activation(square2, x1[:, i, :], ACT.Square, accum_out=ssq[:, i:i + 1]))
                act.wait_ge(s["dve_ms2"], TT + i + 1)
                act.activation(rstd[:, i:i + 1], ssq[:, i:i + 1], ACT.Sqrt).then_inc(s["act_rt2"], 1)

        @block.vector
        def _(dve):
            step = Steps(dve, s["dve_chain"])
            for name in ("dve_mul", "dve_actT", "dve_y"):
                dve.sem_inc(s[name], FREE)
            dve.sem_inc(s["dve_gate"], FREE)
            dve.memset(staged, 0.0).then_inc(s["dve_zero"], 1)
            dve.wait_ge(s["pe_vec"], 1)
            dve.tensor_copy(vec[:, :], bank(7, 0, V_END)).then_inc(s["dve_vec"], 1)
            dve.wait_ge(s["dve_vec"], 1)
            for layer, (b, f) in enumerate(((V_B1, V_F1), (V_B2, V_F2))):
                dve.wait_ge(s["pe_sin"], 2 * layer + 2)
                if layer == 1:
                    dve.wait_ge(s["act_sin"], 1)
                step(dve.tensor_scalar(arg, psum[0:64, layer * 1024:layer * 1024 + 1024], vec[0:64, b:b + 1],
                                       vec[0:64, f:f + 1], ALU.add, ALU.mult))
                step(dve.tensor_scalar(turn, arg, 1.0 / TURN, ROUND, ALU.mult, ALU.add))
                step(dve.tensor_scalar(turn, turn, -ROUND, -TURN, ALU.add, ALU.mult))
                step(dve.tensor_tensor(arg, arg, turn, ALU.add))
                dve.tensor_scalar(arg, arg, PI, -PI, ALU.min, ALU.max).then_inc(s["dve_arg"], 1)
            dve.wait_ge(s["in_window"], 32)
            for i in range(TT):
                dve.wait_ge(s["pe_filt"], i + 1)
                b = 4 + 2 * (i % 2)
                for dst, n in ((fir_f, 0), (fir_b, 1)):
                    step.mark(dve.tensor_tensor(
                        dst.rearrange("p (o w) -> p o w", o=2), bank(b + n).rearrange("p (o w) -> p o w", o=2),
                        window_sb[:, i, n:n + 1, :].to_broadcast([P, 2, BW]), ALU.mult))
                step.sync()
                step.mark(dve.tensor_tensor(fsum[:, i, :], fir_f, fir_b, ALU.add))
                dve.tensor_tensor(fdif[:, i, :], fir_f, fir_b, ALU.subtract).then_inc(s["dve_filt"], 1)
                dve.wait_ge(s["dve_filt"], i + 1)
                step.sync()
            dve.wait_ge(s["act_chain"], AT)
            dve.tensor_scalar(ssq[:, 0:AT], ssq[:, 0:AT], 1.0 / D, EPS, ALU.mult, ALU.add).then_inc(s["dve_vec"], 1)
            dve.wait_ge(s["act_ssq"], 1)
            dve.reciprocal(rstd[:, 0:AT], rstd[:, 0:AT]).then_inc(s["dve_vec"], 1)

            def accumulate(c, sums, rows=range(KT)):
                arrived(dve, K_ADA[c])
                w = slot(K_ADA[c], KT, 512)
                for t in rows:
                    for acc, v in sums:
                        col = cond[:, t, v:v + 1]
                        if t == 0:
                            ins = dve.tensor_scalar(acc, w[:, t, :], col, None, ALU.mult)
                        else:
                            ins = dve.scalar_tensor_tensor(out=acc, in0=w[:, t, :], scalar=col, in1=acc,
                                                           op0=ALU.mult, op1=ALU.add)
                        if t == KT - 1 and v == sums[-1][1]:
                            ins.then_inc(s["dve_acc"], 1)
                        else:
                            step.mark(ins)
                    step.sync()

            def add_up(g, b, dst):
                dve.wait_ge(s["pe_ada"], g + 1)
                dve.tensor_reduce(dst, bank(b).rearrange("p (m k) -> p m k", m=4), AX.X, ALU.add).then_inc(s["dve_ada"], 1)

            def ada_sums(n):
                for v in range(2):
                    add_up(2 * n + v, 4 + 2 * (n % 2) + v, (shift1, scale1)[n // 2][:, v, 4 * (n % 2):4 * (n % 2) + 4])

            def other_acc(c):
                if c >= 2:
                    dve.wait_ge(s["pe_ada"], 8 + c - 1)
                accumulate(4 + c, [(ada_acc2[:, c % 2, :], 0)])

            def other_sum(c, b):
                dst = (shift2, scale2)[c // 2][:, 4 * (c % 2):4 * (c % 2) + 4] if c < 4 else gate_col[:, 4 * c - 16:4 * c - 12]
                at = V_ADAB + 4 * (6, 7, 8, 9, 4, 5, 10, 11)[c]
                add_up(8 + c, b, dst)
                dve.wait_ge(s["dve_ada"], 8 + c + 1)
                step(dve.tensor_tensor(dst, dst, vec[:, at:at + 4], ALU.add))

            def spectrum(g):
                f, part = g // 2, g % 2
                even, odd = spec[:, part, f, :], bank(2 * (g % 2) + 1)
                dve.wait_ge(s["act_even"], g + 1)
                a, b = (even, odd) if part == 0 else (odd, even)
                step(dve.tensor_tensor(spec[:, part, 4 + f, :], a, b, ALU.subtract))
                dve.tensor_tensor(even, even, odd, ALU.add).then_inc(s["dve_filter"], 1)

            def ada_half(n, half):
                accumulate(n, [(ada_acc[:, n, v, :], v) for v in range(2)], range(4 * half, 4 * half + 4))

            dve.wait_ge(s["act_cond"], 1)
            ada_half(0, 0)
            ada_half(0, 1)
            spectrum(0)
            spectrum(1)
            ada_half(1, 0)
            spectrum(2)
            spectrum(3)
            ada_half(1, 1)
            dve.wait_ge(s["pe_fnorm"], 1)
            dve.tensor_scalar(filter_norm, bank(4, 0, 4), 0.5, EPS, ALU.mult, ALU.add).then_inc(s["dve_vec"], 1)
            spectrum(4)
            ada_half(2, 0)
            spectrum(5)
            ada_half(2, 1)
            ada_sums(0)
            ada_sums(1)
            spectrum(6)
            ada_half(3, 0)
            spectrum(7)
            ada_half(3, 1)
            ada_sums(2)
            ada_sums(3)
            dve.wait_ge(s["act_ssq"], 2)
            step(dve.reciprocal(filter_norm, filter_norm))
            dve.wait_ge(s["dve_ada"], 8)
            for v in range(2):
                step(dve.tensor_tensor(shift1[:, v, :], shift1[:, v, :], vec[:, 0:8], ALU.add))
                step(dve.tensor_tensor(scale1[:, v, :], scale1[:, v, :], vec[:, 8:16], ALU.add))
                ins = dve.scalar_tensor_tensor(out=scale1[:, v, :], in0=scale1[:, v, :], scalar=1.0,
                                               in1=vec[:, V_N1:V_N1 + 8], op0=ALU.add, op1=ALU.mult)
                if v == 0:
                    step(ins)
                else:
                    ins.then_inc(s["dve_mod"], 1)
            def fold(ct):
                z = conv[:, ct, :]
                for n, op in enumerate((ALU.add, ALU.subtract)):
                    dve.tensor_tensor(folded[:, n, ct, :], z[:, 0:512], z[:, T - 1:511:-1], op).then_inc(s["dve_fold"], 1)

            for ct in range(6):
                dve.wait_ge(s["act_hy"], 2 * ct + 2)
                if 1 <= ct <= 2:
                    dve.wait_ge(s["dve_conv"], ct)
                    fold(ct - 1)
                tap = [vec[:, V_TAP + 6 * j + ct:V_TAP + 6 * j + ct + 1] for j in range(3)]
                u = raw[:, ct % 2, :]
                step(dve.tensor_scalar(conv[:, ct, :], u[:, 1:T + 1], tap[1], None, ALU.mult))
                step(dve.scalar_tensor_tensor(out=conv[:, ct, :], in0=u[:, 0:T], scalar=tap[0],
                                              in1=conv[:, ct, :], op0=ALU.mult, op1=ALU.add))
                dve.scalar_tensor_tensor(out=conv[:, ct, :], in0=u[:, 2:T + 2], scalar=tap[2],
                                         in1=conv[:, ct, :], op0=ALU.mult, op1=ALU.add)\
                   .then_inc(s["dve_conv"], 1)
            dve.wait_ge(s["dve_conv"], 6)
            for order in range(2):
                for j in range(KT):
                    re, im = (spec[:, n, j:j + 1, order * BW:order * BW + BW].to_broadcast([P, 2, BW]) for n in range(2))
                    u = bank(4 + j % 4).rearrange("p (n w) -> p n w", n=2)
                    if j == 0 and order == 0:
                        dve.wait_ge(s["dve_filter"], 8)
                    dve.wait_ge(s["pe_fwd"], 8 * order + j + 1)
                    step.mark(dve.tensor_tensor(prod_r, u, re, ALU.mult))
                    step(dve.tensor_tensor(prod_i, u, im, ALU.mult))
                    step.mark(dve.tensor_tensor(conv_spec[:, j, 0, :], prod_r[:, 0, :], prod_i[:, 1, :], ALU.subtract))
                    dve.tensor_tensor(conv_spec[:, j, 1, :], prod_r[:, 1, :], prod_i[:, 0, :], ALU.add)\
                       .then_inc(s["dve_spec"], 1)
                    dve.wait_ge(s["dve_spec"], 8 * order + j + 1)
                    step.sync()
                for ct in range(2):
                    dve.wait_ge(s["act_inv"], 4 * order + 2 * ct + 2)
                    a, b = halves[:, ct, 0, :], halves[:, ct, 1, :]
                    step.mark(dve.tensor_tensor(mix[:, 0:512], a, b, ALU.add))
                    step(dve.tensor_tensor(mix[:, T - 1:511:-1], a, b, ALU.subtract))
                    h = V_HB + 2 * order + ct
                    step(dve.scalar_tensor_tensor(out=mix, in0=conv[:, ct, :], scalar=vec[:, h:h + 1], in1=mix,
                                                  op0=ALU.mult, op1=ALU.add))
                    dst = conv[:, ct, :] if order == 0 else oT[1][:, ct, :]
                    dve.tensor_tensor(dst, mix, conv[:, 2 + 2 * order + ct, :], ALU.mult).then_inc(s["dve_z"], 1)
                    dve.wait_ge(s["dve_z"], 2 * order + ct + 1)
                    if order == 0:
                        fold(ct)
            for c in range(4):
                other_acc(c)
                if c == 1:
                    other_sum(0, 6)
                    other_sum(1, 7)
            dve.wait_ge(s["act_tok"], 2)
            for ct in range(2):
                o = oT[2][:, ct, :]
                sn = sine_part[:, ct, :]
                step.mark(dve.tensor_tensor(o[:, 0:512], bank(ct), sn, ALU.add))
                step.mark(dve.tensor_tensor(o[:, T - 1:512:-1], bank(ct, 1, 512), sn[:, 1:512], ALU.subtract))
                dve.tensor_copy(o[:, 512:513], bank(2, ct, ct + 1)).then_inc(s["dve_oc"], 1)
            step.sync()
            other_sum(2, 6)
            other_sum(3, 7)
            for i in range(AT):
                lo = 0 if i < TT else 256
                dve.wait_ge(s["pe_mla"], i + 1)
                dve.tensor_copy(mla_tok[:, i, lo:416], bank(i % 4, lo, 416)).then_inc(s["dve_mla"], 1)
                if i in (3, 6):
                    other_acc(4 + i // 6)
            other_sum(4, 7)
            dve.wait_ge(s["act_msq"], 2 * TT + CT)
            norms = Steps(dve, s["dve_mn"])
            norms.mark(dve.tensor_scalar(ssq[:, 0:8], ssq[:, 0:8], 1.0 / 256, EPS, ALU.mult, ALU.add))
            norms.mark(dve.tensor_scalar(ssq[:, 8:18], ssq[:, 8:18], 1.0 / 128, EPS, ALU.mult, ALU.add))
            dve.wait_ge(s["act_mrt"], 1)
            dve.wait_ge(s["dve_mla"], AT)
            step(dve.reciprocal(rstd[:, 0:18], rstd[:, 0:18]))
            for i in range(TT):
                norms.mark(dve.tensor_scalar(mla_tok[:, i, 0:256], mla_tok[:, i, 0:256], rstd[:, i:i + 1], None, ALU.mult))
            for i in range(AT):
                norms.mark(dve.tensor_scalar(mla_tok[:, i, 256:384], mla_tok[:, i, 256:384], rstd[:, 8 + i:9 + i], None,
                                             ALU.mult))
            other_sum(5, 7)
            for i in range(TT):
                dve.wait_ge(s["pe_uq"], i + 1)
                dve.tensor_copy(q_tok[:, i, :, :], bank(i % 4, 0, 384)).then_inc(s["dve_uq"], 1)
            dve.wait_ge(s["dve_uq"], TT)
            kr = mla_tok[:, 0:TT, KR:416].rearrange("p t (h f) -> p t h f", h=1)
            for x4, heads in ((q_tok[:, :, :, NOPE:QK], HEADS), (kr, 1)):
                cos, sin = (rope_t[:, n, :, :].rearrange("p t (h f) -> p t h f", h=1).to_broadcast([P, TT, heads, 16])
                            for n in range(2))
                even, odd = x4[:, :, :, 0::2], x4[:, :, :, 1::2]
                r = [t[:, :, 0:heads, :] for t in rot]
                step.mark(dve.tensor_tensor(r[0], even, cos, ALU.mult))
                step.mark(dve.tensor_tensor(r[1], odd, sin, ALU.mult))
                step.mark(dve.tensor_tensor(r[2], even, sin, ALU.mult))
                step(dve.tensor_tensor(r[3], odd, cos, ALU.mult))
                step.mark(dve.tensor_tensor(even, r[0], r[1], ALU.subtract))
                step(dve.tensor_tensor(odd, r[2], r[3], ALU.add))
            for h in range(HEADS):
                dve.tensor_copy(k_tok[:, :, h, NOPE:QK], mla_tok[:, :, KR:416]).then_inc(s["dve_rope"], 1)
            for g in range(8):
                if g == 0:
                    dve.wait_ge(s["dve_rope"], HEADS)
                dve.wait_ge(s["pe_qT"], g + 1)
                dve.tensor_copy(qT[:, g // 2, (g % 2) * 512:(g % 2) * 512 + 512], psum[0:QK, (g % 4) * 512:(g % 4) * 512 + 512])\
                   .then_inc(s["dve_qT"], 1)
            dve.wait_ge(s["act_kT"], 12)
            def row_max(h, q):
                c = q % TT
                dve.wait_ge(s["pe_qk"], h * TT + q + 1)
                step(dve.tensor_reduce(neg_max[:, c:c + 1], psum[:, (q % 2) * 1536:(q % 2) * 1536 + KEYS], AX.X, ALU.max))
                dve.tensor_scalar(neg_max[:, c:c + 1], neg_max[:, c:c + 1], -MLA_SCALE, None, ALU.mult)\
                   .then_inc(s["dve_mx"], 1)

            def output(h, q):
                dve.wait_ge(s["act_p"], h * TT + q + 1)
                step(dve.reciprocal(row_inv[:, q:q + 1], row_sum[:, q:q + 1]))
                dve.wait_ge(s["pe_pv"], h * TT + q + 1)
                dve.tensor_scalar(oa_tok[:, q, bass.ds(h * VD, VD)], bank(7, 0, VD),
                                  row_inv[:, q:q + 1], None, ALU.mult).then_inc(s["dve_o"], 1)

            def attend(h, end):
                for q in range(TT):
                    if q + 1 < TT or not end:
                        row_max(h, q + 1)
                    if q >= 1:
                        output(h, q - 1)
                    if q >= 1:
                        dve.wait_ge(s["pe_pv"], h * TT + q)
                    dve.wait_ge(s["pe_t"], h * 3 * TT + 3 * q + 1)
                    dve.tensor_copy(probT[:, 0:4, :], bank(6)).then_inc(s["dve_pt"], 1)
                    dve.wait_ge(s["pe_t"], h * 3 * TT + 3 * q + 3)
                    dve.tensor_copy(probT[:, 8:10, :], bank(6, 0, 256)).then_inc(s["dve_pt"], 1)
                output(h, TT - 1)

            row_max(0, 0)
            with dve.Fori(0, HEADS - 1) as h:
                step.enter(h, 2 * TT)
                attend(h, False)
            step.leave(HEADS - 1, 2 * TT)
            attend(HEADS - 1, True)
            for g in range(10):
                dve.wait_ge(s["pe_nqk"], g + 1)
                dst, lo, w = na_group(g)
                dve.tensor_copy(dst[0:64, (g % 2) * 2 + 1, lo:lo + w], psum[64:128, (g % 4) * 512:(g % 4) * 512 + w])\
                   .then_inc(s["dve_nqk"], 1)
                if g == 1:
                    other_acc(6)
            other_sum(6, 4)
            other_acc(7)
            for b in range(8):
                dve.wait_ge(s["pe_bb"], b + 1)
                dve.tensor_copy(
                    rel_bias.rearrange("p h (r k) -> p (h r) k", k=64)[:, :, 8 * b:8 * b + 8],
                    bank(b, 0, 448).rearrange("p (k r) -> p r k", k=8)).then_inc(s["dve_bb"], 1)
            dve.wait_ge(s["dve_bb"], 8)
            other_sum(7, 7)

            def upper_bits(kept, whole):
                return dve.tensor_scalar(kept.bitcast(I32), whole.bitcast(I32), UPPER, None, ALU.bitwise_and)

            def split_gate(n):
                for half in range(2):
                    k = slice(4 * half, 4 * half + 4)
                    whole, rest = w_gate[:, n, k, :], w_rest[:, n % 2, k, :]
                    step(upper_bits(w_split, whole))
                    step(dve.tensor_tensor(rest, whole, w_split, ALU.subtract))
                    ins = dve.tensor_tensor(w_upper[:, n, k, :], whole, rest.bitcast(F32), ALU.subtract)
                    if half == 0:
                        step(ins)
                    else:
                        ins.then_inc(s["dve_split"], 1)

            def near_max(h, q):
                c = q % TT
                first, n, col = NA_TILES[c]
                dve.wait_ge(s["pe_nqk2"], h * TT + q + 1)
                if q >= 2:
                    dve.wait_ge(s["pe_nt"], h * 2 * TT + 2 * (q - 1))
                local = nprob[:, q % 2, 0:n].rearrange("p (a w) -> p a w", a=1)
                scores = psum[:, (q % 2) * 1024:(q % 2) * 1024 + n + C]
                bias = inner_bias.rearrange("p (a w) -> p a w", a=1) if col is None else \
                    rel_bias[:, bass.ds(h + q // TT, 1), col:col + n]
                step.mark(dve.scalar_tensor_tensor(out=local, in0=scores[:, 0:n].rearrange("p (a w) -> p a w", a=1),
                                                   scalar=NA_SCALE, in1=bias, op0=ALU.mult, op1=ALU.add))
                step(dve.tensor_scalar(nprob[:, q % 2, n:n + C], scores[:, n:n + C], NA_SCALE, None, ALU.mult))
                step(dve.tensor_reduce(neg_max[:, c:c + 1], nprob[:, q % 2, 0:n + C], AX.X, ALU.max))
                dve.tensor_scalar(neg_max[:, c:c + 1], neg_max[:, c:c + 1], -1.0, None, ALU.mult)\
                   .then_inc(s["dve_nmx"], 1)

            def near_output(h, q):
                dve.wait_ge(s["act_np"], h * TT + q + 1)
                step(dve.reciprocal(row_inv[:, q:q + 1], row_sum[:, q:q + 1]))
                dve.wait_ge(s["pe_npv"], h * TT + q + 1)
                dve.tensor_scalar(od_tok[:, q, bass.ds(h * VD, VD)], bank(6 + q % 2, 0, VD),
                                  row_inv[:, q:q + 1], None, ALU.mult).then_inc(s["dve_no"], 1)

            def near_attend(h, end):
                mask = row_mask.rearrange("p a b -> p (a b)").rearrange("p (a w) -> p a w", a=1)
                step(dve.tensor_tensor(inner_bias.rearrange("p (a w) -> p a w", a=1), rel_bias[:, bass.ds(h, 1), 128:768],
                                       mask, ALU.add))

                for q in range(TT):
                    if q >= 2:
                        dve.wait_ge(s["pool_split"], h * (2 * TT) + (2 * q - 2))
                    upper_bits(hT_split[:, q % 2, :, :], hT[:, bass.ds(h * 2 + q // 4, 1), (q % 4) * 256:(q % 4) * 256 + 256])\
                        .then_inc(s["dve_split"], 1)
                    if q + 1 < TT or not end:
                        near_max(h, q + 1)
                    if q >= 1:
                        near_output(h, q - 1)
                near_output(h, TT - 1)
                dve.wait_ge(s["pool_split"], h * (2 * TT) + 2 * TT)

            near_max(0, 0)
            with dve.Fori(0, HEADS - 1) as h:
                step.enter(h, 1 + 4 * TT)
                near_attend(h, False)
            step.leave(HEADS - 1, 1 + 4 * TT)
            near_attend(HEADS - 1, True)
            dve.scalar_tensor_tensor(out=scale2, in0=scale2, scalar=1.0, in1=vec[:, V_N2:V_N2 + 8], op0=ALU.add,
                                     op1=ALU.mult).then_inc(s["dve_ada"], 1)
            dve.wait_ge(s["pe_odT"], 4)
            dve.tensor_copy(gate_cols, gate_col.rearrange("p (a k) -> p a k", k=1).to_broadcast([P, 16, P]))\
               .then_inc(s["dve_ada"], 1)
            dve.wait_ge(in_gate[0], 16)
            split_gate(0)
            for n in range(4):
                dve.wait_ge(s["pe_res"], n + 1)
                dst = (res_gate1, res_gate2)[n // 2][:, (n % 2) * 512:(n % 2) * 512 + 512]
                dve.tensor_copy(dst, bank(4 + n)).then_inc(s["dve_res"], 1)
            def gated_branches(i, last):
                for m in range(16):
                    n, half = (m // 2) % 4, m % 2
                    if half == 0 and not (last and m == 14):
                        n1, d1 = (n + 1) % 4, i * 2 + (m // 2 + 1) // 4
                        dve.wait_ge(s["dve_split"], i * 8 + (HEADS * TT + m // 2 + 1))
                        dve.wait_ge(in_gate[n1], (d1 + 1) * (32 if n1 == 1 else 16))
                        split_gate(n1)
                    dst = merged[:, bass.ds(i * 2 + m // 8, 1), half * 512:half * 512 + 512]
                    g, p = (t.rearrange("p (a w) -> p a w", a=1) for t in (gate_sb[:, m % 2, :], bank(4 + m % 4)))
                    dve.wait_ge(s["pe_gate"], i * 16 + m + 1)
                    dve.wait_ge(s["act_gate"], i * 16 + m + FREE + 1)
                    if n == 0:
                        dve.tensor_tensor(dst, g, p, ALU.mult).then_inc(s["dve_gate"], 1)
                    else:
                        add = gated.rearrange("p (a w) -> p a w", a=1)
                        dve.wait_ge(s["dve_gate"], i * 16 + m + FREE)
                        step(dve.tensor_tensor(add, g, p, ALU.mult))
                        dve.tensor_tensor(dst, dst, add, ALU.add).then_inc(s["dve_gate"], 1)

            with dve.Fori(0, 3) as i:
                step.enter(i, 12 + 5 * 8)
                gated_branches(i, False)
            step.leave(3, 12 + 5 * 8)
            gated_branches(3, True)
            dve.wait_ge(s["in_x1"], 16)
            def second_norm(i):
                dve.wait_ge(s["act_ssq2"], i + 1)
                dve.tensor_scalar(ssq[:, i:i + 1], ssq[:, i:i + 1], 1.0 / D, EPS, ALU.mult, ALU.add).then_inc(s["dve_ms2"], 1)
                dve.wait_ge(s["act_rt2"], i + 1)
                step(dve.reciprocal(rstd[:, i:i + 1], rstd[:, i:i + 1]))
                dve.tensor_scalar(x1n[:, i, :], x1[:, i, :], rstd[:, i:i + 1], None, ALU.mult).then_inc(s["dve_x1n"], 1)

            def logits_out(i):
                dve.wait_ge(s["pe_route"], i + 1)
                dve.tensor_copy(logits_t[:, i * P:i * P + P], psum[0:20, 3072 + (i % 4) * P:3200 + (i % 4) * P])\
                   .then_inc(s["dve_logit"], 1)

            for m in range(3 * TT):
                i, (lo, w) = m % TT, OUT_PASSES[m // TT]
                n = w.shape[-1]
                if m >= 2 * TT + 3:
                    logits_out(i - 3)
                dve.wait_ge(s["pe_out"], m + 1)
                dve.wait_ge(s["dve_x1"], m)
                step(dve.tensor_tensor(gated[:, 0:n], out_bank(m, n), res_gate1[:, lo:lo + n], ALU.mult))
                dve.tensor_tensor(x1[:, i, lo:lo + n], x1[:, i, lo:lo + n], gated[:, 0:n], ALU.add)\
                   .then_inc(s["dve_x1"], 1)
                if m >= 2 * TT:
                    second_norm(i)
            for i in range(TT - 3, TT):
                logits_out(i)

            def column(t):
                return t.rearrange("p (t a) -> p t a", a=1)

            def first_equal(hot, values, top):
                step(dve.tensor_tensor(hot, values, column(top).to_broadcast([P, TT, 4]), ALU.is_equal))
                step(dve.tensor_tensor(hot, hot, before_end, ALU.mult))
                step(dve.tensor_reduce(rc[7], hot, AX.X, ALU.min))
                step(dve.tensor_tensor(hot, hot, column(rc[7]).to_broadcast([P, TT, 4]), ALU.is_equal))

            dve.wait_ge(s["in_router"], 64)
            dve.wait_ge(s["in_tab"], 16)
            step(dve.tensor_scalar(place, column_no[:, 0:4], -4.0, None, ALU.add))
            before_end = place.rearrange("p (a k) -> p a k", a=1).to_broadcast([P, TT, 4])
            step(dve.memset(all_ones, 1.0))
            step(dve.memset(tile_off[:, 0, :], 0.0))
            step(dve.memset(one_row, 1.0))
            dve.wait_ge(s["pe_back"], TT)
            step(dve.tensor_tensor(logits, bank(7, 0, 160).rearrange("p (t n) -> p t n", n=20),
                                   wr_bias.rearrange("p (a n) -> p a n", a=1).to_broadcast([P, TT, 20]), ALU.add))
            group_logit = logits[:, :, 0:4]
            step(dve.tensor_reduce(rc[0], group_logit, AX.X, ALU.max))
            dve.tensor_tensor(group_exp, group_logit, column(rc[0]).to_broadcast([P, TT, 4]), ALU.subtract)\
               .then_inc(s["dve_route"], 1)
            first_equal(group_hot, group_logit, rc[0])
            picked = pick.rearrange("p t (g e) -> p t g e", g=4)
            step(dve.tensor_tensor(picked, logits[:, :, 4:20].rearrange("p t (g e) -> p t g e", g=4),
                                   group_hot.rearrange("p t (g a) -> p t g a", a=1).to_broadcast([P, TT, 4, 4]), ALU.mult))
            step(dve.tensor_reduce(expert_logit, picked.rearrange("p t g e -> p t e g"), AX.X, ALU.add))
            step(dve.tensor_reduce(rc[1], expert_logit, AX.X, ALU.max))
            first_equal(expert_hot, expert_logit, rc[1])
            step(dve.scalar_tensor_tensor(out=expert_logit, in0=expert_hot, scalar=MASK, in1=expert_logit, op0=ALU.mult,
                                          op1=ALU.add))
            step(dve.tensor_reduce(rc[2], expert_logit, AX.X, ALU.max))
            first_equal(second_hot, expert_logit, rc[2])
            dve.tensor_tensor(rc[3], rc[2], rc[1], ALU.subtract).then_inc(s["dve_route"], 1)

            def outer(dst, experts):
                return dve.tensor_tensor(dst.rearrange("p t (g e) -> p t g e", g=4),
                                         group_hot.rearrange("p t (g a) -> p t g a", a=1).to_broadcast([P, TT, 4, 4]),
                                         experts.rearrange("p t (a e) -> p t a e", a=1).to_broadcast([P, TT, 4, 4]), ALU.mult)

            step(outer(first_of, expert_hot))
            step(outer(second_of, second_hot))
            dve.tensor_tensor(both_of, first_of, second_of, ALU.add).then_inc(s["dve_hot"], 1)
            dve.wait_ge(s["act_route"], 2)
            step(dve.tensor_reduce(rc[4], group_exp, AX.X, ALU.add))
            step(dve.tensor_scalar(rc[5], rc[3], 1.0, None, ALU.add))
            step(dve.tensor_tensor(rc[5], rc[5], rc[4], ALU.mult))
            step(dve.reciprocal(rc[5], rc[5]))
            step(dve.tensor_tensor(rc[6], rc[5], rc[3], ALU.mult))
            dve.wait_ge(s["pe_count"], 1)
            inside = bank(5, 0, P).rearrange("p (t e) -> p t e", t=TT)
            total = bank(5, P, 2 * P).rearrange("p (t e) -> p t e", t=TT)
            for t in range(1, TT):
                step(dve.tensor_tensor(tile_off[:, t, :], tile_off[:, t - 1, :], total[:, t - 1, :], ALU.add))
            step(dve.tensor_tensor(count, tile_off[:, TT - 1, :], total[:, TT - 1, :], ALU.add))

            def round_to_integer(t):
                step(dve.tensor_scalar(t, t, ROUND, None, ALU.add))
                step(dve.tensor_scalar(t, t, -ROUND, None, ALU.add))

            step(dve.tensor_scalar(tiles, count, 1.0 / P, (P - 1.0) / P - 0.5 + 0.5 / P, ALU.mult, ALU.add))
            round_to_integer(tiles)
            step(dve.tensor_tensor_scan(upto, one_row, tiles, 0.0, ALU.mult, ALU.add))
            step(dve.tensor_tensor(base_of, upto, tiles, ALU.subtract))
            step(dve.tensor_scalar(base_of, base_of, float(P), None, ALU.mult))
            step(dve.tensor_tensor(slot_of, inside, tile_off, ALU.add))
            step(dve.tensor_tensor(slot_of, slot_of, base_of.rearrange("p (a e) -> p a e", a=1).to_broadcast([P, TT, EXPERTS]),
                                   ALU.add))
            for n, hot in enumerate((first_of, second_of)):
                step(dve.tensor_tensor(masked, hot, slot_of, ALU.mult))
                step(dve.tensor_reduce(slots_f[:, n, :], masked, AX.X, ALU.add))
            step(dve.tensor_scalar(slot_tile, slots_f, 1.0 / P, -0.5 + 0.5 / P, ALU.mult, ALU.add))
            round_to_integer(slot_tile)
            step(dve.scalar_tensor_tensor(out=slot_row, in0=slot_tile, scalar=-float(P), in1=slots_f, op0=ALU.mult, op1=ALU.add))
            for n in range(2):
                step(dve.tensor_tensor(row_hot[:, n, :, :], column_no.rearrange("p (a k) -> p a k", a=1).to_broadcast([P, TT, P]),
                                       column(slot_row[:, n, :]).to_broadcast([P, TT, P]), ALU.is_equal))
                hot = tile_hot[:, n, :, 1, :]
                step(dve.tensor_tensor(hot, column_no[:, 0:32].rearrange("p (a k) -> p a k", a=1).to_broadcast([P, TT, 32]),
                                       column(slot_tile[:, n, :]).to_broadcast([P, TT, 32]), ALU.is_equal))
                step(dve.tensor_tensor(tile_hot[:, n, :, 0, :], hot, column(token_no).to_broadcast([P, TT, 32]), ALU.mult))
                dve.tensor_tensor(hot, hot, column(rc[5 + n]).to_broadcast([P, TT, 32]), ALU.mult).then_inc(s["dve_hot"], 1)
            step(dve.tensor_tensor(ended, upto.rearrange("p (a e) -> p a e", a=1).to_broadcast([P, 34, EXPERTS]),
                                   column_no[:, 0:34].rearrange("p (k a) -> p k a", a=1).to_broadcast([P, 34, EXPERTS]),
                                   ALU.is_le))
            step(dve.tensor_reduce(ended_sum, ended, AX.X, ALU.add))
            step(dve.tensor_scalar(expert_of, ended_sum, EXPERTS - 1.0, None, ALU.min))
            step(dve.tensor_scalar(pairs_f[:, 0:1], upto[:, EXPERTS - 1:EXPERTS], 0.5, 0.25, ALU.mult, ALU.add))
            round_to_integer(pairs_f[:, 0:1])
            step(dve.tensor_copy(pair_count, pairs_f[0:1, 0:1]))
            step(dve.tensor_copy(slots_i, slots_f))
            step(dve.memset(token_of, 0))
            dve.wait_ge(s["pe_table"], 1)
            step(dve.tensor_copy(weight_t, bank(6, 32, 64)))
            dve.tensor_copy(token_of[:, 0:32], bank(6, 0, 32)).then_inc(s["dve_table"], 1)
            dve.wait_ge(s["dve_table"], 1)
            pairs = dve.value_load(pair_count, min_val=8, max_val=16)

            def modulate(j, m):
                dve.wait_ge(s["pe_au"], j + (FREE - 1))
                dve.wait_ge(s["pe_x"], j + (1 + FREE))
                for kt in range(4, KT):
                    dve.tensor_scalar(slot_hT[:, m, kt, :], bank(3, (kt - 4) * P, (kt - 3) * P), scale2[:, kt:kt + 1],
                                      shift2[:, kt:kt + 1], ALU.mult, ALU.add).then_inc(s["dve_h"], 1)

            def multiply(j, m):
                dve.wait_ge(s["pe_actT"], j + (FREE - 1))
                dve.wait_ge(s["act_silu"], j + 1)
                dve.tensor_tensor(act_tok[:, m, :], silu[:, m, :], bank(m, HID, 2 * HID), ALU.mult)\
                   .then_inc(s["dve_mul"], 1)

            def hidden_out(j, m):
                dve.wait_ge(s["pe_down"], j * 2 + (FREE - 2))
                dve.wait_ge(s["pe_actT"], j + (FREE + 1))
                dve.tensor_copy(actT[:, m, :], bank(4 + m, 0, HID)).then_inc(s["dve_actT"], 1)

            def weigh(j, m, stores):
                dve.wait_ge(y_stored[m], stores * 16 + 16)
                for half in range(2):
                    dve.wait_ge(s["pe_down"], j * 2 + (half + 1 + FREE))
                    lo = half * 512
                    dve.scalar_tensor_tensor(out=slot_y[:, m, lo:lo + 512], in0=bank(6 + half),
                                             scalar=weight_t[:, bass.ds(j, 1)], in1=res_gate2[:, lo:lo + 512],
                                             op0=ALU.mult, op1=ALU.mult).then_inc(s["dve_y"], 1)

            modulate(0, 0)
            multiply(0, 0)
            modulate(1, 1)
            hidden_out(0, 0)
            with dve.Fori(0, pairs - 1) as i:
                for m in range(2):
                    multiply(i * 2 + (m + 1), 1 - m)
                    modulate(i * 2 + (m + 2), m)
                    weigh(i * 2 + m, m, i)
                    hidden_out(i * 2 + (m + 1), 1 - m)
            final = pairs * 2
            multiply(final - 1, 1)
            weigh(final - 2, 0, pairs - 1)
            hidden_out(final - 1, 1)
            weigh(final - 1, 1, pairs - 1)
            def residual(i):
                done = 32 * (i // 4 + 1)
                dve.wait_ge(in_parts[i % 4], done if i % 4 < 2 else pairs * 16 + done)
                step(dve.tensor_tensor(x1[:, i, :], x1[:, i, :], parts[:, i % 4, 0, :], ALU.add))
                dve.tensor_tensor(x1[:, i, :], x1[:, i, :], parts[:, i % 4, 1, :], ALU.add).then_inc(s["dve_moe"], 1)

            residual(0)
            dve.wait_ge(s["in_res"], 16)
            for i in range(TT):
                if i + 1 < TT:
                    residual(i + 1)
                dve.wait_ge(s["act_ssq2"], TT + i + 1)
                dve.tensor_scalar(ssq[:, i:i + 1], ssq[:, i:i + 1], 1.0 / D, EPS, ALU.mult, ALU.add).then_inc(s["dve_ms2"], 1)
                dve.wait_ge(s["act_rt2"], TT + i + 1)
                step(dve.reciprocal(rstd[:, i:i + 1], rstd[:, i:i + 1]))
                dve.scalar_tensor_tensor(out=x1[:, i, :], in0=x1[:, i, :], scalar=rstd[:, i:i + 1], in1=final_gain,
                                         op0=ALU.mult, op1=ALU.mult).then_inc(s["dve_fin"], 1)

        @block.tensor
        def _(pe):
            def mm(dst, lhsT, rhs, first, last):
                return pe.matmul(dst, lhsT, rhs, start=first, stop=last)

            for name in ("pe_au", "pe_x", "pe_actT", "pe_down"):
                pe.sem_inc(s[name], FREE)
            pe.wait_ge(s["pool_const"], 3)
            pe.wait_ge(s["in_vec"], 16 * 11)
            pe.transpose(bank(7, 0, P), staged, ident[:, :]).then_inc(s["pe_vec"], 1)
            pe.wait_ge(s["in_feat"], 80)
            for layer in range(2):
                for half in range(2):
                    lo = half * 512
                    dst = psum[0:64, layer * 1024 + lo:layer * 1024 + lo + 512]
                    if layer == 1:
                        pe.wait_ge(s["act_sin"], 1)
                    mm(dst, w1_sb if layer == 0 else w2_sb, (feat if layer == 0 else hid)[:, lo:lo + 512], True, True)\
                        .then_inc(s["pe_sin"], 1)
            pe.wait_ge(s["in_window"], 32)
            pe.wait_ge(s["act_sin"], 2)
            pe.wait_ge(s["dve_vec"], 1)
            for i in range(TT):
                if i >= 2:
                    pe.wait_ge(s["dve_filt"], i - 1)
                b = 4 + 2 * (i % 2)
                mm(bank(b), hid[:, i * P:i * P + P], w3_sb[:, 0:512], True, True)
                mm(bank(b + 1), hid[:, i * P:i * P + P], w3_sb[:, 512:1024], True, True).then_inc(s["pe_filt"], 1)
            def turn(acc, b):
                for m in range(4):
                    last = pe.transpose(bank(b, m * P, m * P + P), acc[:, m * P:m * P + P], ident[:, :])
                last.then_inc(s["pe_ada"], 1)

            def ada_turns(n):
                pe.wait_ge(s["dve_acc"], n + 1)
                for v in range(2):
                    turn(ada_acc[:, n, v, :], 4 + 2 * (n % 2) + v)

            def other_turn(c, b):
                pe.wait_ge(s["dve_acc"], 4 + c + 1)
                turn(ada_acc2[:, c % 2, :], b)

            pe.wait_ge(s["dve_filt"], TT)
            for g in range(8):
                f, part = g // 2, g % 2
                arrived(pe, K_SPEC[f])
                if g >= 2:
                    pe.wait_ge(s["dve_filter"], g - 1)
                table = slot(K_SPEC[f], TT, 2, P)
                for i in range(TT):
                    last = mm(bank(2 * (g % 2) + i // 4), table[:, i, part, :], (fsum, fdif)[part][:, i, :],
                              i % 4 == 0, i % 4 == 3)
                last.then_inc(s["pe_spec"], 1)
                if g == 2:
                    pe.wait_ge(s["pool_sq"], 4 * TT - 1)
                    for n in range(4):
                        last = mm(bank(4, n, n + 1), sq_acc[:, n * P:n * P + P], ones[:, 0:1], True, True)
                    last.then_inc(s["pe_fnorm"], 1)
                if g == 5:
                    pe.wait_ge(s["dve_vec"], 4)
                    for n in range(2):
                        ada_turns(n)
            pe.wait_ge(s["dve_ada"], 4)
            for n in (2, 3):
                ada_turns(n)
            pe.wait_ge(s["act_xn"], AT)
            pe.wait_ge(s["dve_filter"], 8)
            for n in range(3 * KT):
                kt, g = n // 3, n % 3
                if n >= 4:
                    pe.wait_ge(s["act_hT"], n - 3)
                for i in range(4 if g < 2 else CT):
                    src = x_sb[:, 4 * g + i, :] if g < 2 else x_ctx[:, i, :]
                    last = pe.transpose(bank(n % 4, i * P, i * P + P), src[:, kt * P:kt * P + P], ident[:, :])
                last.then_inc(s["pe_xT"], 1)
            pe.wait_ge(s["act_hT"], 3 * KT)
            pe.wait_ge(s["dve_mod"], 1)
            for g in range(12):
                ct, half = g // 2, g % 2
                n = K_HY[ct // 4]
                arrived(pe, n)
                if g >= 4:
                    pe.wait_ge(s["act_hy"], g - 3)
                w = slot(n, KT, 512 if ct < 4 else 256)
                for k in range(KT):
                    last = mm(bank(4 + g % 4), w[:, k, (ct % 4) * P:(ct % 4) * P + P],
                              hT[:, k, half * 512:half * 512 + 512], k == 0, k == KT - 1)
                last.then_inc(s["pe_hy"], 1)
            pe.wait_ge(s["act_hy"], 12)

            for order in range(2):
                if order == 1:
                    pe.wait_ge(s["act_inv"], 4)
                for ct in range(2):
                    pe.wait_ge(s["dve_fold"], 4 * order + 2 * ct + 2)
                    for tt in range(4):
                        for n in range(2):
                            last = pe.transpose(bank(tt, (2 * n + ct) * P, (2 * n + ct + 1) * P),
                                                folded[:, n, ct, tt * P:tt * P + P], ident[:, :])
                        if ct == 1:
                            last.then_inc(s["pe_fold"], 1)
                pe.wait_ge(s["act_fold"], 4 * order + 4)
                for j in range(KT):
                    n = K_CONV[order][0][j // 4]
                    arrived(pe, n)
                    table = slot(n, 4, 4, 2, P)
                    if 8 * order + j >= 4:
                        pe.wait_ge(s["dve_spec"], 8 * order + j - 3)
                    for m in range(2):
                        src = m if j < 4 else 1 - m
                        for tt in range(4):
                            last = mm(bank(4 + j % 4, m * BW, m * BW + BW), table[:, j % 4, tt, m, :],
                                      folded_t[:, tt, src, :], tt == 0, tt == 3)
                    last.then_inc(s["pe_fwd"], 1)
                for jj, cts in ((range(4), (0, 1)), (range(4, KT), (0,)), (range(4, KT), (1,))):
                    for j in jj:
                        n = K_CONV[order][1][j // 4]
                        arrived(pe, n)
                        table = slot(n, 4, 2, 512)
                        pe.wait_ge(s["dve_spec"], 8 * order + j + 1)
                        for ct in cts:
                            for m in range(2):
                                ab = m if j < 4 else 1 - m
                                last = mm(bank(2 * ct + ab), conv_spec[:, j, m, ct * P:ct * P + P],
                                          table[:, j % 4, m, :], j == 0, j == KT - 1)
                    last.then_inc(s["pe_inv"], 1)
            pe.wait_ge(s["act_inv"], 8)
            arrived(pe, K_FN)
            w = slot(K_FN, KT, BW)
            for g in range(4):
                for k in range(KT):
                    last = mm(bank(g), w[:, k, (g // 2) * P:(g // 2) * P + P],
                              hT[:, k, (g % 2) * 512:(g % 2) * 512 + 512], k == 0, k == KT - 1)
                last.then_inc(s["pe_fn"], 1)
            for c in range(2):
                other_turn(c, 6 + c)
            pe.wait_ge(s["act_fn"], 4)
            pe.wait_ge(s["in_x"], 48)
            for i in range(TT):
                if i >= 4:
                    pe.wait_ge(s["act_chan"], i - 3)
                elif i >= 2:
                    pe.wait_ge(s["dve_ada"], 8 + i - 1)
                for ct in range(2):
                    last = mm(bank(4 + i % 4, ct * 256, ct * 256 + 256), fnT[:, ct, i * P:i * P + P], chan_basis,
                              True, True)
                last.then_inc(s["pe_chan"], 1)
            pe.wait_ge(s["act_chan"], TT)
            for part in range(2):
                arrived(pe, K_TOK[part])
                table = slot(K_TOK[part], TT, 512)
                for ct in range(2):
                    for i in range(TT):
                        last = mm(bank(4 * part + ct), chan_mixed[:, i, ct, part, :], table[:, i, :], i == 0, i == TT - 1)
                    if part == 0:
                        for i in range(TT):
                            last = mm(bank(2, ct, ct + 1), chan_mixed[:, i, ct, 0, :], alternate, i == 0, i == TT - 1)
                last.then_inc(s["pe_tok"], 1)
            for c in (2, 3):
                other_turn(c, 4 + c)
            arrived(pe, K_MLA)
            pe.wait_ge(s["dve_oc"], 2)
            w = slot(K_MLA, KT, 416)
            for i in range(AT):
                if i >= 4:
                    pe.wait_ge(s["dve_mla"], i - 3)
                lo = 0 if i < TT else 256
                for k in range(KT):
                    last = mm(bank(i % 4, lo, 416), hT[:, k, i * P:i * P + P], w[:, k, lo:416], k == 0, k == KT - 1)
                last.then_inc(s["pe_mla"], 1)
            pe.wait_ge(s["dve_ada"], 12)
            other_turn(4, 7)
            pe.wait_ge(s["dve_mn"], 2 + TT + AT)
            for g in range(7):
                src = mla_tok[:, :, (g // 2) * P:(g // 2) * P + P] if g < 4 else mla_tok[:, :, 256:384]
                t0 = 4 * (g % 2 if g < 4 else g - 4)
                for i in range(4 if g < 6 else CT):
                    last = pe.transpose(bank(g, i * P, i * P + P), src[:, t0 + i, :], ident[:, :])
                last.then_inc(s["pe_mT"], 1)
            pe.wait_ge(s["dve_ada"], 13)
            other_turn(5, 7)
            pe.wait_ge(s["act_mT"], 7)
            pe.wait_ge(s["in_uq"], 32)
            pe.wait_ge(s["dve_ada"], 14)
            for i in range(AT):
                if i < TT:
                    if i >= 4:
                        pe.wait_ge(s["dve_uq"], i - 3)
                    for k in range(2):
                        last = mm(bank(i % 4, 0, 384), cqT[:, k, i * P:i * P + P], w_uq[:, k, :], k == 0, k == 1)
                    last.then_inc(s["pe_uq"], 1)
                if i >= 4:
                    pe.wait_ge(s["act_ukv"], 2 * (i - 3))
                mm(bank(4 + i % 4), ckvT[:, i * P:i * P + P], w_ukv, True, True).then_inc(s["pe_ukv"], 1)
            pe.wait_ge(s["dve_rope"], HEADS)
            for g in range(8):
                if g >= 4:
                    pe.wait_ge(s["dve_qT"], g - 3)
                for i in range(4):
                    last = pe.transpose(psum[0:QK, (g % 4) * 512 + i * P:(g % 4) * 512 + i * P + P],
                                        q_tok[:, 4 * (g % 2) + i, g // 2, :], ident[:, :])
                last.then_inc(s["pe_qT"], 1)
            pe.wait_ge(s["act_ukv"], 2 * AT)
            for g in range(12):
                if g >= 4:
                    pe.wait_ge(s["act_kT"], g - 3)
                for i in range(4 if g % 3 < 2 else CT):
                    last = pe.transpose(psum[0:QK, (4 + g % 4) * 512 + i * P:(4 + g % 4) * 512 + i * P + P],
                                        k_tok[:, 4 * (g % 3) + i, g // 3, :], ident[:, :])
                last.then_inc(s["pe_kT"], 1)
            pe.wait_ge(s["act_kT"], 12)
            pe.wait_ge(s["dve_qT"], 8)
            def scores(h, q):
                pe.wait_ge(s["pool_q"], h * TT + q + 1)
                if q >= 2:
                    pe.wait_ge(s["act_p"], h * TT + q - 1)
                base = (q % 2) * 1536
                for lo, hi in ((0, 512), (512, 1024), (1024, 1280)):
                    last = mm(psum[:, base + lo:base + hi], q_now[:, q % 2, :], kT[:, bass.ds(h + q // TT, 1), lo:hi], True, True)
                last.then_inc(s["pe_qk"], 1)

            def values(h, q):
                pe.wait_ge(s["dve_pt"], h * 2 * TT + 2 * q + 2)
                pe.wait_ge(s["act_pt"], h * TT + q + 1)
                for i in range(AT):
                    last = mm(bank(7, 0, VD), probT[:, i, :],
                              v_tok[:, i, bass.ds(h * VD, VD)], i == 0, i == AT - 1)
                last.then_inc(s["pe_pv"], 1)

            def attend(h, end):
                for q in range(TT):
                    if q + 1 < TT or not end:
                        scores(h, q + 1)
                    if q >= 1:
                        values(h, q - 1)
                    pe.wait_ge(s["act_p"], h * TT + q + 1)
                    for r in range(3):
                        if r == 0 and q >= 1:
                            pe.wait_ge(s["dve_pt"], h * 2 * TT + 2 * q)
                        elif r == 1 and q >= 1:
                            pe.wait_ge(s["dve_o"], h * TT + q)
                        elif r == 2:
                            pe.wait_ge(s["dve_pt"], h * 2 * TT + 2 * q + 1)
                        for i in range(4 * r, min(4 * r + 4, AT)):
                            last = pe.transpose(bank(6 + r % 2, (i % 4) * P, (i % 4) * P + P),
                                                prob[:, q % 2, i * P:i * P + P], ident[:, :])
                        last.then_inc(s["pe_t"], 1)
                values(h, TT - 1)
                pe.wait_ge(s["dve_o"], h * TT + TT)

            scores(0, 0)
            with pe.Fori(0, HEADS - 1) as h:
                attend(h, False)
            attend(HEADS - 1, True)
            for g in range(4):
                for i in range(4):
                    last = pe.transpose(bank(g, i * P, i * P + P), oa_tok[:, 4 * (g % 2) + i, (g // 2) * P:(g // 2) * P + P],
                                        ident[:, :])
                last.then_inc(s["pe_oaT"], 1)
            pe.wait_ge(s["act_oaT"], 4)
            arrived(pe, K_NQK)
            w = slot(K_NQK, KT, 512)
            for g in range(10):
                if g >= 4:
                    pe.wait_ge(s["act_nqk"], g - 3)
                    pe.wait_ge(s["dve_nqk"], g - 3)
                _, lo, n = na_group(g)
                col = (g % 2) * P + (0 if g < 4 else BW)
                for k in range(KT):
                    last = mm(bank(g % 4, 0, n), w[:, k, col:col + P], hT[:, k, lo:lo + n], k == 0, k == KT - 1)
                last.then_inc(s["pe_nqk"], 1)
            other_turn(6, 4)
            arrived(pe, K_NV)
            w = slot(K_NV, KT, BW)
            pe.wait_ge(s["dve_ada"], 15)
            for i in range(AT):
                if i >= 4:
                    pe.wait_ge(s["act_nv"], i - 3)
                for k in range(KT):
                    last = mm(bank(4 + i % 4, 0, BW), hT[:, k, i * P:i * P + P], w[:, k, :], k == 0, k == KT - 1)
                last.then_inc(s["pe_nv"], 1)
            pe.wait_ge(s["in_rpb"], 16 * 8)
            pe.wait_ge(s["act_nqk"], 10)
            pe.wait_ge(s["dve_nqk"], 10)
            pe.wait_ge(s["act_nv"], AT)
            for kc in range(64):
                if kc % 32 == 0:
                    arrived(pe, K_REL[kc // 32])
                table = slot(K_REL[kc // 32], 32, P, rows=64)
                last = mm(bank(kc // 8, (kc % 8) * 56, (kc % 8) * 56 + 56), table[:, kc % 32, :],
                          rpb_t.rearrange("p h r -> p (h r)"), True, True)
                if kc % 8 == 7:
                    last.then_inc(s["pe_bb"], 1)
            pe.wait_ge(s["dve_bb"], 8)
            other_turn(7, 7)
            pe.wait_ge(s["dve_ada"], 16)
            pe.wait_ge(s["pool_pad"], 4)
            def near_scores(h, q):
                first, n, _ = NA_TILES[q % TT]
                pe.wait_ge(s["pool_nq"], h * TT + q + 1)
                if q >= 2:
                    pe.wait_ge(s["dve_nmx"], h * TT + q - 1)
                base = (q % 2) * 1024
                for lo, hi, key in [(0, 512, first * P)] + ([(512, 640, first * P + 512)] if n == 640 else []) + \
                        [(n, n + C, T)]:
                    last = mm(psum[:, base + lo:base + hi], nq_now[:, q % 2, :],
                              nkT[:, bass.ds(h + q // TT, 1), key:key + hi - lo], True, True)
                last.then_inc(s["pe_nqk2"], 1)

            def near_values(h, q):
                first, n, _ = NA_TILES[q]
                pe.wait_ge(s["act_npt"], h * 2 * TT + 2 * q + 2)
                if q >= 2:
                    pe.wait_ge(s["dve_no"], h * TT + q - 1)
                tiles = [first + i for i in range(n // P)] + [TT, TT + 1]
                for i, t in enumerate(tiles):
                    last = mm(bank(6 + q % 2, 0, VD), nprobT[:, i, :],
                              nv_tok[:, t, bass.ds(h * VD, VD)], i == 0, i == len(tiles) - 1)
                last.then_inc(s["pe_npv"], 1)

            def near_attend(h, end):
                for q in range(TT):
                    if q + 1 < TT or not end:
                        near_scores(h, q + 1)
                    if q >= 1:
                        near_values(h, q - 1)
                    n = (NA_TILES[q][1] + C) // P
                    pe.wait_ge(s["act_np"], h * TT + q + 1)
                    if q >= 1:
                        pe.wait_ge(s["act_npt"], h * 2 * TT + 2 * q)
                    for r in range(2):
                        for i in range(4 * r, min(4 * r + 4, n)):
                            last = pe.transpose(bank(4 + r, (i % 4) * P, (i % 4) * P + P),
                                                nprob[:, q % 2, i * P:i * P + P], ident[:, :])
                        last.then_inc(s["pe_nt"], 1)
                near_values(h, TT - 1)
                pe.wait_ge(s["dve_no"], h * TT + TT)

            near_scores(0, 0)
            with pe.Fori(0, HEADS - 1) as h:
                near_attend(h, False)
            near_attend(HEADS - 1, True)
            for g in range(4):
                for i in range(4):
                    last = pe.transpose(bank(g, i * P, i * P + P), od_tok[:, 4 * (g % 2) + i, (g // 2) * P:(g // 2) * P + P],
                                        ident[:, :])
                last.then_inc(s["pe_odT"], 1)
            pe.wait_ge(s["dve_ada"], 18)
            for n in range(4):
                for m in range(4):
                    last = mm(bank(4 + n, m * P, m * P + P), gate_cols[:, 4 * n + m, :], ident[:, :], True, True)
                last.then_inc(s["pe_res"], 1)
            pe.wait_ge(s["act_odT"], 4)
            pe.wait_ge(s["pool_split"], 2 * HEADS * TT)
            with pe.Fori(0, KT // 2) as i:
                for m in range(16):
                    slot_n, n, half = m // 8, (m // 2) % 4, m % 2
                    if half == 0:
                        pe.wait_ge(s["dve_split"], i * 8 + (HEADS * TT + m // 2 + 1))
                    for name in ("act_gate", "dve_gate"):
                        pe.wait_ge(s[name], i * 16 + m + FREE - 3)
                    for k in range(KT):
                        h, h_rest = (t[:, k, half * 512:half * 512 + 512] for t in (hT_upper, hT_rest))
                        w, rest = w_upper[:, n, k, :], w_rest[:, n % 2, k, :]
                        mm(bank(m % 4), w, h, k == 0, False)
                        mm(bank(m % 4), w, h_rest, False, False)
                        last = mm(bank(m % 4), rest, h, False, k == KT - 1)
                    last.then_inc(s["pe_gg"], 1)
                    pe.wait_ge(in_gate[1], i * 64 + 32 * (slot_n + 1))
                    pe.wait_ge(s["dve_res"], 4)
                    for k in range(2):
                        last = mm(bank(4 + m % 4), wb[:, slot_n, 2 * n + k, :], oT[n][:, k, half * 512:half * 512 + 512],
                                  k == 0, k == 1)
                    last.then_inc(s["pe_gate"], 1)
            pe.wait_ge(s["dve_gate"], 64 + FREE)
            def second_rows(i):
                pe.wait_ge(s["dve_x1n"], i + 1)
                if i >= 1:
                    pe.wait_ge(s["act_hT2"], i * KT)
                for kt in range(KT):
                    last = pe.transpose(bank(4 + kt // 4, (kt % 4) * P, (kt % 4) * P + P), x1n[:, i, kt * P:kt * P + P],
                                        ident[:, :])
                last.then_inc(s["pe_hT2"], 1)

            def route(i):
                pe.wait_ge(s["act_hT2"], i * KT + KT)
                if i >= 1:
                    pe.wait_ge(s["dve_logit"], i)
                for k in range(KT):
                    last = mm(psum[0:20, 3072 + (i % 4) * P:3200 + (i % 4) * P], wr[:, k, :], h2T[:, i % 2, k, :],
                              k == 0, k == KT - 1)
                last.then_inc(s["pe_route"], 1)

            def back(i):
                pe.wait_ge(s["dve_logit"], i + 1)
                pe.transpose(bank(7, 20 * i, 20 * i + 20), logits_t[:, i * P:i * P + P], ident[0:20, 0:20])\
                  .then_inc(s["pe_back"], 1)

            def follow(i):
                if 1 <= i <= TT:
                    second_rows(i - 1)
                if 2 <= i <= TT + 1:
                    route(i - 2)
                if 3 <= i <= TT + 2:
                    back(i - 3)

            for m in range(3 * TT):
                t, (_, w) = m % TT, OUT_PASSES[m // TT]
                if t == 0:
                    pe.wait_ge(s["in_w_out"], 16 if m == 0 else 32)
                if m >= 8:
                    pe.wait_ge(s["dve_x1"], m - 7 if m < 20 else m - 3)
                for k in range(KT):
                    last = mm(out_bank(m, w.shape[-1]), merged[:, k, t * P:t * P + P], w[:, k, :], k == 0, k == KT - 1)
                last.then_inc(s["pe_out"], 1)
                if m == 2 * TT:
                    pe.wait_ge(s["in_router"], 64)
                if m >= 2 * TT:
                    follow(t)
            for i in range(TT, TT + 3):
                follow(i)
            pe.wait_ge(s["in_tab"], 16)
            pe.wait_ge(s["dve_hot"], 1)
            both = both_of.rearrange("p t e -> p (t e)")
            mm(bank(5, 0, P), before, both, True, True)
            mm(bank(5, P, 2 * P), all_ones, both, True, True).then_inc(s["pe_count"], 1)
            for n in range(2):
                pe.wait_ge(s["dve_hot"], n + 2)
                for t in range(TT):
                    last = mm(bank(6, 0, 64), row_hot[:, n, t, :], tile_hot[:, n, t, :, :].rearrange("p a b -> p (a b)"),
                              n == 0 and t == 0, n == 1 and t == TT - 1)
            last.then_inc(s["pe_table"], 1)
            pe.wait_ge(s["dve_table"], 1)
            pairs = pe.value_load(pair_count, min_val=8, max_val=16)

            def rows(m):
                for kt in range(KT):
                    last = pe.transpose(bank(2 + kt // 4, (kt % 4) * P, (kt % 4) * P + P), slot_x[:, m, kt * P:kt * P + P],
                                        ident[:, :])
                last.then_inc(s["pe_x"], 1)

            def gate_up(j, m, loads):
                pe.wait_ge(in_expert[m], loads * 32 + 32)
                pe.wait_ge(s["act_h"], j * 4 + 4)
                pe.wait_ge(s["dve_h"], j * 4 + 4)
                pe.wait_ge(s["dve_mul"], j + (FREE - 1))
                for k in range(KT):
                    last = mm(bank(m), slot_hT[:, m, k, :], expert_slots[:, m, k, :], k == 0, k == KT - 1)
                last.then_inc(s["pe_au"], 1)

            def hidden(j, m):
                pe.wait_ge(s["dve_mul"], j + (FREE + 1))
                pe.wait_ge(s["dve_actT"], j + (FREE - 1))
                for f in range(2):
                    last = pe.transpose(bank(4 + m, f * P, f * P + P), act_tok[:, m, f * P:f * P + P], ident[:, :])
                last.then_inc(s["pe_actT"], 1)

            def down(j, m, loads):
                pe.wait_ge(in_down[m], loads * 16 + 16)
                pe.wait_ge(s["dve_actT"], j + (FREE + 1))
                for half in range(2):
                    pe.wait_ge(s["dve_y"], j * 2 + (half - 1 + FREE))
                    for f in range(2):
                        last = mm(bank(6 + half), actT[:, m, f * P:f * P + P], w_down[:, m, f, half * 512:half * 512 + 512],
                                  f == 0, f == 1)
                    last.then_inc(s["pe_down"], 1)

            for m in range(2):
                pe.wait_ge(in_slots[m], 16)
                rows(m)
                if m == 0:
                    gate_up(0, 0, 0)
            hidden(0, 0)
            with pe.Fori(0, pairs - 1) as i:
                for m in range(2):
                    gate_up(i * 2 + (m + 1), 1 - m, i + m)
                    pe.wait_ge(in_slots[m], i * 16 + 32)
                    rows(m)
                    down(i * 2 + m, m, i)
                    hidden(i * 2 + (m + 1), 1 - m)
            final = pairs * 2
            gate_up(final - 1, 1, pairs - 1)
            down(final - 2, 0, pairs - 1)
            hidden(final - 1, 1)
            down(final - 1, 1, pairs - 1)


def _tables():
    import numpy as np
    P, T, pi = 128, 1024, np.pi
    f32 = np.float32
    tb = {}
    order = np.concatenate([np.arange(0, T, 2), np.arange(1, T, 2)])
    t = np.linspace(0.0, 1.0, T, dtype=f32)
    bands = np.linspace(1e-4, 15, 16, dtype=f32)
    ang = (f32(2.0 * pi / T) * np.arange(T, dtype=f32)[:, None] * bands).astype(f32)
    tb["features"] = np.concatenate([t[:, None], np.cos(ang), -np.sin(ang)], axis=1)[order].T
    dl = np.linspace(np.log(1e-2) / 1.5, np.log(1e-2) / 0.3, 256)
    win = np.exp(-np.linspace(0, 1, T)[:, None] * np.abs(dl))
    back = win.copy()
    back[0] = 0.0
    tb["window"] = np.stack([win, back], 1)[order].reshape(8, P, 2, 256).transpose(1, 0, 2, 3)
    k = np.concatenate([np.arange(0, T, 2), T - 1 - np.arange(0, T, 2)])
    a = pi * (((2 * k[None, :512] + 1) * order[:, None]) % (4 * T)) / (2 * T)
    g = np.stack([np.cos(a), -np.sin(a)], 1)
    tb["filter_basis"] = g.reshape(8, P, 2, 4, P).transpose(1, 3, 0, 2, 4)
    th = pi * (((2 * k[None, :] + 1) * (2 * np.arange(512)[:, None] + 1)) % (8 * T)) / (4 * T)
    cas = np.stack([np.cos(th) + np.sin(th), np.cos(th) - np.sin(th)], 1)
    tb["forward_basis"] = cas.reshape(4, P, 2, 8, P).transpose(1, 3, 0, 2, 4)
    tb["inverse_basis"] = (cas / (2 * T)).transpose(2, 1, 0).reshape(8, P, 2, 512).transpose(1, 0, 2, 3)
    b = 2 * pi * ((np.arange(T)[:, None] * np.arange(512)[None, :]) % T) / T
    tb["token_basis"] = np.stack([np.cos(b), -np.sin(b)], 0).reshape(2, 8, P, 512).transpose(2, 0, 1, 3)
    c = 2 * pi * ((np.arange(64)[:, None] * np.arange(64)[None, :]) % 64) / 64
    chan = np.zeros((P, 2, P))
    for n in range(2):
        chan[n * 64:n * 64 + 64, 0, n * 64:n * 64 + 64] = np.cos(c) / 256
        chan[n * 64:n * 64 + 64, 1, n * 64:n * 64 + 64] = np.sin(c) / 256
    tok = np.arange(T)
    inv = (f32(10000.0) ** (-np.arange(8, dtype=f32) / f32(8))).astype(f32)
    ra = np.concatenate([(tok // 64).astype(f32)[:, None] * inv, (tok % 64).astype(f32)[:, None] * inv], 1)
    rope = np.stack([np.cos(ra), np.sin(ra)], 1).reshape(8, P, 2, 16).transpose(1, 2, 0, 3)
    rows = np.full((P, 10, 64), -1e30)
    rows[:64, 0:8] = 0
    rows[64:, 1:9] = 0
    qc, kc = np.arange(64)[:, None], np.arange(64)[None, :]
    start = np.clip(qc - 8, 0, 48)
    ok = (kc >= start) & (kc < start + 16)
    sel = np.zeros((2, 32, 64, 2, 64))
    for r in range(2):
        for q in range(64):
            for kk in range(64):
                if ok[q, kk]:
                    sel[r, kk - q + 15, kk, r, q] = 1
                else:
                    sel[r, 31, kk, r, q] = 1
    tb["relative_columns"] = sel.reshape(64, 64 * P)
    alt = (1 - 2 * (np.arange(P) % 2))[:, None]
    tb["pack"] = np.concatenate([x.reshape(P, -1) for x in (rope, rows, chan, alt)], 1)
    col = np.tile(np.arange(160), (P, 1))
    tb["routing_tab"] = np.concatenate([col, np.arange(T).reshape(8, P).T, np.triu(np.ones((P, P)), 1)], 1)
    return {n: np.ascontiguousarray(v, dtype=f32) for n, v in tb.items()}


_INS = ['x', 'c', 'ctx', 'c_ctx', 'ada_w', 'ada_b', 'norm1_g', 'norm2_g', 'w_in', 'mla_q_norm', 'mla_w_uq',
        'mla_kv_norm', 'mla_w_ukv', 'hy_short_w', 'hy_w1', 'hy_b1', 'hy_freq1', 'hy_w2', 'hy_b2', 'hy_freq2',
        'hy_w3', 'hy_bias', 'na_rpb', 'w_branch', 'w_out', 'moe_w_group', 'moe_b_group', 'moe_w_expert',
        'moe_b_expert', 'moe_w_gate', 'moe_w_up', 'moe_w_down', 'final_norm_g']
_OUTS = [((1, 1024, 1024), 'float32')]


def kernel(**inputs):
    import numpy as _np
    import concourse.bacc as _bacc
    from concourse import mybir as _mybir
    from concourse.bass_utils import run_bass_kernel_spmd as _run

    nc = _bacc.Bacc("TRN2", target_bir_lowering=False, num_devices=1)
    arrays, args = {}, {}
    for name, a in [(n, inputs[n]) for n in _INS] + list(_tables().items()):
        a = _np.ascontiguousarray(a)
        arrays[f"in_{name}_dram"] = a
        args[name] = nc.dram_tensor(f"in_{name}_dram", a.shape, _mybir.dt.from_np(a.dtype), kind="ExternalInput").ap()
    for i, (shape, dtype) in enumerate(_OUTS):
        dt = _mybir.dt.from_np(_np.dtype(dtype))
        args["out"] = nc.dram_tensor(f"out_{i}_dram", shape, dt, kind="ExternalOutput").ap()
    hybrid_flow_backbone(nc, **args)
    r = _run(nc, [arrays], core_ids=[0])
    return r.results[0]["out_0_dram"]
```
